# Optimizing a Trainium2 kernel written in Bass

```python
import math
import jax, jax.numpy as jnp
from jax import lax
import numpy as np

D_MODEL = 1024
BATCH = 1
SEQ = 512
DEPTH = 2

N_MIXERS = 2
N_RWKV = (DEPTH + 1) // 2
N_CONV = DEPTH // 2
RWKV_HEAD = 64
RWKV_HEADS = D_MODEL // RWKV_HEAD
D_DECAY_LORA = 64
D_AAA_LORA = 64
D_GATE_LORA = 128
N_LERP = 6
LNX_EPS = RWKV_HEAD * 1e-5
CONV_WIDTH = 31
CONV_LN_EPS = 1e-5
N_GROUPS = 4
EXPERTS_PER_GROUP = 8
N_EXPERTS = N_GROUPS * EXPERTS_PER_GROUP
TOP_K = 2
D_EXPERT = D_MODEL // 4
RMS_EPS = 1e-6

kernel_name = "hybrid_rwkv7_conformer_hmoe"

def rms_norm(x, g):
    xf = x.astype(jnp.float32)
    y = xf * lax.rsqrt(jnp.mean(xf * xf, axis=-1, keepdims=True) + RMS_EPS)
    return (y * g.astype(jnp.float32)).astype(x.dtype)

def token_shift(x):
    return jnp.pad(x[:, :-1], ((0, 0), (1, 0), (0, 0)))

def rwkv7_recurrence(r, decay, k, v, aa, bb):
    B, T, H, N = r.shape

    def step(S, inp):
        r_t, w_t, k_t, v_t, a_t, b_t = inp
        sa = jnp.einsum('bhij,bhj->bhi', S, a_t)
        S = S * w_t[:, :, None, :] + sa[..., None] * b_t[:, :, None, :] + v_t[..., None] * k_t[:, :, None, :]
        y = jnp.einsum('bhij,bhj->bhi', S, r_t)
        return S, y

    xs = tuple(jnp.moveaxis(t, 1, 0) for t in (r, decay, k, v, aa, bb))
    S0 = jnp.zeros((B, H, N, N), jnp.float32)
    _, y = lax.scan(step, S0, xs)
    return jnp.moveaxis(y, 0, 1)

def rwkv7_time_mix(x, mu, w_rkv, w0, w1, w2, a0, a1, a2, g1, g2, k_k, k_a, r_k, ln_g, ln_b, w_o):
    B, T, C = x.shape
    H, N = RWKV_HEADS, RWKV_HEAD
    xx = token_shift(x) - x
    xs = x[None] + xx[None] * mu[:, None, None, :]
    xr, xw, xk, xv, xa, xg = xs[0], xs[1], xs[2], xs[3], xs[4], xs[5]
    rkv = jnp.einsum('nbtc,ncd->nbtd', jnp.stack([xr, xk, xv]), w_rkv)
    r, k, v = rkv[0], rkv[1], rkv[2]
    w = -jax.nn.softplus(-(w0 + jnp.tanh(xw @ w1) @ w2)) - 0.5
    a = jax.nn.sigmoid(a0 + (xa @ a1) @ a2)
    g = jax.nn.sigmoid(xg @ g1) @ g2
    f32 = jnp.float32
    kk = (k * k_k).astype(f32).reshape(B, T, H, N)
    kk = kk / jnp.maximum(jnp.linalg.norm(kk, axis=-1, keepdims=True), 1e-12)
    k = k * (1.0 + (a - 1.0) * k_a)
    rh = r.astype(f32).reshape(B, T, H, N)
    kh = k.astype(f32).reshape(B, T, H, N)
    vh = v.astype(f32).reshape(B, T, H, N)
    ah = a.astype(f32).reshape(B, T, H, N)
    decay = jnp.exp(-jnp.exp(w.astype(f32))).reshape(B, T, H, N)
    y = rwkv7_recurrence(rh, decay, kh, vh, -kk, kk * ah)
    mean = jnp.mean(y, axis=-1, keepdims=True)
    var = jnp.mean(jnp.square(y - mean), axis=-1, keepdims=True)
    y = ((y - mean) * lax.rsqrt(var + LNX_EPS)).reshape(B, T, C) * ln_g.astype(f32) + ln_b.astype(f32)
    bonus = jnp.sum(rh * kh * r_k.astype(f32), axis=-1, keepdims=True) * vh
    y = (y + bonus.reshape(B, T, C)).astype(x.dtype)
    return (y * g) @ w_o

def conformer_conv(x, w_pw1, b_pw1, w_dw, b_dw, ln_g, ln_b, w_pw2, b_pw2):
    u = x @ w_pw1 + b_pw1
    u = u[..., :D_MODEL] * jax.nn.sigmoid(u[..., D_MODEL:])
    u = lax.conv_general_dilated(
        u, w_dw[:, None, :].astype(u.dtype), window_strides=(1,),
        padding=[(CONV_WIDTH - 1, 0)], dimension_numbers=('NWC', 'WIO', 'NWC'),
        feature_group_count=D_MODEL) + b_dw
    uf = u.astype(jnp.float32)
    m = jnp.mean(uf, axis=-1, keepdims=True)
    var = jnp.mean(jnp.square(uf - m), axis=-1, keepdims=True)
    u = ((uf - m) * lax.rsqrt(var + CONV_LN_EPS) * ln_g.astype(jnp.float32) + ln_b.astype(jnp.float32)).astype(x.dtype)
    u = jax.nn.silu(u)
    return u @ w_pw2 + b_pw2

def hierarchical_moe(h, w_group, b_group, w_expert, b_expert, w_gate, w_up, w_down):
    B, T, D = h.shape
    ht = h.reshape(-1, D)
    f32 = jnp.float32
    gp = jax.nn.softmax((ht @ w_group + b_group).astype(f32), axis=-1)
    p_top, g_idx = lax.top_k(gp, 1)
    el = (ht @ w_expert + b_expert).astype(f32).reshape(-1, N_GROUPS, EXPERTS_PER_GROUP)
    el_sel = jnp.take_along_axis(el, g_idx[:, :, None], axis=1)[:, 0]
    top_l, e_idx = lax.top_k(el_sel, TOP_K)
    w_in = jax.nn.softmax(top_l, axis=-1) * p_top
    within = jnp.sum(jax.nn.one_hot(e_idx, EXPERTS_PER_GROUP, dtype=f32) * w_in[..., None], axis=1)
    gates = (jax.nn.one_hot(g_idx[:, 0], N_GROUPS, dtype=f32)[:, :, None] * within[:, None, :])
    gates = gates.reshape(-1, N_EXPERTS).astype(h.dtype)

    def expert_step(acc, p):
        wg, wu, wd, ge = p
        z = jax.nn.silu(ht @ wg) * (ht @ wu)
        return acc + ge[:, None] * (z @ wd), None

    y, _ = lax.scan(expert_step, jnp.zeros_like(ht), (w_gate, w_up, w_down, gates.T))
    return y.reshape(B, T, D)

def setup_inputs(seed: int = 0) -> dict:
    key = jax.random.key(seed)
    ks = iter(jax.random.split(key, 64))
    D, f = D_MODEL, jnp.float32

    def nrm(shape, scale):
        return jax.random.normal(next(ks), shape, f) * scale

    def unif(shape, lo, hi):
        return jax.random.uniform(next(ks), shape, f, lo, hi)

    n_idx = jnp.arange(D, dtype=f) / (D - 1)
    w0_base = -7.0 + 5.0 * n_idx ** 0.9 + 0.5
    inp = {}
    inp["x"] = nrm((BATCH, SEQ, D), 1.0)
    inp["norm1_g"] = 1.0 + nrm((DEPTH, D), 0.02)
    inp["norm2_g"] = 1.0 + nrm((DEPTH, D), 0.02)
    inp["final_g"] = 1.0 + nrm((D,), 0.02)
    R = N_RWKV
    inp["rwkv_mu"] = unif((R, N_LERP, D), 0.0, 1.0)
    inp["rwkv_w_rkv"] = nrm((R, 3, D, D), D ** -0.5)
    inp["rwkv_w0"] = w0_base[None] + nrm((R, D), 0.1)
    inp["rwkv_w1"] = nrm((R, D, D_DECAY_LORA), D ** -0.5)
    inp["rwkv_w2"] = nrm((R, D_DECAY_LORA, D), 0.1 * D_DECAY_LORA ** -0.5)
    inp["rwkv_a0"] = nrm((R, D), 0.1)
    inp["rwkv_a1"] = nrm((R, D, D_AAA_LORA), D ** -0.5)
    inp["rwkv_a2"] = nrm((R, D_AAA_LORA, D), 0.1 * D_AAA_LORA ** -0.5)
    inp["rwkv_g1"] = nrm((R, D, D_GATE_LORA), D ** -0.5)
    inp["rwkv_g2"] = nrm((R, D_GATE_LORA, D), D_GATE_LORA ** -0.5)
    inp["rwkv_k_k"] = 0.85 + nrm((R, D), 0.02)
    inp["rwkv_k_a"] = 1.0 + nrm((R, D), 0.02)
    inp["rwkv_r_k"] = -0.04 + nrm((R, RWKV_HEADS, RWKV_HEAD), 0.02)
    inp["rwkv_ln_g"] = 1.0 + nrm((R, D), 0.02)
    inp["rwkv_ln_b"] = nrm((R, D), 0.02)
    inp["rwkv_w_o"] = nrm((R, D, D), D ** -0.5)
    Cn = N_CONV
    inp["conv_w_pw1"] = nrm((Cn, D, 2 * D), D ** -0.5)
    inp["conv_b_pw1"] = nrm((Cn, 2 * D), 0.02)
    inp["conv_w_dw"] = nrm((Cn, CONV_WIDTH, D), CONV_WIDTH ** -0.5)
    inp["conv_b_dw"] = nrm((Cn, D), 0.02)
    inp["conv_ln_g"] = 1.0 + nrm((Cn, D), 0.02)
    inp["conv_ln_b"] = nrm((Cn, D), 0.02)
    inp["conv_w_pw2"] = nrm((Cn, D, D), D ** -0.5)
    inp["conv_b_pw2"] = nrm((Cn, D), 0.02)
    inp["moe_w_group"] = nrm((DEPTH, D, N_GROUPS), D ** -0.5)
    inp["moe_b_group"] = nrm((DEPTH, N_GROUPS), 0.01)
    inp["moe_w_expert"] = nrm((DEPTH, D, N_EXPERTS), D ** -0.5)
    inp["moe_b_expert"] = nrm((DEPTH, N_EXPERTS), 0.01)
    inp["moe_w_gate"] = nrm((DEPTH, N_EXPERTS, D, D_EXPERT), D ** -0.5)
    inp["moe_w_up"] = nrm((DEPTH, N_EXPERTS, D, D_EXPERT), D ** -0.5)
    inp["moe_w_down"] = nrm((DEPTH, N_EXPERTS, D_EXPERT, D), D_EXPERT ** -0.5)
    return inp

def reference(x, norm1_g, norm2_g, final_g,
              rwkv_mu, rwkv_w_rkv, rwkv_w0, rwkv_w1, rwkv_w2, rwkv_a0, rwkv_a1, rwkv_a2,
              rwkv_g1, rwkv_g2, rwkv_k_k, rwkv_k_a, rwkv_r_k, rwkv_ln_g, rwkv_ln_b, rwkv_w_o,
              conv_w_pw1, conv_b_pw1, conv_w_dw, conv_b_dw, conv_ln_g, conv_ln_b, conv_w_pw2, conv_b_pw2,
              moe_w_group, moe_b_group, moe_w_expert, moe_b_expert, moe_w_gate, moe_w_up, moe_w_down):
    h = x
    for i in range(DEPTH):
        j = i // N_MIXERS
        hn = rms_norm(h, norm1_g[i])
        if i % N_MIXERS == 0:
            mix = rwkv7_time_mix(hn, rwkv_mu[j], rwkv_w_rkv[j], rwkv_w0[j], rwkv_w1[j], rwkv_w2[j],
                                 rwkv_a0[j], rwkv_a1[j], rwkv_a2[j], rwkv_g1[j], rwkv_g2[j],
                                 rwkv_k_k[j], rwkv_k_a[j], rwkv_r_k[j], rwkv_ln_g[j], rwkv_ln_b[j], rwkv_w_o[j])
        else:
            mix = conformer_conv(hn, conv_w_pw1[j], conv_b_pw1[j], conv_w_dw[j], conv_b_dw[j],
                                 conv_ln_g[j], conv_ln_b[j], conv_w_pw2[j], conv_b_pw2[j])
        h = h + mix
        hn = rms_norm(h, norm2_g[i])
        h = h + hierarchical_moe(hn, moe_w_group[i], moe_b_group[i], moe_w_expert[i], moe_b_expert[i],
                                 moe_w_gate[i], moe_w_up[i], moe_w_down[i])
    return rms_norm(h, final_g)


_drawn_inputs = setup_inputs


def setup_inputs(seed=0):
    import zlib

    import numpy as np

    out = dict(_drawn_inputs(seed))
    spreads = {}
    factors = {'final_g': 3.004,
     'rwkv_w1': 3.97,
     'rwkv_w2': 3.971,
     'conv_b_pw1': 2.74,
     'conv_ln_b': 2.846,
     'conv_b_pw2': 3.231,
     'moe_b_expert': 2.922}
    for name, (base, spread) in spreads.items():
        noise = np.random.default_rng([zlib.crc32(name.encode()), seed]).standard_normal(out[name].shape)
        drawn = base * np.exp(spread * noise) if base else spread * noise
        out[name] = __import__('jax').numpy.asarray(drawn.astype(out[name].dtype))
    for name, factor in factors.items():
        out[name] = (out[name] * factor).astype(out[name].dtype)
    return out
```

```python
import numpy as np

import concourse.bass as bass
from concourse import mybir
from contextlib import ExitStack

D = 1024
T = 512
DEPTH = 2
P = 128
TT = T // P
C = D // P
N_EXP = 32
N_GRP = 4
PER_GRP = N_EXP // N_GRP
F_EXP = 256
SLOTS = 64
RING = 4
NG = N_EXP // RING
RMS_EPS = 1e-6
FAR = 60000.0
LNX_EPS = 64e-5
LN_EPS = 1e-5


class Arena:

    def __init__(self, tensor, start=0):
        self.tensor, self.at = tensor, start

    def take(self, *shape, parts=P):
        n = 1
        for s in shape:
            n *= s
        v = self.tensor[0:parts, self.at:self.at + n]
        self.at += n
        assert self.at <= self.tensor.shape[1], (self.at, self.tensor.shape)
        if len(shape) == 2:
            v = v.rearrange("p (a b) -> p a b", b=shape[1])
        if len(shape) == 3:
            v = v.rearrange("p (a b c) -> p a b c", b=shape[1], c=shape[2])
        return v


class Steps:

    def __init__(self, sem):
        self.sem, self.n = sem, 0

    def done(self, ins):
        self.n += 1
        ins.then_inc(self.sem, 1)
        return self.n


class Signal:

    def __init__(self, made, sem, at, per_trip):
        self.made, self.sem, self.at, self.per_trip = made, sem, at, per_trip

    def by(self, trip):
        return self.per_trip * trip + self.at

    def now(self):
        assert self.made[0] % self.per_trip == self.at - 1, self.at
        self.made[0] += 1
        return self.sem


def signals(sem, n):
    made = [0]
    return [Signal(made, sem, i + 1, n) for i in range(n)]


def bass_hybrid_rwkv7_conformer_hmoe(nc, a, out):
    fp32 = mybir.dt.float32
    u32 = mybir.dt.uint32
    i32 = mybir.dt.int32
    ALU = mybir.AluOpType
    ACT = mybir.ActivationFunctionType
    AX = mybir.AxisListType
    ctx = ExitStack()
    with ctx:
        def sb(name, shape, dt=fp32):
            return ctx.enter_context(nc.sbuf_tensor(name, shape, dt))

        def sem(name):
            return ctx.enter_context(nc.semaphore(name))

        h = sb("h", [P, TT, D])
        ident = sb("ident", [P, P])
        ones = sb("ones", [P, P])
        earlier = sb("earlier", [P, P])
        slot_of_col = sb("slot_of_col", [P, P])
        expert_iota = sb("expert_iota", [P, N_EXP])
        group_iota = sb("group_iota", [P, N_EXP])
        round_starts = sb("round_starts", [P, T // SLOTS - 1])
        token_code = sb("token_code", [P, TT, 2])
        token_next = sb("token_next", [P, TT, 2])
        half_shift = sb("half_shift", [P, 1])
        big = sb("big", [P, 48500 - TT * D])

        psum = ctx.enter_context(nc.psum_tensor("psum", [P, 8 * 512], fp32))
        bank = [psum[:, i * 512:(i + 1) * 512] for i in range(8)]

        normed = [nc.dram_tensor(f"normed{i}", [T, D], fp32, kind="Internal").ap() for i in range(DEPTH)]
        chosen = [nc.dram_tensor(f"chosen{i}", [T * 4, D // 2], fp32, kind="Internal").ap() for i in range(DEPTH)]

        wg_rows = a["moe_w_gate"].rearrange("l e (p c) f -> (l e) p c f", p=P)
        wu_rows = a["moe_w_up"].rearrange("l e (p c) f -> (l e) p c f", p=P)
        wd_rows = a["moe_w_down"].rearrange("l e (k p) d -> (l e) p k d", p=P)

        top = Arena(big)
        ring = [dict(up=top.take(2, C, F_EXP), down=top.take(2, D)) for _ in range(RING)]
        stage_base = top.at

        class Moe:

            def __init__(self, layer):
                m = Arena(big, stage_base)
                self.layer = layer
                self.n_params = 5
                self.g_row = m.take(D)
                self.w_route = m.take(C, N_GRP + N_EXP)
                self.b_route = m.take(N_GRP + N_EXP)
                self.hn = [m.take(D) for _ in range(2)]
                self.hnT = m.take(C, T)
                self.xg = [m.take(D) for _ in range(2)]
                self.dump = self.xg[0]
                self.xT = [m.take(C, P) for _ in range(2)]
                self.silu = [m.take(P) for _ in range(2)]
                self.z = [m.take(P) for _ in range(2)]
                self.zT = [m.take(2, SLOTS) for _ in range(2)]
                self.y = [m.take(D // 2) for _ in range(RING)]
                n = N_GRP + N_EXP
                self.ss = m.take(TT)
                self.rstd = m.take(TT)
                self.logits = m.take(TT, n)
                self.gl = m.take(TT, 8)
                self.gmax = m.take(TT, 8)
                self.gidx = m.take(TT, 8)
                self.gidx_f = m.take(TT)
                self.in_group = m.take(TT, N_EXP)
                self.el = m.take(TT, N_EXP)
                self.emax = m.take(TT, 8)
                self.eidx = m.take(TT, 8)
                self.eidx_f = m.take(TT, 2)
                self.pick = m.take(TT, 2, N_EXP)
                self.picks = m.take(TT, N_EXP)
                self.ranked = m.take(TT, 2, N_EXP)
                self.rank = m.take(TT, 2)
                self.route_rhs = m.take(TT, 2, 2 * N_EXP)
                self.gexp = m.take(TT, N_GRP)
                self.gsum = m.take(TT)
                self.p_top = m.take(TT)
                self.ediff = m.take(TT)
                self.eexp = m.take(TT)
                self.gate = m.take(2, TT)
                self.cmax = m.take(1)
                self.over = m.take(T // SLOTS - 1)
                self.n_over = m.take(1)
                self.rounds = m.take(1)
                self.hot = m.take(TT * 2, P)
                self.far = m.take(2 * N_EXP)
                self.idx = m.take(2 * N_EXP)
                self.scatter_at = m.take(N_EXP)
                self.gather_at = m.take(N_EXP // 2)
                self.scatter_now = m.take(RING)
                self.gather_now = m.take(2)
                self.back = [self.hnT.rearrange("p c t -> p (c t)")[:, 2 * D * b:2 * D * (b + 1)] for b in range(2)]
                s = f"{layer}"
                self.params_in = sem("moe_params_in" + s)
                self.squares = sem("squares" + s)
                self.rstd_step = sem("rstd_step" + s)
                self.hn_ready = sem("hn_ready" + s)
                self.hn_stored = [sem(f"hn_stored{b}_" + s) for b in range(2)]
                self.hnT_in_psum = sem("hnT_in_psum" + s)
                self.hnT_ready = sem("hnT_ready" + s)
                self.logits_in_psum = sem("logits_in_psum" + s)
                self.route = sem("route" + s)
                self.exp_ready = sem("exp_ready" + s)
                self.rank_in_psum = sem("rank_in_psum" + s)
                self.rounds_ready = sem("rounds_ready" + s)
                self.hot_ready = sem("hot_ready" + s)
                self.slots_in_psum = sem("slots_in_psum" + s)
                self.slot_step = sem("slot_step" + s)
                self.tables_ready = sem("tables_ready" + s)
                self.round_done = sem("round_done" + s)
                self.w_in = [sem(f"w_in{j}_" + s) for j in range(RING)]
                self.index_ready = sem("index_ready" + s)
                self.xg_cleared = sem("xg_cleared" + s)
                self.xg_in = [sem(f"xg_in{b}_" + s) for b in range(2)]
                self.xT_in_psum = sem("xT_in_psum" + s)
                self.xT_ready = sem("xT_ready" + s)
                self.gate_up_done = sem("gate_up_done" + s)
                self.silu_ready = sem("silu_ready" + s)
                self.z_ready = sem("z_ready" + s)
                self.zT_in_psum = sem("zT_in_psum" + s)
                self.zT_ready = sem("zT_ready" + s)
                self.down_done = sem("down_done" + s)
                self.y_ready = sem("y_ready" + s)
                self.y_stored = sem("y_stored" + s)
                self.y_free = sem("y_free" + s)
                self.back_in = [sem(f"back_in{b}_" + s) for b in range(2)]
                self.h_step = sem("h_step" + s)

        moe = [Moe(i) for i in range(DEPTH)]
        ROUTED = 18
        consts_ready = sem("consts_ready")
        const_step = sem("const_step")
        h_in = sem("h_in")
        out_stored = sem("out_stored")
        pool_tick = sem("pool_tick")


        def pool_constants():
            st = Steps(const_step)

            def wait():
                nc.gpsimd.wait_ge(const_step, st.n)

            st.done(nc.gpsimd.memset(ones[:], 1.0))
            st.done(nc.gpsimd.memset(half_shift[0:SLOTS, :], -2.0))
            wait()
            st.done(nc.gpsimd.memset(half_shift[SLOTS:P, :], -1.0))
            wait()
            st.done(nc.gpsimd.affine_select(out=ident[:], in_=ones[:], compare_op=ALU.is_equal, fill=0.0, base=0,
                                            pattern=[[-1, P]], channel_multiplier=1))
            st.done(nc.gpsimd.affine_select(out=earlier[:], in_=ones[:], compare_op=ALU.is_gt, fill=0.0, base=0,
                                            pattern=[[1, P]], channel_multiplier=-1))
            st.done(nc.gpsimd.iota(slot_of_col[:], pattern=[[0, 2], [1, SLOTS]], base=0, channel_multiplier=0,
                                   allow_small_or_imprecise_dtypes=True))
            st.done(nc.gpsimd.iota(expert_iota[:], pattern=[[1, N_EXP]], base=0, channel_multiplier=0,
                                   allow_small_or_imprecise_dtypes=True))
            st.done(nc.gpsimd.iota(group_iota[:], pattern=[[1, N_GRP], [0, PER_GRP]], base=0, channel_multiplier=0,
                                   allow_small_or_imprecise_dtypes=True))
            st.done(nc.gpsimd.iota(round_starts[:], pattern=[[SLOTS, T // SLOTS - 1]], base=SLOTS, channel_multiplier=0,
                                   allow_small_or_imprecise_dtypes=True))
            st.done(nc.gpsimd.iota(token_code[:].rearrange("p t k -> p (t k)"), pattern=[[2 * P, TT], [1, 2]], base=1,
                                   channel_multiplier=2, allow_small_or_imprecise_dtypes=True))
            nc.gpsimd.iota(token_next[:].rearrange("p t k -> p (t k)"), pattern=[[P, TT], [0, 2]], base=1,
                           channel_multiplier=1, allow_small_or_imprecise_dtypes=True).then_inc(consts_ready, 1)

        FREE2 = 2
        FREE1 = 1

        def sp_moe_params(m, sp):
            i = m.layer
            with nc.allow_non_contiguous_dma("small router tables"):
                sp.dma_start(m.g_row, a["norm2_g"][i:i + 1, :].broadcast_to([P, D])).then_inc(m.params_in, 16)
                sp.dma_start(m.w_route[:, :, 0:N_GRP],
                             a["moe_w_group"][i].rearrange("(p c) g -> p c g", p=P)).then_inc(m.params_in, 16)
                sp.dma_start(m.w_route[:, :, N_GRP:],
                             a["moe_w_expert"][i].rearrange("(p c) g -> p c g", p=P)).then_inc(m.params_in, 16)
                sp.dma_start(m.b_route[:, 0:N_GRP],
                             a["moe_b_group"][i:i + 1, :].broadcast_to([P, N_GRP])).then_inc(m.params_in, 16)
                sp.dma_start(m.b_route[:, N_GRP:],
                             a["moe_b_expert"][i:i + 1, :].broadcast_to([P, N_EXP])).then_inc(m.params_in, 16)

        def sp_load_expert(m, sp, j, e):
            n = m.layer * N_EXP + e
            for src, dst in ((wg_rows, ring[j]["up"][:, 0]), (wu_rows, ring[j]["up"][:, 1]), (wd_rows, ring[j]["down"])):
                s = src[n:n + 1] if isinstance(n, int) else src[bass.ds(n, 1)]
                sp.dma_start(dst, s.rearrange("o p k f -> (o p) k f")).then_inc(m.w_in[j], 16)

        def sp_moe_weights(m, sp, first_free):
            for j in range(RING):
                first_free(j)
                sp_load_expert(m, sp, j, j)
            with sp.Fori(1, NG) as g:
                for j in range(RING):
                    sp.wait_ge(m.down_done, FREE2 + 4 * g + (j - 3))
                    sp_load_expert(m, sp, j, g * RING + j)
            sp.wait_ge(m.rounds_ready, 1)
            rounds = sp.value_load(m.rounds[0:1, 0:1].bitcast(i32), min_val=1, max_val=T // SLOTS)
            with sp.If(rounds > 1):
                with sp.Fori(1, rounds) as r:
                    with sp.Fori(0, NG) as g:
                        for j in range(RING):
                            sp.wait_ge(m.down_done, FREE2 + N_EXP * r + 4 * g + (j - 3))
                            sp_load_expert(m, sp, j, g * RING + j)
            return rounds

        def act_norm(m, act, store):
            for t in range(TT):
                nc.scalar.activation(m.dump, h[:, t, :], ACT.Square,
                                     accum_out=m.ss[:, t:t + 1]).then_inc(m.squares, 1)
                act.wait_ge(m.squares, t + 1)
            act.wait_ge(m.rstd_step, 1)
            nc.scalar.activation(m.rstd, m.rstd, ACT.Ln).then_inc(m.rstd_step, 1)
            act.wait_ge(m.rstd_step, 2)
            nc.scalar.activation(m.rstd, m.rstd, ACT.Exp, scale=-0.5).then_inc(m.rstd_step, 1)
            for t in range(TT):
                if store:
                    act.wait_ge(m.hn_ready, t + 1)
                    act.dma_start(normed[m.layer][t * P:(t + 1) * P, :], m.hn[t % 2]).then_inc(m.hn_stored[t % 2], 16)
                act.wait_ge(m.hnT_in_psum, t + 1)
                for half in range(2):
                    nc.scalar.copy(m.hnT[:, 4 * half:4 * half + 4, t * P:(t + 1) * P],
                                   bank[half].rearrange("p (c t) -> p c t", t=P)).then_inc(m.hnT_ready, 1)

        def dve_norm(m, dve, store):
            dve.wait_ge(m.squares, TT)
            nc.vector.tensor_scalar(m.rstd, m.ss, 1.0 / D, RMS_EPS, ALU.mult, ALU.add).then_inc(m.rstd_step, 1)
            dve.wait_ge(m.rstd_step, 3)
            dve.wait_ge(m.params_in, 16 * m.n_params)
            for t in range(TT):
                if t >= 2:
                    if store:
                        dve.wait_ge(m.hn_stored[t % 2], 16)
                    dve.wait_ge(m.hnT_in_psum, t - 1)
                nc.vector.scalar_tensor_tensor(out=m.hn[t % 2], in0=h[:, t, :], scalar=m.rstd[:, t:t + 1], in1=m.g_row,
                                               op0=ALU.mult, op1=ALU.mult).then_inc(m.hn_ready, 1)

        def pe_norm(m, pe):
            pe.wait_ge(consts_ready, 1)
            for t in range(TT):
                pe.wait_ge(m.hn_ready, t + 1)
                if t:
                    pe.wait_ge(m.hnT_ready, 2 * t)
                rows = m.hn[t % 2].rearrange("p (f c) -> p c f", c=C)
                for c in range(C):
                    last = nc.tensor.transpose(bank[c // 4][:, (c % 4) * P:(c % 4 + 1) * P], rows[:, c, :], ident[:])
                last.then_inc(m.hnT_in_psum, 1)

        def pe_logits(m, pe):
            pe.wait_ge(m.params_in, 16 * m.n_params)
            n = N_GRP + N_EXP
            for t in range(TT):
                pe.wait_ge(m.hnT_ready, 2 * t + 2)
                for c in range(C):
                    last = nc.tensor.matmul(bank[2][:, t * n:(t + 1) * n], m.hnT[:, c, t * P:(t + 1) * P],
                                            m.w_route[:, c, :], start=(c == 0), stop=(c == C - 1))
            last.then_inc(m.logits_in_psum, 1)

        def dve_route(m, dve):
            st = Steps(m.route)

            def step(ins):
                dve.wait_ge(m.route, st.done(ins))

            n = N_GRP + N_EXP
            dve.wait_ge(consts_ready, 1)
            step(nc.vector.memset(m.gl, -3.0e38))
            dve.wait_ge(m.logits_in_psum, 1)
            step(nc.vector.tensor_tensor(m.logits, bank[2][:, 0:TT * n].rearrange("p (t n) -> p t n", n=n),
                                         m.b_route.unsqueeze(1).broadcast_to([P, TT, n]), ALU.add))
            step(nc.vector.tensor_copy(m.gl[:, :, 0:N_GRP], m.logits[:, :, 0:N_GRP]))
            for t in range(TT):
                last = nc.vector.max(m.gmax[:, t, :], m.gl[:, t, :])
            step(last)
            for t in range(TT):
                last = nc.vector.max_index(m.gidx[:, t, :].bitcast(u32), m.gmax[:, t, :], m.gl[:, t, :])
            step(last)
            step(nc.vector.tensor_copy(m.gidx_f, m.gidx[:, :, 0].bitcast(u32)))
            step(nc.vector.tensor_tensor(m.in_group, group_iota[:].unsqueeze(1).broadcast_to([P, TT, N_EXP]),
                                         m.gidx_f.unsqueeze(2).broadcast_to([P, TT, N_EXP]), ALU.is_equal))
            step(nc.vector.tensor_scalar(m.in_group, m.in_group, -1.0, 3.0e38, ALU.add, ALU.mult))
            step(nc.vector.tensor_tensor(m.el, m.in_group, m.logits[:, :, N_GRP:], ALU.add))
            for t in range(TT):
                last = nc.vector.max(m.emax[:, t, :], m.el[:, t, :])
            step(last)
            for t in range(TT):
                last = nc.vector.max_index(m.eidx[:, t, :].bitcast(u32), m.emax[:, t, :], m.el[:, t, :])
            step(last)
            step(nc.vector.tensor_copy(m.eidx_f, m.eidx[:, :, 0:2].bitcast(u32)))
            for k in range(2):
                last = nc.vector.tensor_tensor(m.pick[:, :, k, :], expert_iota[:].unsqueeze(1).broadcast_to([P, TT, N_EXP]),
                                               m.eidx_f[:, :, k:k + 1].broadcast_to([P, TT, N_EXP]), ALU.is_equal)
            step(last)
            step(nc.vector.tensor_tensor(m.picks, m.pick[:, :, 0, :], m.pick[:, :, 1, :], ALU.add))
            step(nc.vector.tensor_tensor(m.gexp, m.logits[:, :, 0:N_GRP], m.gmax[:, :, 0:1].broadcast_to([P, TT, N_GRP]),
                                         ALU.subtract))
            step(nc.vector.tensor_tensor(m.ediff, m.emax[:, :, 1], m.emax[:, :, 0], ALU.subtract))
            for half, code in enumerate((token_code, token_next)):
                last = nc.vector.tensor_tensor(m.route_rhs[:, :, :, half * N_EXP:(half + 1) * N_EXP], m.pick,
                                               code[:].unsqueeze(3).broadcast_to([P, TT, 2, N_EXP]), ALU.mult)
            step(last)
            dve.wait_ge(m.exp_ready, 2)
            step(nc.vector.tensor_reduce(m.gsum, m.gexp, AX.X, ALU.add))
            assert st.n == ROUTED
            step(nc.vector.reciprocal(m.p_top, m.gsum))
            step(nc.vector.tensor_scalar(m.ediff, m.eexp, 1.0, None, ALU.add))
            step(nc.vector.reciprocal(m.ediff, m.ediff))
            step(nc.vector.tensor_tensor(m.gate[:, 0, :], m.ediff, m.p_top, ALU.mult))
            step(nc.vector.tensor_tensor(m.gate[:, 1, :], m.gate[:, 0, :], m.eexp, ALU.mult))
            dve.wait_ge(m.rank_in_psum, 1)
            ranks = bank[3][:, 0:TT * N_EXP].rearrange("p (t e) -> p t e", e=N_EXP)
            for k in range(2):
                last = nc.vector.tensor_tensor(m.ranked[:, :, k, :], ranks, m.pick[:, :, k, :], ALU.mult)
            step(last)
            step(nc.vector.tensor_reduce(m.rank, m.ranked, AX.X, ALU.add))
            step(nc.vector.tensor_reduce(m.cmax, bank[3][:, TT * N_EXP:(TT + 1) * N_EXP], AX.X, ALU.max))
            step(nc.vector.tensor_scalar(m.over, round_starts[:], m.cmax, None, ALU.is_lt))
            step(nc.vector.tensor_reduce(m.n_over, m.over, AX.X, ALU.add))
            nc.vector.tensor_scalar(m.rounds.bitcast(i32), m.n_over, 1.0, None, ALU.add).then_inc(m.rounds_ready, 1)

        def act_route(m, act):
            act.wait_ge(m.route, 16)
            nc.scalar.activation(m.gexp, m.gexp, ACT.Exp).then_inc(m.exp_ready, 1)
            nc.scalar.activation(m.eexp, m.ediff, ACT.Exp).then_inc(m.exp_ready, 1)

        def pe_ranks(m, pe):
            pe.wait_ge(m.route, 14)
            for t in range(TT + 1):
                o = bank[3][:, t * N_EXP:(t + 1) * N_EXP]
                for u in range(min(t + 1, TT)):
                    last = nc.tensor.matmul(o, earlier[:] if u == t else ones[:], m.picks[:, u, :],
                                            start=(u == 0), stop=(u == min(t, TT - 1)))
            last.then_inc(m.rank_in_psum, 1)

        def load_rounds(m, eng):
            eng.wait_ge(m.rounds_ready, 1)
            return eng.value_load(m.rounds[0:1, 0:1].bitcast(i32), min_val=1, max_val=T // SLOTS)

        def dve_slots(m, dve, r):
            for i in range(TT * 2):
                nc.vector.tensor_scalar(m.hot[:, i, :], slot_of_col[:], m.rank[:, i // 2, i % 2:i % 2 + 1], None,
                                        ALU.is_equal).then_inc(m.hot_ready, 1)
            S = 7
            dve.wait_ge(m.hot_ready, TT * 2 * (r + 1))
            nc.vector.tensor_scalar(m.rank, m.rank, -float(SLOTS), None, ALU.add).then_inc(m.slot_step, 1)
            dve.wait_ge(m.slot_step, S * r + 1)
            dve.wait_ge(m.slots_in_psum, r + 1)
            dve.wait_ge(m.round_done, r + 1)
            v = bank[2][:, 0:2 * N_EXP]
            nc.vector.tensor_scalar(m.far, v, 0.0, FAR, ALU.is_equal, ALU.mult).then_inc(m.slot_step, 1)
            nc.vector.tensor_scalar(m.idx[:, 0:N_EXP], v[:, 0:N_EXP], 2.0, half_shift[:, 0:1], ALU.mult,
                                    ALU.add).then_inc(m.slot_step, 1)
            nc.vector.tensor_scalar(m.idx[:, N_EXP:], v[:, N_EXP:], -1.0, None, ALU.add).then_inc(m.slot_step, 1)
            dve.wait_ge(m.slot_step, S * r + 4)
            nc.vector.tensor_tensor(m.scatter_at.bitcast(i32), m.idx[:, 0:N_EXP], m.far[:, 0:N_EXP],
                                    ALU.add).then_inc(m.slot_step, 1)
            for half in range(2):
                p = slice(half * SLOTS, (half + 1) * SLOTS)
                pairs = m.idx[p, N_EXP:].rearrange("p (m b) -> p b m", b=2)[:, half, :]
                fars = m.far[p, N_EXP:].rearrange("p (m b) -> p b m", b=2)[:, half, :]
                nc.vector.tensor_tensor(m.gather_at[p, :].bitcast(i32), pairs, fars, ALU.add).then_inc(m.slot_step, 1)
            dve.wait_ge(m.slot_step, S * r + S)
            dve.sem_inc(m.tables_ready, 1)

        def pe_slots(m, pe, r):
            for i in range(TT * 2):
                pe.wait_ge(m.hot_ready, TT * 2 * r + i + 1)
                last = nc.tensor.matmul(bank[2][:, 0:2 * N_EXP], m.hot[:, i, :], m.route_rhs[:, i // 2, i % 2, :],
                                        start=(i == 0), stop=(i == TT * 2 - 1))
            last.then_inc(m.slots_in_psum, 1)

        def pool_moe(m, pool):
            for b in range(2):
                pool.wait_ge(m.squares, TT)
                nc.gpsimd.memset(m.xg[b], 0.0).then_inc(m.xg_cleared, 1)
            pool.wait_ge(m.xg_cleared, 2)
            pool.sem_inc(m.z_ready, FREE2)
            pool.sem_inc(m.gate_up_done, FREE2)
            pool.sem_inc(m.down_done, FREE2)
            pool.sem_inc(m.y_ready, FREE2)
            pool.sem_inc(m.zT_ready, FREE1)
            pool.sem_inc(m.xT_ready, FREE1)
            pool.sem_inc(m.y_free, RING)
            pool.sem_inc(m.round_done, 1)
            rounds = load_rounds(m, pool)
            for b in range(2):
                pool.wait_ge(m.hn_stored[b], 16 * TT // 2)

            def gather(b, pair, copies):
                nc.gpsimd.tensor_copy(m.gather_now[:, b:b + 1].bitcast(i32),
                                      m.gather_at[:, bass.ds(pair, 1)].bitcast(i32)).then_inc(m.index_ready, 1)
                pool.wait_ge(m.index_ready, copies + 1)
                pool.sem_inc(pool_tick)
                nc.gpsimd.indirect_dma_start(
                    m.xg[b], None, normed[m.layer],
                    bass.IndirectOffsetOnAxis(ap=m.gather_now[:, b:b + 1].bitcast(u32), axis=0),
                    bounds_check=T - 1, oob_is_err=False).then_inc(m.xg_in[b], 16)

            with pool.Fori(0, rounds) as r:
                pool.wait_ge(m.tables_ready, r + 1)
                pool.sem_inc(pool_tick)
                copied = (N_EXP + NG * 2) * r
                for b in range(2):
                    gather(b, b, copied + b)

                def scatter(n, j, e, copies):
                    pool.wait_ge(m.y_ready, FREE2 + n + 1)
                    pool.sem_inc(pool_tick)
                    nc.gpsimd.tensor_copy(m.scatter_now[:, j:j + 1].bitcast(i32),
                                          m.scatter_at[:, bass.ds(e, 1)].bitcast(i32)).then_inc(m.index_ready, 1)
                    pool.wait_ge(m.index_ready, copies + 1)
                    pool.sem_inc(pool_tick)
                    nc.gpsimd.indirect_dma_start(
                        chosen[m.layer],
                        bass.IndirectOffsetOnAxis(ap=m.scatter_now[:, j:j + 1].bitcast(u32), axis=0),
                        m.y[j], None, bounds_check=T * 4 - 1, oob_is_err=False).then_inc(m.y_stored, 16)

                def scattered(n):
                    pool.wait_ge(m.y_stored, 16 * n + 16)
                    pool.sem_inc(m.y_free)

                with pool.Fori(0, NG - 1) as g:
                    for j in range(RING):
                        scatter(N_EXP * r + 4 * g + j, j, 4 * g + j, copied + 2 + 6 * g + j + (j + 1) // 2)
                        if j % 2 == 0:
                            pool.wait_ge(m.xT_in_psum, NG * 2 * r + 2 * g + (j // 2 + 1))
                            pool.sem_inc(pool_tick)
                            gather(j // 2, 2 * g + (j // 2 + 2), copied + 2 + 6 * g + 3 * (j // 2) + 1)
                        scattered(N_EXP * r + 4 * g + j)
                for j in range(RING):
                    e = N_EXP - RING + j
                    scatter(N_EXP * r + e, j, e, copied + 2 + 6 * (NG - 1) + j)
                    scattered(N_EXP * r + e)
                pool.sem_inc(m.round_done, 1)
            return rounds

        def pe_moe(m, pe):
            rounds = load_rounds(m, pe)
            with pe.Fori(0, rounds) as r:
                pe_slots(m, pe, r)

                def gate_up(g, j):
                    n = N_EXP * r + 4 * g + j
                    pair = NG * 2 * r + 2 * g + j // 2
                    b = j // 2
                    if j % 2 == 0:
                        pe.wait_ge(m.xg_in[b], 16 * NG * r + 16 * g + 16)
                        pe.wait_ge(m.xT_ready, FREE1 + pair)
                        rows = m.xg[b].rearrange("p (f c) -> p c f", c=C)
                        for c in range(C):
                            last = nc.tensor.transpose(bank[c // 4][:, (c % 4) * P:(c % 4 + 1) * P], rows[:, c, :],
                                                       ident[:])
                        last.then_inc(m.xT_in_psum, 1)
                        pe.wait_ge(m.xT_ready, FREE1 + 1 + pair)
                    pe.wait_ge(m.w_in[j], 48 * NG * r + 48 * g + 48)
                    pe.wait_ge(m.z_ready, n + 1)
                    o = bank[4 + j % 2]
                    for c in range(C):
                        for half in range(2):
                            last = nc.tensor.matmul(
                                o[half * SLOTS:(half + 1) * SLOTS, 0:F_EXP].rearrange("p (u f) -> p u f", u=2),
                                m.xT[b][:, c, (j % 2) * SLOTS:(j % 2 + 1) * SLOTS],
                                ring[j]["up"][:, :, c, half * P:(half + 1) * P], start=(c == 0), stop=(c == C - 1))
                    last.then_inc(m.gate_up_done, 1)

                def down(g, j):
                    n = N_EXP * r + 4 * g + j
                    pe.wait_ge(m.z_ready, FREE2 + 1 + n)
                    pe.wait_ge(m.zT_ready, FREE1 + n)
                    nc.tensor.transpose(bank[3][:, 0:P], m.z[j % 2], ident[:]).then_inc(m.zT_in_psum, 1)
                    pe.wait_ge(m.zT_ready, FREE1 + 1 + n)
                    pe.wait_ge(m.y_ready, n + 1)
                    for k in range(2):
                        for half in range(2):
                            last = nc.tensor.matmul(bank[6 + j % 2][half * SLOTS:(half + 1) * SLOTS, :],
                                                    m.zT[j % 2][:, k, :],
                                                    ring[j]["down"][:, k, half * 512:(half + 1) * 512],
                                                    start=(k == 0), stop=(k == 1))
                    last.then_inc(m.down_done, 1)

                gate_up(0, 0)
                with pe.Fori(0, NG - 1) as g:
                    for j in range(RING):
                        gate_up(g + (j + 1) // RING, (j + 1) % RING)
                        down(g, j)
                for j in range(RING):
                    if j + 1 < RING:
                        gate_up(NG - 1, j + 1)
                    down(NG - 1, j)

        def act_moe(m, act):
            rounds = load_rounds(m, act)
            with act.Fori(0, rounds) as r:
                with act.Fori(0, NG) as g:
                    for j in range(RING):
                        n = N_EXP * r + 4 * g + j
                        act.wait_ge(m.gate_up_done, FREE2 + 1 + n)
                        act.wait_ge(m.z_ready, n + 1)
                        nc.scalar.activation(m.silu[j % 2], bank[4 + j % 2][:, 0:P], ACT.Silu).then_inc(m.silu_ready, 1)
                        act.wait_ge(m.zT_in_psum, n + 1)
                        act.wait_ge(m.down_done, n + 1)
                        nc.scalar.copy(m.zT[j % 2].rearrange("p k s -> p (k s)"), bank[3][:, 0:P]).then_inc(m.zT_ready, 1)
                        act.wait_ge(m.down_done, FREE2 + 1 + n)
                        act.wait_ge(m.y_free, n + 1)
                        nc.scalar.copy(m.y[j], bank[6 + j % 2][:]).then_inc(m.y_ready, 1)
            return rounds

        def dve_moe(m, dve):
            rounds = load_rounds(m, dve)
            with dve.Fori(0, rounds) as r:
                dve_slots(m, dve, r)
                with dve.Fori(0, NG) as g:
                    for j in range(RING):
                        n = N_EXP * r + 4 * g + j
                        if j % 2 == 0:
                            pair = NG * 2 * r + 2 * g + j // 2
                            dve.wait_ge(m.xT_in_psum, pair + 1)
                            dve.wait_ge(m.gate_up_done, n)
                            flat = m.xT[j // 2].rearrange("p c s -> p (c s)")
                            nc.vector.tensor_copy(flat[:, 0:512], bank[0][:])
                            nc.vector.tensor_copy(flat[:, 512:1024], bank[1][:]).then_inc(m.xT_ready, 1)
                        dve.wait_ge(m.silu_ready, n + 1)
                        nc.vector.tensor_tensor(m.z[j % 2], m.silu[j % 2], bank[4 + j % 2][:, P:2 * P],
                                                ALU.mult).then_inc(m.z_ready, 1)
            return rounds

        def act_load_back(m, act, rounds):
            back = chosen[m.layer].rearrange("(t p c) n -> t p (c n)", p=P, c=4)
            act.wait_ge(m.round_done, rounds + 1)
            for t in range(TT):
                if t >= 2:
                    act.wait_ge(m.h_step, 2 * (t - 1))
                act.dma_start(m.back[t % 2], back[t]).then_inc(m.back_in[t % 2], 16)

        def dve_combine(m, dve):
            for t in range(TT):
                dve.wait_ge(m.back_in[t % 2], 16 * (t // 2 + 1))
                for k in range(2):
                    if k:
                        dve.wait_ge(m.h_step, 2 * t + 1)
                    nc.vector.scalar_tensor_tensor(out=h[:, t, :], in0=m.back[t % 2][:, k * D:(k + 1) * D],
                                                   scalar=m.gate[:, k, t:t + 1], in1=h[:, t, :], op0=ALU.mult,
                                                   op1=ALU.add).then_inc(m.h_step, 1)

        CH = 64
        HD = 64
        NCH = T // CH
        CP = NCH // 2
        PAIRS = D // P
        DECAY = float(np.exp(-0.5))
        N_VEC = 10
        W0, A0, KK, KA, RK, LNG, LNB, NW0, NA0, KA1 = range(N_VEC)


        class Rwkv:
            def __init__(self):
                m = Arena(big)
                self.layer = 0
                self.hnT = m.take(C, T)
                self.xr, self.xk, self.xv = (m.take(C, T) for _ in range(3))
                self.yg = m.take(PAIRS, T)
                self.w = m.take(3, C, P)
                self.w_lora = m.take(3, P)
                self.hid = m.take(3, T)
                self.vec = m.take(N_VEC, PAIRS)
                self.pv = m.take(N_VEC)
                hn_at = m.at
                self.hn = [m.take(D) for _ in range(2)]
                self.lora1 = m.take(C, 2 * 64 + P)
                self.mu = m.take(6, C)
                self.ss, self.rstd = m.take(TT), m.take(TT)
                self.keep = m.take(T)
                self.upper = m.take(CH)
                self.upper_incl = m.take(CH)
                self.u_in, self.u_out = m.take(CH), m.take(CH)
                self.l_in, self.l_out = m.take(CH), m.take(CH)
                self.eye = m.take(CH)
                self.block16 = m.take(CH)
                self.tmp_mask = m.take(CH)
                self.heads = m.take(P)
                self.head_mean = m.take(P)
                tiles = m.at
                t = Arena(big, tiles)
                self.dump = big[:, tiles:tiles + D]
                self.g_row = big[:, tiles + D:tiles + 2 * D]
                self.xx = big[:, tiles + 2 * D:tiles + 2 * D + C * T].rearrange("p (c t) -> p c t", t=T)
                self.xw = self.yg
                self.xa = big[:, tiles + 6 * D:tiles + 6 * D + C * T].rearrange("p (c t) -> p c t", t=T)
                self.xg_ = self.xv
                f = Arena(big, tiles)
                lo = Arena(big, 0)
                (self.sig, self.a, self.cum, self.cprev, self.wc, self.winv, self.wprev, self.kk2, self.kkn,
                 self.at, self.kka, self.bt, self.km, self.k2, self.kt, self.rt, self.rk, self.v, self.g, self.rs,
                 self.bv) = (f.take(T) for _ in range(21))
                (self.ud, self.uo, self.ld, self.lo_, self.mrb, self.lak, self.mrk, self.lv) = (lo.take(2, CP, CH) for _ in range(8))
                dead = Arena(big, hn_at)
                (self.att, self.btt, self.ktt, self.vt) = (dead.take(CP, P) for _ in range(4))
                self.dr, self.x1 = (dead.take(2, CP, 2 * CH) for _ in range(2))
                self.wz = self.dr
                (self.v1, self.u2, self.l2, self.u4, self.v2, self.l4, self.v4, self.l8, self.dt, self.mm, self.mt,
                 self.m2) = (
                    x.rearrange("p (h c t) -> p h c t", h=2, t=CH) for x in (
                        self.sig, self.cum, self.cprev, self.winv, self.wprev, self.kk2, self.kkn, self.kka,
                        self.km, self.k2, self.rs, self.a))
                self.gi = f.take(2, CP, CH)
                self.rh = self.x1.rearrange("p h c t -> p (h c t)")[:, 0:T].rearrange(
                    "p (b c t) -> p b c t", b=2, t=CH)
                self.st = f.take(NCH, HD)
                self.y = self.ktt.rearrange("p c t -> p (c t)")
                self.yc = self.att.rearrange("p c t -> p (c t)")
                self.ysq = self.gi.rearrange("p b c t -> p (b c t)")
                self.yr = self.x1.rearrange("p h c t -> p (h c t)")[:, T:2 * T]
                self.wo = big[:, C * T:C * T + PAIRS * D].rearrange("p (q d) -> p q d", d=D)
                self.n_params = 1
                (self.params_in, self.squares, self.rstd_step, self.hn_ready, self.hnT_in_psum, self.hnT_ready,
                 self.mask_step, self.masks_ready, self.vec_in, self.vec_ready, self.mu_in, self.lora_in,
                 self.xx_ready, self.xw_ready, self.xa_ready, self.xg_ready, self.xr_ready, self.xk_ready,
                 self.xv_ready, self.hw_in_psum, self.ha_in_psum, self.hg_in_psum, self.hw_ready, self.ha_ready,
                 self.hg_exp, self.hg_step, self.w_in, self.projected, self.s_ps, self.s_ready, self.pair_done,
                 self.wo_in, self.mix_ps, self.mixed) = (sem("rwkv_" + n) for n in (
                    "params_in squares rstd_step hn_ready hnT_in_psum hnT_ready mask_step masks_ready "
                    "vec_in vec_ready mu_in lora_in xx_ready xw_ready xa_ready xg_ready xr_ready "
                    "xk_ready xv_ready hw_in_psum ha_in_psum hg_in_psum hw_ready ha_ready hg_exp "
                    "hg_step w_in projected s_ps s_ready pair_done wo_in mix_ps mixed").split())
                (self.w_ps, self.a_ps, self.k_ps, self.r_ps, self.n2_ps, self.v_ps, self.g_ps, self.bonus_ps,
                 self.vt_ps, self.att_ps, self.btt_ps, self.ktt_ps, self.ub_ps, self.l_ps, self.lk_ps, self.u2_ps,
                 self.l2_ps, self.u4_ps, self.v2_ps, self.l4_ps, self.lv_ps, self.v4_ps, self.l8_ps, self.dt_ps,
                 self.mm_ps, self.mt_ps, self.dr_ps, self.m2_ps, self.x1_ps, self.wz_ps, self.rg_ps, self.z_ps,
                 self.y_ps, self.mean_ps, self.var_ps) = signals(sem("rwkv_tensor_results"), 35)
                (self.ew, self.ea, self.kk2_ready, self.wc_ready, self.winv_ready, self.wprev_ready, self.ln_ready,
                 self.rs_ready, self.v_ready, self.g_ready, self.vt_ready, self.att_ready, self.btt_ready,
                 self.ktt_ready, self.l2_ready, self.u4_ready, self.l4_ready, self.lv_ready, self.l8_ready,
                 self.mm_ready, self.dr_ready, self.m2_ready, self.y_ready, self.ysq_ready, self.yln_ready,
                 self.yrstd) = signals(sem("rwkv_scalar_results"), 26)
                (self.pv_ready, self.sig1_ready, self.sig_ready, self.cum_ready, self.cprev_ready, self.a1_ready,
                 self.a_ready, self.km_ready, self.n2_ready, self.k2_ready, self.kt_ready, self.kkn_ready,
                 self.at_ready, self.kka_ready, self.bt_ready, self.rt_ready, self.rk_ready, self.bv_ready,
                 self.ud_ready, self.masked_ub, self.masked_l, self.v1_ready, self.masked_lk, self.u2_ready,
                 self.v2_ready, self.v4_ready, self.dt_ready, self.mt_ready, self.x1_ready, self.wz_ready,
                 self.gi_ready, self.rh_ready, self.yc_ready, self.yvar, self.yn1_ready, self.yn2_ready,
                 self.yn3_ready) = signals(sem("rwkv_vector_results"), 37)

        rw = Rwkv()
        pe_tick = sem("pe_tick")

        def pe_wait(pe, s, value):
            pe.wait_ge(s, value)
            pe.sem_inc(pe_tick)

        def pool_rwkv_masks(m, pool):
            st = Steps(m.mask_step)

            def step(ins):
                pool.wait_ge(m.mask_step, st.done(ins))

            sel = nc.gpsimd.affine_select
            step(nc.gpsimd.memset(m.keep, 1.0))
            step(nc.gpsimd.memset(m.keep.rearrange("p (c t) -> p c t", t=CH)[:, :, 0:1], 0.0))
            step(nc.gpsimd.memset(m.heads, 0.0))
            step(nc.gpsimd.memset(m.head_mean, 0.0))
            for half in range(2):
                p = slice(half * CH, half * CH + CH)
                step(nc.gpsimd.memset(m.heads[p, half * HD:half * HD + HD], 1.0))
                step(nc.gpsimd.memset(m.head_mean[p, half * HD:half * HD + HD], 1.0 / HD))
                one = ones[p, 0:CH]
                step(sel(out=m.upper[p, :], in_=one, compare_op=ALU.is_gt, fill=0.0, base=0, pattern=[[1, CH]],
                         channel_multiplier=-1))
                step(sel(out=m.upper_incl[p, :], in_=one, compare_op=ALU.is_ge, fill=0.0, base=0, pattern=[[1, CH]],
                         channel_multiplier=-1))
                step(sel(out=m.eye[p, :], in_=one, compare_op=ALU.is_equal, fill=0.0, base=0, pattern=[[-1, CH]],
                         channel_multiplier=1))
                step(sel(out=m.tmp_mask[p, :], in_=one, compare_op=ALU.is_ge, fill=0.0, base=0,
                         pattern=[[-16, CH // 16], [0, 16]], channel_multiplier=1))
                step(sel(out=m.block16[p, :], in_=m.tmp_mask[p, :], compare_op=ALU.is_ge, fill=0.0, base=15,
                         pattern=[[16, CH // 16], [0, 16]], channel_multiplier=-1))
                step(sel(out=m.u_in[p, :], in_=m.block16[p, :], compare_op=ALU.is_gt, fill=0.0, base=0,
                         pattern=[[1, CH]], channel_multiplier=-1))
                step(sel(out=m.l_in[p, :], in_=m.block16[p, :], compare_op=ALU.is_gt, fill=0.0, base=0,
                         pattern=[[-1, CH]], channel_multiplier=1))
                step(sel(out=m.l_out[p, :], in_=one, compare_op=ALU.is_gt, fill=0.0, base=0, pattern=[[-1, CH]],
                         channel_multiplier=1))
            step(nc.gpsimd.tensor_tensor(m.u_out, m.upper, m.u_in, ALU.subtract))
            nc.gpsimd.tensor_tensor(m.l_out, m.l_out, m.l_in, ALU.subtract).then_inc(m.masks_ready, 1)
            pool.sem_inc(m.pair_done, 1)

        def sp_rwkv(m, sp):
            i = 0
            sp.dma_start(h[:], a["x"].rearrange("b (t p) d -> (b p) t d", p=P)).then_inc(h_in, 16)
            sp.dma_start(m.g_row, a["norm1_g"][0:1, :].broadcast_to([P, D])).then_inc(m.params_in, 16)
            with nc.allow_non_contiguous_dma("per-channel vectors"):
                sp.dma_start(m.mu, a["rwkv_mu"][i].rearrange("n (p c) -> p n c", p=P)).then_inc(m.mu_in, 16)
                for n, src in ((W0, a["rwkv_w0"][i]), (A0, a["rwkv_a0"][i]), (KK, a["rwkv_k_k"][i]),
                               (KA, a["rwkv_k_a"][i]), (RK, a["rwkv_r_k"][i].rearrange("h n -> (h n)")),
                               (LNG, a["rwkv_ln_g"][i]), (LNB, a["rwkv_ln_b"][i])):
                    sp.dma_start(m.vec[:, n, :], src.rearrange("(q p) -> p q", p=P)).then_inc(m.vec_in, 16)
            col = 0
            for src, n in (("rwkv_w1", 64), ("rwkv_a1", 64), ("rwkv_g1", P)):
                sp.dma_start(m.lora1[:, :, col:col + n],
                             a[src][i].rearrange("(p c) n -> p c n", p=P)).then_inc(m.lora_in, 16)
                col += n
            w_rkv = a["rwkv_w_rkv"][i].rearrange("n (p c) d -> p n c d", p=P)

            def load_pair(q):
                for n in range(3):
                    sp.dma_start(m.w[:, n], w_rkv[:, n, :, bass.ds(q * P, P)]).then_inc(m.w_in, 16)
                for n, (src, rows) in enumerate((("rwkv_w2", 64), ("rwkv_a2", 64), ("rwkv_g2", P))):
                    sp.dma_start(m.w_lora[0:rows, n], a[src][i][:, bass.ds(q * P, P)]).then_inc(m.w_in, 16)

            load_pair(0)
            with sp.Fori(1, PAIRS) as q:
                sp.wait_ge(m.projected, q)
                load_pair(q)
            sp.wait_ge(m.projected, PAIRS)
            sp.dma_start(m.wo, a["rwkv_w_o"][i].rearrange("(q p) d -> p q d", p=P)).then_inc(m.wo_in, 16)

        def dve_rwkv_lerps(m, dve):
            dve.wait_ge(m.hnT_ready, 2 * TT)
            nc.vector.tensor_scalar(m.xx[:, :, 0:1], m.hnT[:, :, 0:1], -1.0, None, ALU.mult)
            nc.vector.tensor_tensor(m.xx[:, :, 1:T], m.hnT[:, :, 0:T - 1], m.hnT[:, :, 1:T],
                                    ALU.subtract).then_inc(m.xx_ready, 1)
            dve.wait_ge(m.xx_ready, 1)
            dve.wait_ge(m.mu_in, 16)
            for out_, n, s in ((m.xw, 1, m.xw_ready), (m.xa, 4, m.xa_ready), (m.xg_, 5, m.xg_ready),
                               (m.xk, 2, m.xk_ready), (m.xr, 0, m.xr_ready), (m.xv, 3, m.xv_ready)):
                if n == 3:
                    dve.wait_ge(m.hg_in_psum, 1)
                for c in range(C):
                    last = nc.vector.scalar_tensor_tensor(out=out_[:, c, :], in0=m.xx[:, c, :],
                                                          scalar=m.mu[:, n, c:c + 1], in1=m.hnT[:, c, :],
                                                          op0=ALU.mult, op1=ALU.add)
                last.then_inc(s, 1)
            dve.wait_ge(m.vec_in, 16 * 7)
            nc.vector.tensor_scalar(m.vec[:, NW0, :], m.vec[:, W0, :], -1.0, None, ALU.mult)
            nc.vector.tensor_scalar(m.vec[:, NA0, :], m.vec[:, A0, :], -1.0, None, ALU.mult)
            nc.vector.tensor_scalar(m.vec[:, KA1, :], m.vec[:, KA, :], -1.0, 1.0, ALU.mult, ALU.add).then_inc(m.vec_ready, 1)
            dve.wait_ge(m.hg_exp, 1)
            nc.vector.tensor_scalar(m.hid[:, 2, :], m.hid[:, 2, :], 1.0, None, ALU.add).then_inc(m.hg_step, 1)
            dve.wait_ge(m.hg_step, 1)
            nc.vector.reciprocal(m.hid[:, 2, :], m.hid[:, 2, :]).then_inc(m.hg_step, 1)

        def pe_rwkv_hidden(m, pe):
            pe.wait_ge(m.lora_in, 48)
            col = 0
            for x, rows, s, done, o in ((m.xw, 64, m.xw_ready, m.hw_in_psum, bank[2]),
                                        (m.xa, 64, m.xa_ready, m.ha_in_psum, bank[3]),
                                        (m.xg_, P, m.xg_ready, m.hg_in_psum, bank[4])):
                pe.wait_ge(s, 1)
                for c in range(C):
                    last = nc.tensor.matmul(o[0:rows, :], m.lora1[:, c, col:col + rows], x[:, c, :], start=(c == 0),
                                            stop=(c == C - 1))
                last.then_inc(done, 1)
                col += rows

        def act_rwkv_hidden(m, act):
            act.wait_ge(m.hw_in_psum, 1)
            nc.scalar.activation(m.hid[0:64, 0, :], bank[2][0:64, :], ACT.Tanh).then_inc(m.hw_ready, 1)
            act.wait_ge(m.ha_in_psum, 1)
            nc.scalar.copy(m.hid[0:64, 1, :], bank[3][0:64, :]).then_inc(m.ha_ready, 1)
            act.wait_ge(m.hg_in_psum, 1)
            nc.scalar.activation(m.hid[:, 2, :], bank[4], ACT.Exp, scale=-1.0).then_inc(m.hg_exp, 1)

        B_W, B_A, B_K, B_R, B_V, B_G, B_N2, B_BONUS = range(8)

        def units():
            for hd in range(2):
                for cp in range(CP):
                    for par in range(2):
                        yield hd, cp, par

        def half(i):
            return slice(64 * i, 64 * i + 64)

        def two_banks(i, lo_, n):
            return psum[:, i * 512:(i + 2) * 512].rearrange("p (b n) -> p b n", b=2)[:, :, lo_:lo_ + n]

        def pe_rwkv_pair(m, pe, q):
            def project(n, x, s, b, done):
                pe.wait_ge(s, 1)
                for c in range(C):
                    last = nc.tensor.matmul(bank[b], m.w[:, n, c, :], x[:, c, :], start=(c == 0), stop=(c == C - 1))
                last.then_inc(done.now(), 1)

            pe_wait(pe, m.w_in, 96 * q + 96)
            pe_wait(pe, m.pair_done, q + 1)
            pe.wait_ge(m.hw_ready, 1)
            nc.tensor.matmul(bank[B_W], m.w_lora[0:64, 0], m.hid[0:64, 0, :], start=True, stop=True).then_inc(m.w_ps.now(), 1)
            pe.wait_ge(m.ha_ready, 1)
            nc.tensor.matmul(bank[B_A], m.w_lora[0:64, 1], m.hid[0:64, 1, :], start=True, stop=True).then_inc(m.a_ps.now(), 1)
            project(1, m.xk, m.xk_ready, B_K, m.k_ps)
            project(0, m.xr, m.xr_ready, B_R, m.r_ps)
            pe_wait(pe, m.kk2_ready.sem, m.kk2_ready.by(q))
            nc.tensor.matmul(bank[B_N2], m.heads, m.kk2, start=True, stop=True).then_inc(m.n2_ps.now(), 1)
            project(2, m.xv, m.xv_ready, B_V, m.v_ps)
            pe.wait_ge(m.hg_step, 2)
            nc.tensor.matmul(bank[B_G], m.w_lora[:, 2], m.hid[:, 2, :], start=True, stop=True).then_inc(m.g_ps.now(), 1)
            pe_wait(pe, m.g_ps.sem, m.g_ps.by(q))
            pe.sem_inc(m.projected)
            pe_wait(pe, m.rk_ready.sem, m.rk_ready.by(q))
            nc.tensor.matmul(bank[B_BONUS], m.heads, m.rk, start=True, stop=True).then_inc(m.bonus_ps.now(), 1)

            def flip(src, b, done):
                for i in range(CP):
                    last = nc.tensor.transpose(bank[b][:, i * P:(i + 1) * P], src[:, i * P:(i + 1) * P], ident[:])
                last.then_inc(done.now(), 1)

            pe_wait(pe, m.v_ready.sem, m.v_ready.by(q))
            flip(m.v, B_V, m.vt_ps)
            pe_wait(pe, m.at_ready.sem, m.at_ready.by(q))
            flip(m.at, B_W, m.att_ps)
            pe_wait(pe, m.bt_ready.sem, m.bt_ready.by(q))
            flip(m.bt, B_A, m.btt_ps)
            pe_wait(pe, m.kt_ready.sem, m.kt_ready.by(q))
            pe_wait(pe, m.g_ready.sem, m.g_ready.by(q))
            flip(m.kt, B_G, m.ktt_ps)

            def product(lhs, rhs, b, lo_):
                for hd, cp, par in units():
                    c = slice((2 * cp + par) * CH, (2 * cp + par + 1) * CH)
                    last = nc.tensor.matmul(bank[b + hd][half(par), lo_ + cp * CH:lo_ + (cp + 1) * CH],
                                            lhs[half(hd), c], rhs[half(hd), c], start=True, stop=True)
                return last

            pe_wait(pe, m.rt_ready.sem, m.rt_ready.by(q))
            pe_wait(pe, m.k2_ready.sem, m.k2_ready.by(q))
            product(m.bt, m.at, B_K, 0)
            product(m.bt, m.rt, B_K, 256).then_inc(m.ub_ps.now(), 1)
            pe_wait(pe, m.btt_ready.sem, m.btt_ready.by(q))
            pe_wait(pe, m.att_ready.sem, m.att_ready.by(q))
            product(m.at, m.bt, B_W, 0).then_inc(m.l_ps.now(), 1)
            pe_wait(pe, m.bv_ready.sem, m.bv_ready.by(q))
            product(m.kt, m.at, B_N2, 0)
            product(m.kt, m.rt, B_N2, 256).then_inc(m.lk_ps.now(), 1)

            def blocks(lhs, rhs, b, n=CH, lo_=0):
                for hd, cp, par in units():
                    o = bank[b] if n == CH else bank[b + hd]
                    at = (hd * CP + cp) * CH if n == CH else cp * 2 * CH + lo_
                    w = rhs(hd, cp, par)
                    last = nc.tensor.matmul(o[half(par), at:at + w.shape[1]], lhs(hd, cp, par), w, start=True, stop=True)
                return last

            def mat(x):
                return lambda hd, cp, par: x[half(par), hd, cp, :]

            def tok(x):
                return lambda hd, cp, par: x[half(par), cp, hd * HD:(hd + 1) * HD]

            pe_wait(pe, m.masked_l.sem, m.masked_l.by(q))
            pe_wait(pe, m.masked_ub.sem, m.masked_ub.by(q))
            pe_wait(pe, m.vt_ready.sem, m.vt_ready.by(q))
            pe_wait(pe, m.ktt_ready.sem, m.ktt_ready.by(q))
            blocks(mat(m.ld), mat(m.ud), 4).then_inc(m.u2_ps.now(), 1)
            blocks(mat(m.ud), mat(m.ld), 5).then_inc(m.l2_ps.now(), 1)
            pe_wait(pe, m.l2_ready.sem, m.l2_ready.by(q))
            pe_wait(pe, m.u2_ready.sem, m.u2_ready.by(q))
            pe_wait(pe, m.v1_ready.sem, m.v1_ready.by(q))
            blocks(mat(m.l2), mat(m.u2), 2).then_inc(m.u4_ps.now(), 1)
            blocks(mat(m.l2), mat(m.v1), 3).then_inc(m.v2_ps.now(), 1)
            pe_wait(pe, m.masked_lk.sem, m.masked_lk.by(q))
            blocks(mat(m.u2), mat(m.l2), 6).then_inc(m.l4_ps.now(), 1)
            blocks(mat(m.lak), tok(m.vt), 0).then_inc(m.lv_ps.now(), 1)
            pe_wait(pe, m.l4_ready.sem, m.l4_ready.by(q))
            pe_wait(pe, m.v2_ready.sem, m.v2_ready.by(q))
            blocks(mat(m.l4), mat(m.v2), 7).then_inc(m.v4_ps.now(), 1)
            pe_wait(pe, m.u4_ready.sem, m.u4_ready.by(q))
            blocks(mat(m.u4), mat(m.l4), 4).then_inc(m.l8_ps.now(), 1)
            pe_wait(pe, m.l8_ready.sem, m.l8_ready.by(q))
            pe_wait(pe, m.v4_ready.sem, m.v4_ready.by(q))
            blocks(mat(m.l8), mat(m.v4), 5).then_inc(m.dt_ps.now(), 1)
            pe_wait(pe, m.dt_ready.sem, m.dt_ready.by(q))
            blocks(mat(m.lo_), mat(m.dt), 2).then_inc(m.mm_ps.now(), 1)
            blocks(mat(m.dt), mat(m.lo_), 3).then_inc(m.mt_ps.now(), 1)
            pe_wait(pe, m.lv_ready.sem, m.lv_ready.by(q))
            blocks(mat(m.dt), tok(m.att), 6, n=2 * CH)
            blocks(mat(m.dt), mat(m.lv), 6, n=2 * CH, lo_=CH).then_inc(m.dr_ps.now(), 1)
            pe_wait(pe, m.mm_ready.sem, m.mm_ready.by(q))
            pe_wait(pe, m.mt_ready.sem, m.mt_ready.by(q))
            blocks(mat(m.mt), mat(m.mm), 4).then_inc(m.m2_ps.now(), 1)
            pe_wait(pe, m.dr_ready.sem, m.dr_ready.by(q))
            blocks(mat(m.mm), mat(m.dr), 0, n=2 * CH).then_inc(m.x1_ps.now(), 1)
            pe_wait(pe, m.m2_ready.sem, m.m2_ready.by(q))
            pe_wait(pe, m.x1_ready.sem, m.x1_ready.by(q))
            blocks(mat(m.m2), mat(m.x1), 4, n=2 * CH).then_inc(m.wz_ps.now(), 1)
            pe_wait(pe, m.wz_ready.sem, m.wz_ready.by(q))

            for hd, cp, par in units():
                w = m.wz[half(par), hd, cp, 0:CH]
                nc.tensor.matmul(bank[2 + par][half(hd), cp * CH:(cp + 1) * CH], w, m.mrb[half(par), hd, cp, :],
                                 start=True, stop=True)
                last = nc.tensor.matmul(bank[2 + par][half(hd), 256 + cp * CH:256 + (cp + 1) * CH], w,
                                        m.btt[half(par), cp, hd * HD:(hd + 1) * HD], start=True, stop=True)
            last.then_inc(m.rg_ps.now(), 1)
            for hd, cp, par in units():
                z = m.wz[half(par), hd, cp, CH:2 * CH]
                v = m.vt[half(par), cp, hd * HD:(hd + 1) * HD]
                o = bank[0 + par][half(hd), cp * CH:(cp + 1) * CH]
                nc.tensor.matmul(o, m.btt[half(par), cp, hd * HD:(hd + 1) * HD], z, start=(cp == 0), stop=False,
                                 skip_group_check=True)
                nc.tensor.matmul(o, m.ktt[half(par), cp, hd * HD:(hd + 1) * HD], v, start=False, stop=False,
                                 skip_group_check=True)
                o = bank[6 + par][half(hd), cp * CH:(cp + 1) * CH]
                nc.tensor.matmul(o, z, m.mrb[half(par), hd, cp, :], start=(cp == 0), stop=False, skip_group_check=True)
                last = nc.tensor.matmul(o, v, m.mrk[half(par), hd, cp, :], start=False, stop=False,
                                        skip_group_check=True)
            last.then_inc(m.z_ps.now(), 1)
            pe_wait(pe, m.gi_ready.sem, m.gi_ready.by(q))
            pe_wait(pe, m.rh_ready.sem, m.rh_ready.by(q))
            pe_wait(pe, m.z_ps.sem, m.z_ps.by(q))
            for c in range(NCH):
                cp, par = c // 2, c % 2
                pe_wait(pe, m.s_ready, NCH * q + c + 1)
                if c + 1 < NCH:
                    for hd in range(2):
                        last = nc.tensor.matmul(bank[0 + par][half(hd), cp * CH:(cp + 1) * CH],
                                                m.gi[half(hd), par, cp, :], m.st[half(hd), c, :], start=False, stop=True,
                                                skip_group_check=True)
                    last.then_inc(m.s_ps, 1)
                for hd in range(2):
                    last = nc.tensor.matmul(bank[6 + par][half(hd), cp * CH:(cp + 1) * CH], m.st[half(hd), c, :],
                                            m.rh[half(hd), par, cp, :], start=False, stop=True, skip_group_check=True)
            last.then_inc(m.y_ps.now(), 1)
            pe_wait(pe, m.y_ready.sem, m.y_ready.by(q))
            nc.tensor.matmul(bank[2], m.head_mean, m.y, start=True, stop=True).then_inc(m.mean_ps.now(), 1)
            pe_wait(pe, m.ysq_ready.sem, m.ysq_ready.by(q))
            nc.tensor.matmul(bank[3], m.head_mean, m.ysq, start=True, stop=True).then_inc(m.var_ps.now(), 1)

        def act_rwkv_pair(m, act, q):
            pv = m.pv
            act.wait_ge(m.pv_ready.sem, m.pv_ready.by(q))
            act.wait_ge(m.w_ps.sem, m.w_ps.by(q))
            nc.scalar.activation(m.sig, bank[B_W], ACT.Exp, bias=pv[:, NW0:NW0 + 1], scale=-1.0).then_inc(m.ew.now(), 1)
            act.wait_ge(m.a_ps.sem, m.a_ps.by(q))
            nc.scalar.activation(m.a, bank[B_A], ACT.Exp, bias=pv[:, NA0:NA0 + 1], scale=-1.0).then_inc(m.ea.now(), 1)
            act.wait_ge(m.k_ps.sem, m.k_ps.by(q))
            nc.scalar.activation(m.kk2, bank[B_K], ACT.Square, scale=pv[:, KK:KK + 1]).then_inc(m.kk2_ready.now(), 1)
            act.wait_ge(m.cum_ready.sem, m.cum_ready.by(q))
            nc.scalar.activation(m.wc, m.cum, ACT.Exp, scale=-DECAY).then_inc(m.wc_ready.now(), 1)
            nc.scalar.activation(m.winv, m.cum, ACT.Exp, scale=DECAY).then_inc(m.winv_ready.now(), 1)
            act.wait_ge(m.cprev_ready.sem, m.cprev_ready.by(q))
            nc.scalar.activation(m.wprev, m.cprev, ACT.Exp, scale=-DECAY).then_inc(m.wprev_ready.now(), 1)
            act.wait_ge(m.n2_ready.sem, m.n2_ready.by(q))
            nc.scalar.activation(m.rs, m.rs, ACT.Ln).then_inc(m.ln_ready.now(), 1)
            act.wait_ge(m.ln_ready.sem, m.ln_ready.by(q))
            nc.scalar.activation(m.rs, m.rs, ACT.Exp, scale=-0.5).then_inc(m.rs_ready.now(), 1)
            act.wait_ge(m.v_ps.sem, m.v_ps.by(q))
            nc.scalar.copy(m.v, bank[B_V]).then_inc(m.v_ready.now(), 1)
            act.wait_ge(m.g_ps.sem, m.g_ps.by(q))
            nc.scalar.copy(m.g, bank[B_G]).then_inc(m.g_ready.now(), 1)

            def take(s, dst, src, done):
                act.wait_ge(s.sem, s.by(q))
                nc.scalar.copy(dst, src).then_inc(done.now(), 1)

            def flat(x):
                return x.rearrange("p a b c -> p (a b c)") if len(x.shape) == 4 else x.rearrange("p a b -> p (a b)")

            take(m.vt_ps, flat(m.vt), bank[B_V], m.vt_ready)
            take(m.att_ps, flat(m.att), bank[B_W], m.att_ready)
            take(m.btt_ps, flat(m.btt), bank[B_A], m.btt_ready)
            take(m.ktt_ps, flat(m.ktt), bank[B_G], m.ktt_ready)
            take(m.l2_ps, flat(m.l2), bank[5], m.l2_ready)
            take(m.u4_ps, flat(m.u4), bank[2], m.u4_ready)
            take(m.l4_ps, flat(m.l4), bank[6], m.l4_ready)
            take(m.lv_ps, flat(m.lv), bank[0], m.lv_ready)
            take(m.l8_ps, flat(m.l8), bank[4], m.l8_ready)
            take(m.mm_ps, flat(m.mm), bank[2], m.mm_ready)
            take(m.dr_ps, flat(m.dr), psum[:, 6 * 512:8 * 512], m.dr_ready)
            take(m.m2_ps, flat(m.m2), bank[4], m.m2_ready)
            for c in range(NCH - 1):
                cp, par = c // 2, c % 2
                act.wait_ge(m.s_ps, (NCH - 1) * q + c + 1)
                end = (c + 1) * CH - 1
                nc.scalar.activation(m.st[:, c + 1, :], bank[0 + par][:, cp * CH:(cp + 1) * CH], ACT.Copy,
                                     scale=m.wc[:, end:end + 1]).then_inc(m.s_ready, 1)
            act.wait_ge(m.y_ps.sem, m.y_ps.by(q))
            nc.scalar.copy(m.y.rearrange("p (c b t) -> p b c t", b=2, t=CH),
                           two_banks(6, 0, 256).rearrange("p b (c t) -> p b c t", t=CH)).then_inc(m.y_ready.now(), 1)
            act.wait_ge(m.yc_ready.sem, m.yc_ready.by(q))
            nc.scalar.activation(m.ysq, m.yc, ACT.Square).then_inc(m.ysq_ready.now(), 1)
            act.wait_ge(m.yvar.sem, m.yvar.by(q))
            nc.scalar.activation(m.yr, m.yr, ACT.Ln).then_inc(m.yln_ready.now(), 1)
            act.wait_ge(m.yln_ready.sem, m.yln_ready.by(q))
            nc.scalar.activation(m.yr, m.yr, ACT.Exp, scale=-0.5).then_inc(m.yrstd.now(), 1)

        def dve_rwkv_pair(m, dve, q):
            pv = m.pv
            TTn, STT, TS = nc.vector.tensor_tensor, nc.vector.scalar_tensor_tensor, nc.vector.tensor_scalar

            def w(*ss):
                for s in ss:
                    dve.wait_ge(s.sem, s.by(q))

            dve.wait_ge(m.pair_done, q + 1)
            nc.vector.tensor_copy(pv, m.vec[:, :, bass.ds(q, 1)].rearrange("p n o -> p (n o)")).then_inc(m.pv_ready.now(), 1)
            w(m.pv_ready, m.ew)
            TS(m.sig, m.sig, 1.0, None, ALU.add).then_inc(m.sig1_ready.now(), 1)
            w(m.sig1_ready)
            nc.vector.reciprocal(m.sig, m.sig).then_inc(m.sig_ready.now(), 1)
            w(m.sig_ready)
            nc.vector.tensor_tensor_scan(m.cum, m.keep, m.sig, 0.0, ALU.mult, ALU.add).then_inc(m.cum_ready.now(), 1)
            w(m.ea, m.cum_ready)
            TTn(m.cprev, m.cum, m.sig, ALU.subtract).then_inc(m.cprev_ready.now(), 1)
            TS(m.a, m.a, 1.0, None, ALU.add).then_inc(m.a1_ready.now(), 1)
            w(m.a1_ready)
            nc.vector.reciprocal(m.a, m.a).then_inc(m.a_ready.now(), 1)
            w(m.a_ready)
            TS(m.km, m.a, pv[:, KA:KA + 1], pv[:, KA1:KA1 + 1], ALU.mult, ALU.add).then_inc(m.km_ready.now(), 1)
            w(m.k_ps, m.kk2_ready, m.n2_ps)
            TS(m.rs, bank[B_N2], 1e-24, None, ALU.max).then_inc(m.n2_ready.now(), 1)
            w(m.km_ready)
            TTn(m.k2, bank[B_K], m.km, ALU.mult).then_inc(m.k2_ready.now(), 1)
            w(m.k2_ready, m.winv_ready)
            TTn(m.kt, m.k2, m.winv, ALU.mult).then_inc(m.kt_ready.now(), 1)
            w(m.rs_ready)
            STT(out=m.kkn, in0=bank[B_K], scalar=pv[:, KK:KK + 1], in1=m.rs, op0=ALU.mult, op1=ALU.mult).then_inc(m.kkn_ready.now(), 1)
            w(m.kkn_ready, m.wprev_ready)
            STT(out=m.at, in0=m.kkn, scalar=-1.0, in1=m.wprev, op0=ALU.mult, op1=ALU.mult).then_inc(m.at_ready.now(), 1)
            TTn(m.kka, m.kkn, m.a, ALU.mult).then_inc(m.kka_ready.now(), 1)
            w(m.kka_ready)
            TTn(m.bt, m.kka, m.winv, ALU.mult).then_inc(m.bt_ready.now(), 1)
            w(m.r_ps, m.wc_ready)
            TTn(m.rt, bank[B_R], m.wc, ALU.mult).then_inc(m.rt_ready.now(), 1)
            STT(out=m.rk, in0=bank[B_R], scalar=pv[:, RK:RK + 1], in1=m.k2, op0=ALU.mult, op1=ALU.mult).then_inc(m.rk_ready.now(), 1)
            w(m.bonus_ps, m.v_ready)
            TTn(m.bv, bank[B_BONUS], m.v, ALU.mult).then_inc(m.bv_ready.now(), 1)

            def mask(x):
                return x.unsqueeze(1).unsqueeze(1).broadcast_to([P, 2, CP, CH])

            def four(x):
                return x.rearrange("p b (c t) -> p b c t", t=CH)

            ub, ub2 = four(two_banks(B_K, 0, 256)), four(two_banks(B_K, 256, 256))
            w(m.ub_ps)
            TTn(m.ud, ub, mask(m.u_in), ALU.mult).then_inc(m.ud_ready.now(), 1)
            TTn(m.mrb, ub2, mask(m.upper_incl), ALU.mult).then_inc(m.masked_ub.now(), 1)
            w(m.l_ps)
            lb = four(two_banks(B_W, 0, 256))
            TTn(m.ld, lb, mask(m.l_in), ALU.mult)
            TTn(m.lo_, lb, mask(m.l_out), ALU.mult).then_inc(m.masked_l.now(), 1)
            w(m.ud_ready)
            TTn(m.v1, m.ud, mask(m.eye), ALU.add).then_inc(m.v1_ready.now(), 1)
            w(m.lk_ps)
            TTn(m.lak, four(two_banks(B_N2, 0, 256)), mask(m.upper), ALU.mult)
            TTn(m.mrk, four(two_banks(B_N2, 256, 256)), mask(m.upper_incl), ALU.mult).then_inc(m.masked_lk.now(), 1)

            def flat(x):
                return x.rearrange("p a b c -> p (a b c)")

            w(m.u2_ps)
            nc.vector.tensor_copy(flat(m.u2), bank[4]).then_inc(m.u2_ready.now(), 1)
            w(m.v1_ready, m.v2_ps)
            TTn(flat(m.v2), bank[3], flat(m.v1), ALU.add).then_inc(m.v2_ready.now(), 1)
            w(m.v2_ready, m.v4_ps)
            TTn(flat(m.v4), bank[7], flat(m.v2), ALU.add).then_inc(m.v4_ready.now(), 1)
            w(m.v4_ready, m.dt_ps)
            TTn(flat(m.dt), bank[5], flat(m.v4), ALU.add).then_inc(m.dt_ready.now(), 1)
            w(m.mt_ps)
            nc.vector.tensor_copy(flat(m.mt), bank[3]).then_inc(m.mt_ready.now(), 1)
            w(m.x1_ps, m.dr_ready)
            TTn(flat(m.x1), psum[:, 0:1024], flat(m.dr), ALU.add).then_inc(m.x1_ready.now(), 1)
            w(m.wz_ps, m.x1_ready)
            TTn(flat(m.wz), psum[:, 4 * 512:6 * 512], flat(m.x1), ALU.add).then_inc(m.wz_ready.now(), 1)
            w(m.rg_ps, m.wz_ready)
            TTn(m.gi, four(two_banks(2, 256, 256)), mask(m.eye), ALU.add).then_inc(m.gi_ready.now(), 1)
            TTn(m.rh, four(two_banks(2, 0, 256)), m.rt.rearrange("p (c b t) -> p b c t", b=2, t=CH),
                ALU.add).then_inc(m.rh_ready.now(), 1)
            nc.vector.memset(m.st[:, 0, :], 0.0).then_inc(m.s_ready, 1)
            w(m.y_ready, m.mean_ps)
            TTn(m.yc, m.y, bank[2], ALU.subtract).then_inc(m.yc_ready.now(), 1)
            w(m.var_ps)
            TS(m.yr, bank[3], 1.0, LNX_EPS, ALU.mult, ALU.add).then_inc(m.yvar.now(), 1)
            w(m.yrstd)
            TTn(m.yc, m.yc, m.yr, ALU.mult).then_inc(m.yn1_ready.now(), 1)
            w(m.yn1_ready)
            TS(m.yc, m.yc, pv[:, LNG:LNG + 1], pv[:, LNB:LNB + 1], ALU.mult, ALU.add).then_inc(m.yn2_ready.now(), 1)
            w(m.yn2_ready)
            TTn(m.yc, m.yc, m.bv, ALU.add).then_inc(m.yn3_ready.now(), 1)
            w(m.yn3_ready)
            TTn(m.yg[:, bass.ds(q, 1), :].rearrange("p o t -> p (o t)"), m.yc, m.g, ALU.mult).then_inc(m.pair_done, 1)

        def pe_mix_out(m, pe, src, wts, wts_in):
            pe.wait_ge(wts_in, 16)
            for t in range(TT):
                if t >= 2:
                    pe.wait_ge(m.mixed, t - 1)
                for nh in range(2):
                    for c in range(C):
                        last = nc.tensor.matmul(bank[4 * (t % 2) + nh], src[:, c, t * P:(t + 1) * P],
                                                wts[:, c, nh * 512:(nh + 1) * 512], start=(c == 0), stop=(c == C - 1))
                last.then_inc(m.mix_ps, 1)

        def dve_mix_out(m, dve):
            for t in range(TT):
                dve.wait_ge(m.mix_ps, t + 1)
                b = 4 * (t % 2)
                nc.vector.tensor_tensor(h[:, t, :], psum[:, b * 512:(b + 2) * 512], h[:, t, :],
                                        ALU.add).then_inc(m.mixed, 1)

        def pe_rwkv(m, pe):
            pe_norm(m, pe)
            pe_rwkv_hidden(m, pe)
            pe.wait_ge(m.masks_ready, 1)
            with pe.Fori(0, PAIRS) as q:
                pe_rwkv_pair(m, pe, q)
            pe.wait_ge(m.pair_done, PAIRS + 1)
            pe_mix_out(m, pe, m.yg, m.wo, m.wo_in)

        def act_rwkv(m, act):
            act.wait_ge(h_in, 16)
            act_norm(m, act, False)
            act_rwkv_hidden(m, act)
            with act.Fori(0, PAIRS) as q:
                act_rwkv_pair(m, act, q)

        def dve_rwkv(m, dve):
            dve.wait_ge(h_in, 16)
            dve_norm(m, dve, False)
            dve_rwkv_lerps(m, dve)
            dve.wait_ge(m.masks_ready, 1)
            dve.wait_ge(m.vec_ready, 1)
            dve.wait_ge(m.xw_ready, 1)
            with dve.Fori(0, PAIRS) as q:
                dve_rwkv_pair(m, dve, q)
            dve_mix_out(m, dve)

        TAPS = a["conv_w_dw"].shape[1]
        PAD = TAPS - 1
        B1A, B1B, BDW, CLG, CLB = range(5)
        CONV_RING = RING // 2

        def top_of_ring(places):
            return places * (2 * C * F_EXP + 2 * D)

        class Conv:
            def __init__(self):
                m = Arena(big, top_of_ring(CONV_RING))
                self.layer = 1
                self.n_params = 1
                self.w2 = m.take(C, D)
                self.w1 = [m.take(C, 2, P) for _ in range(2)]
                m.at = max(m.at, stage_base)
                self.hn = [m.take(D) for _ in range(2)]
                self.dump = self.hn[0]
                self.g_row = m.take(D)
                self.hnT = m.take(C, T)
                self.u = [m.take(PAD + T) for _ in range(2)]
                self.sig = [m.take(T) for _ in range(2)]
                self.co = m.take(C, T)
                self.vec = m.take(5, C)
                self.taps = m.take(C, TAPS)
                self.ss, self.rstd = m.take(TT), m.take(TT)
                self.mean_of = m.take(P)
                self.mean = m.take(T)
                self.rs = m.take(T)
                self.sq = [self.u[b][:, 0:T] for b in range(2)]
                (self.params_in, self.squares, self.rstd_step, self.hn_ready, self.hnT_in_psum, self.hnT_ready,
                 self.vec_in, self.w1_in0, self.w1_in1, self.w2_in, self.pads_ready, self.up_ps, self.sig_ready,
                 self.gated, self.tap, self.co_ready, self.mean_ps, self.centred, self.sq_ready, self.var_ps,
                 self.rs_step, self.normed_, self.act_ready, self.mix_ps, self.mixed, self.bias_in, self.biased,
                 self.mean_of_ready) = (sem("conv_" + n) for n in (
                    "params_in squares rstd_step hn_ready hnT_in_psum hnT_ready vec_in w1_in0 w1_in1 "
                    "w2_in pads_ready up_ps sig_ready gated tap co_ready mean_ps centred sq_ready "
                    "var_ps rs_step normed_ act_ready mix_ps mixed bias_in biased mean_of_ready").split())

        cv = Conv()

        def sp_conv(m, sp, memory_free):
            memory_free()
            sp.dma_start(m.g_row, a["norm1_g"][1:2, :].broadcast_to([P, D])).then_inc(m.params_in, 16)
            w1 = a["conv_w_pw1"][0].rearrange("(p c) (u q n) -> p c u q n", p=P, u=2, n=P)

            def load_w1(q, b):
                for u in range(2):
                    src = w1[:, :, u, q, :] if isinstance(q, int) else \
                        w1[:, :, u, bass.ds(q, 1), :].rearrange("p c o n -> p c (o n)")
                    sp.dma_start(m.w1[b][:, :, u, :], src).then_inc(m.w1_in0 if b == 0 else m.w1_in1, 16)

            for b in range(2):
                load_w1(b, b)
            with nc.allow_non_contiguous_dma("per-channel vectors"):
                for n, src in ((B1A, a["conv_b_pw1"][0][0:D]), (B1B, a["conv_b_pw1"][0][D:2 * D]),
                               (BDW, a["conv_b_dw"][0]), (CLG, a["conv_ln_g"][0]), (CLB, a["conv_ln_b"][0])):
                    sp.dma_start(m.vec[:, n, :], src.rearrange("(q p) -> p q", p=P)).then_inc(m.vec_in, 16)
                for q in range(C):
                    sp.dma_start(m.taps[:, q, :],
                                 a["conv_w_dw"][0][:, q * P:(q + 1) * P].rearrange("k p -> p k")).then_inc(m.vec_in, 16)
            sp.dma_start(m.w2, a["conv_w_pw2"][0].rearrange("(q p) d -> p q d", p=P)).then_inc(m.w2_in, 16)
            with sp.Fori(1, C // 2) as g:
                for b in range(2):
                    sp.wait_ge(m.up_ps, 2 * g + (b - 1))
                    load_w1(2 * g + b, b)
            sp.wait_ge(m.hn_ready, TT)
            sp.dma_start(m.g_row, a["conv_b_pw2"][0:1, :].broadcast_to([P, D])).then_inc(m.bias_in, 16)

        def pool_conv(m, pool, memory_free):
            memory_free()
            nc.gpsimd.memset(m.u[0][:, 0:PAD], 0.0).then_inc(m.pads_ready, 1)
            nc.gpsimd.memset(m.u[1][:, 0:PAD], 0.0).then_inc(m.pads_ready, 1)
            nc.gpsimd.memset(m.mean_of, 1.0 / D).then_inc(m.mean_of_ready, 1)
            pool.sem_inc(m.gated, FREE2)
            pool.sem_inc(m.co_ready, FREE2)

        def pe_conv(m, pe):
            pe_norm(m, pe)
            pe.wait_ge(m.hnT_ready, 2 * TT)
            with pe.Fori(0, C // 2) as g:
                for b in range(2):
                    q = 2 * g + b
                    pe_wait(pe, m.w1_in0 if b == 0 else m.w1_in1, 32 * g + 32)
                    pe_wait(pe, m.gated, q + 1)
                    for u in range(2):
                        for c in range(C):
                            last = nc.tensor.matmul(bank[2 + 2 * b + u], m.w1[b][:, c, u, :], m.hnT[:, c, :],
                                                    start=(c == 0), stop=(c == C - 1))
                    last.then_inc(m.up_ps, 1)
            pe.wait_ge(m.mean_of_ready, 1)
            for q in range(C):
                pe.wait_ge(m.co_ready, FREE2 + q + 1)
                last = nc.tensor.matmul(bank[0], m.mean_of, m.co[:, q, :], start=(q == 0), stop=(q == C - 1))
            last.then_inc(m.mean_ps, 1)
            for q in range(C):
                pe.wait_ge(m.sq_ready, q + 1)
                nc.tensor.matmul(bank[1], m.mean_of, m.sq[q % 2], start=(q == 0),
                                 stop=(q == C - 1)).then_inc(m.var_ps, 1)
            pe.wait_ge(m.act_ready, C)
            pe_mix_out(m, pe, m.co, m.w2, m.w2_in)

        def act_conv(m, act, memory_free):
            memory_free()
            act_norm(m, act, False)
            act.wait_ge(m.vec_in, 16 * (5 + C))
            with act.Fori(0, C // 2) as g:
                for b in range(2):
                    q = 2 * g + b
                    act.wait_ge(m.up_ps, q + 1)
                    act.wait_ge(m.gated, q + 1)
                    nc.scalar.activation(m.sig[b], bank[3 + 2 * b], ACT.Sigmoid,
                                         bias=m.vec[:, B1B, bass.ds(q, 1)]).then_inc(m.sig_ready, 1)
            for q in range(C):
                act.wait_ge(m.centred, q + 1)
                if q >= 2:
                    act.wait_ge(m.var_ps, q - 1)
                nc.scalar.activation(m.sq[q % 2], m.co[:, q, :], ACT.Square).then_inc(m.sq_ready, 1)
            act.wait_ge(m.rs_step, 1)
            nc.scalar.activation(m.rs, m.rs, ACT.Ln).then_inc(m.rs_step, 1)
            act.wait_ge(m.rs_step, 2)
            nc.scalar.activation(m.rs, m.rs, ACT.Exp, scale=-0.5).then_inc(m.rs_step, 1)
            for q in range(C):
                act.wait_ge(m.normed_, q + 1)
                nc.scalar.activation(m.co[:, q, :], m.co[:, q, :], ACT.Silu, bias=m.vec[:, CLB, q:q + 1],
                                     scale=m.vec[:, CLG, q:q + 1]).then_inc(m.act_ready, 1)

        def dve_conv(m, dve, memory_free):
            memory_free()
            dve_norm(m, dve, False)
            dve.wait_ge(m.vec_in, 16 * (5 + C))
            dve.wait_ge(m.pads_ready, 2)
            with dve.Fori(0, C // 2) as g:
                for b in range(2):
                    q = 2 * g + b
                    dve.wait_ge(m.sig_ready, q + 1)
                    dve.wait_ge(m.co_ready, q + 1)
                    nc.vector.scalar_tensor_tensor(out=m.u[b][:, PAD:], in0=bank[2 + 2 * b],
                                                   scalar=m.vec[:, B1A, bass.ds(q, 1)], in1=m.sig[b], op0=ALU.add,
                                                   op1=ALU.mult).then_inc(m.gated, 1)
                    dve.wait_ge(m.gated, FREE2 + q + 1)
                    o = m.co[:, bass.ds(q, 1), :].rearrange("p o t -> p (o t)")
                    w = m.taps[:, bass.ds(q, 1), :].rearrange("p o k -> p (o k)")
                    nc.vector.tensor_scalar(o, m.u[b][:, 0:T], w[:, 0:1], m.vec[:, BDW, bass.ds(q, 1)], ALU.mult,
                                            ALU.add).then_inc(m.tap, 1)
                    for k in range(1, TAPS):
                        dve.wait_ge(m.tap, (TAPS - 1) * q + k)
                        last = nc.vector.scalar_tensor_tensor(out=o, in0=m.u[b][:, k:k + T], scalar=w[:, k:k + 1],
                                                              in1=o, op0=ALU.mult, op1=ALU.add)
                        last.then_inc(m.tap if k < TAPS - 1 else m.co_ready, 1)
            dve.wait_ge(m.bias_in, 16)
            for t in range(TT):
                nc.vector.tensor_tensor(h[:, t, :], h[:, t, :], m.g_row, ALU.add).then_inc(m.biased, 1)
            dve.wait_ge(m.mean_ps, 1)
            nc.vector.tensor_copy(m.mean, bank[0]).then_inc(m.mean_of_ready, 1)
            dve.wait_ge(m.mean_of_ready, 2)
            for q in range(C):
                nc.vector.tensor_tensor(m.co[:, q, :], m.co[:, q, :], m.mean, ALU.subtract).then_inc(m.centred, 1)
            dve.wait_ge(m.var_ps, C)
            nc.vector.tensor_scalar(m.rs, bank[1], LN_EPS, None, ALU.add).then_inc(m.rs_step, 1)
            dve.wait_ge(m.rs_step, 3)
            for q in range(C):
                nc.vector.tensor_tensor(m.co[:, q, :], m.co[:, q, :], m.rs, ALU.mult).then_inc(m.normed_, 1)
            dve.wait_ge(m.biased, TT)
            dve_mix_out(m, dve)

        block = ctx.enter_context(nc.Block())

        class Final:

            def __init__(self):
                m = Arena(big)
                self.n_params = 1
                self.hn = [m.take(D) for _ in range(2)]
                self.dump = m.take(D)
                self.g_row = m.take(D)
                self.ss, self.rstd = m.take(TT), m.take(TT)
                (self.params_in, self.squares, self.rstd_step, self.hn_ready, self.stored0, self.stored1) = (sem("final_" + n) for n in (
                    "params_in squares rstd_step hn_ready stored0 stored1").split())
                self.hn_stored = [self.stored0, self.stored1]

        fin = Final()

        @block.sync
        def _(sp):
            sp_rwkv(rw, sp)
            sp.wait_ge(rw.mixed, TT)
            sp_moe_params(moe[0], sp)
            sp_moe_weights(moe[0], sp, lambda j: None)
            sp_conv(cv, sp, lambda: sp.wait_ge(moe[0].h_step, 2 * TT))

            def place_free(j):
                if j == CONV_RING:
                    sp.wait_ge(cv.mixed, TT)
                    sp_moe_params(moe[1], sp)

            sp_moe_weights(moe[1], sp, place_free)
            sp.wait_ge(moe[1].h_step, 2 * TT)
            sp.dma_start(fin.g_row, a["final_g"].rearrange("(o d) -> o d", o=1).broadcast_to([P, D])
                         ).then_inc(fin.params_in, 16)
            out_tiles = out.rearrange("b (t p) d -> (b t) p d", p=P)
            for t in range(TT):
                sp.wait_ge(fin.hn_ready, t + 1)
                sp.dma_start(out_tiles[t], fin.hn[t % 2]).then_inc(fin.hn_stored[t % 2], 16)
            for b in range(2):
                sp.wait_ge(fin.hn_stored[b], 16 * TT // 2)

        @block.gpsimd
        def _(pool):
            pool_constants()
            pool.wait_ge(consts_ready, 1)
            pool_rwkv_masks(rw, pool)
            pool_moe(moe[0], pool)
            pool_conv(cv, pool, lambda: pool.wait_ge(moe[0].h_step, 2 * TT))
            pool_moe(moe[1], pool)

        @block.scalar
        def _(act):
            act_rwkv(rw, act)
            for m, before in ((moe[0], rw.mixed), (moe[1], cv.mixed)):
                act.wait_ge(before, TT)
                act_norm(m, act, True)
                act_route(m, act)
                rounds = act_moe(m, act)
                act_load_back(m, act, rounds)
                if m is moe[0]:
                    act_conv(cv, act, lambda: act.wait_ge(moe[0].h_step, 2 * TT))
            act.wait_ge(moe[1].h_step, 2 * TT)
            for t in range(TT):
                nc.scalar.activation(fin.dump, h[:, t, :], ACT.Square,
                                     accum_out=fin.ss[:, t:t + 1]).then_inc(fin.squares, 1)
                act.wait_ge(fin.squares, t + 1)
            act.wait_ge(fin.rstd_step, 1)
            nc.scalar.activation(fin.rstd, fin.rstd, ACT.Ln).then_inc(fin.rstd_step, 1)
            act.wait_ge(fin.rstd_step, 2)
            nc.scalar.activation(fin.rstd, fin.rstd, ACT.Exp, scale=-0.5).then_inc(fin.rstd_step, 1)

        @block.vector
        def _(dve):
            dve_rwkv(rw, dve)
            for m, before in ((moe[0], rw.mixed), (moe[1], cv.mixed)):
                dve.wait_ge(before, TT)
                dve_norm(m, dve, True)
                dve_route(m, dve)
                dve_moe(m, dve)
                dve_combine(m, dve)
                if m is moe[0]:
                    dve_conv(cv, dve, lambda: dve.wait_ge(moe[0].h_step, 2 * TT))
            dve.wait_ge(fin.squares, TT)
            nc.vector.tensor_scalar(fin.rstd, fin.ss, 1.0 / D, RMS_EPS, ALU.mult, ALU.add).then_inc(fin.rstd_step, 1)
            dve.wait_ge(fin.rstd_step, 3)
            dve.wait_ge(fin.params_in, 16)
            for t in range(TT):
                if t >= 2:
                    dve.wait_ge(fin.hn_stored[t % 2], 16)
                nc.vector.scalar_tensor_tensor(out=fin.hn[t % 2], in0=h[:, t, :], scalar=fin.rstd[:, t:t + 1],
                                               in1=fin.g_row, op0=ALU.mult, op1=ALU.mult).then_inc(fin.hn_ready, 1)

        @block.tensor
        def _(pe):
            pe_rwkv(rw, pe)
            for m in moe:
                pe_norm(m, pe)
                pe_logits(m, pe)
                pe_ranks(m, pe)
                pe_moe(m, pe)
                if m is moe[0]:
                    pe_conv(cv, pe)


_INS = ["x", "norm1_g", "norm2_g", "final_g", "rwkv_mu", "rwkv_w_rkv", "rwkv_w0", "rwkv_w1", "rwkv_w2", "rwkv_a0",
        "rwkv_a1", "rwkv_a2", "rwkv_g1", "rwkv_g2", "rwkv_k_k", "rwkv_k_a", "rwkv_r_k", "rwkv_ln_g", "rwkv_ln_b",
        "rwkv_w_o", "conv_w_pw1", "conv_b_pw1", "conv_w_dw", "conv_b_dw", "conv_ln_g", "conv_ln_b", "conv_w_pw2",
        "conv_b_pw2", "moe_w_group", "moe_b_group", "moe_w_expert", "moe_b_expert", "moe_w_gate", "moe_w_up",
        "moe_w_down"]


def kernel(**inputs):
    import numpy as _np
    import concourse.bacc as _bacc
    from concourse import mybir as _mybir
    from concourse.bass_utils import run_bass_kernel_spmd as _run

    nc = _bacc.Bacc("TRN2", target_bir_lowering=False, num_devices=1)
    arrays, args = {}, {}
    for name in _INS:
        v = _np.ascontiguousarray(inputs[name])
        arrays[f"in_{name}_dram"] = v
        args[name] = nc.dram_tensor(f"in_{name}_dram", v.shape, _mybir.dt.from_np(v.dtype), kind="ExternalInput").ap()
    out = nc.dram_tensor("out_dram", (1, T, D), _mybir.dt.float32, kind="ExternalOutput").ap()
    bass_hybrid_rwkv7_conformer_hmoe(nc, args, out)
    r = _run(nc, [arrays], core_ids=[0])
    return r.results[0]["out_dram"]
```

```python
import numpy as np

import concourse.bass as bass
from concourse import mybir
from contextlib import ExitStack

D = 1024
T = 512
DEPTH = 2
P = 128
TT = T // P
C = D // P
N_EXP = 32
N_GRP = 4
PER_GRP = N_EXP // N_GRP
F_EXP = 256
SLOTS = 64
RING = 4
NG = N_EXP // RING
RMS_EPS = 1e-6
FAR = 60000.0
LNX_EPS = 64e-5
LN_EPS = 1e-5


class Arena:

    def __init__(self, tensor, start=0):
        self.tensor, self.at = tensor, start

    def take(self, *shape, parts=P):
        n = 1
        for s in shape:
            n *= s
        v = self.tensor[0:parts, self.at:self.at + n]
        self.at += n
        assert self.at <= self.tensor.shape[1], (self.at, self.tensor.shape)
        if len(shape) == 2:
            v = v.rearrange("p (a b) -> p a b", b=shape[1])
        if len(shape) == 3:
            v = v.rearrange("p (a b c) -> p a b c", b=shape[1], c=shape[2])
        return v


class Steps:

    def __init__(self, sem):
        self.sem, self.n = sem, 0

    def done(self, ins):
        self.n += 1
        ins.then_inc(self.sem, 1)
        return self.n


class Signal:

    def __init__(self, made, sem, at, per_trip):
        self.made, self.sem, self.at, self.per_trip = made, sem, at, per_trip

    def by(self, trip):
        return self.per_trip * trip + self.at

    def now(self):
        assert self.made[0] % self.per_trip == self.at - 1, self.at
        self.made[0] += 1
        return self.sem


def signals(sem, n):
    made = [0]
    return [Signal(made, sem, i + 1, n) for i in range(n)]


def bass_hybrid_rwkv7_conformer_hmoe(nc, a, out):
    fp32 = mybir.dt.float32
    u32 = mybir.dt.uint32
    i32 = mybir.dt.int32
    ALU = mybir.AluOpType
    ACT = mybir.ActivationFunctionType
    AX = mybir.AxisListType
    ctx = ExitStack()
    with ctx:
        def sb(name, shape, dt=fp32):
            return ctx.enter_context(nc.sbuf_tensor(name, shape, dt))

        def sem(name):
            return ctx.enter_context(nc.semaphore(name))

        h = sb("h", [P, TT, D])
        ident = sb("ident", [P, P])
        ones = sb("ones", [P, P])
        earlier = sb("earlier", [P, P])
        slot_of_col = sb("slot_of_col", [P, P])
        expert_iota = sb("expert_iota", [P, N_EXP])
        group_iota = sb("group_iota", [P, N_EXP])
        round_starts = sb("round_starts", [P, T // SLOTS - 1])
        token_code = sb("token_code", [P, TT, 2])
        half_shift = sb("half_shift", [P, 1])
        big = sb("big", [P, 48500 - TT * D])

        psum = ctx.enter_context(nc.psum_tensor("psum", [P, 8 * 512], fp32))
        bank = [psum[:, i * 512:(i + 1) * 512] for i in range(8)]

        chosen = [nc.dram_tensor(f"chosen{i}", [T * 4, D // 2], fp32, kind="Internal").ap() for i in range(DEPTH)]

        wg_rows = a["moe_w_gate"].rearrange("l e (p c) f -> (l e) p c f", p=P)
        wu_rows = a["moe_w_up"].rearrange("l e (p c) f -> (l e) p c f", p=P)
        wd_rows = a["moe_w_down"].rearrange("l e (k p) d -> (l e) p k d", p=P)

        top = Arena(big)
        ring = [dict(up=top.take(2, C, F_EXP), down=top.take(2, D)) for _ in range(RING)]
        stage_base = top.at

        class Moe:

            def __init__(self, layer):
                m = Arena(big, stage_base)
                self.layer = layer
                self.n_params = 5
                self.g_row = m.take(D)
                self.w_route = m.take(C, N_GRP + N_EXP)
                self.b_route = m.take(N_GRP + N_EXP)
                self.hn = [m.take(D) for _ in range(TT)]
                self.hnT = m.take(C, T)
                self.dump = self.hn[TT - 1]
                self.takes = [m.take(TT, 2 * SLOTS) for _ in range(2)]
                self.xT = [m.take(C, P) for _ in range(2)]
                self.silu = [m.take(P) for _ in range(2)]
                self.z = [m.take(P) for _ in range(2)]
                self.zT = [m.take(2, SLOTS) for _ in range(2)]
                self.y = [m.take(D // 2) for _ in range(RING)]
                n = N_GRP + N_EXP
                self.ss = m.take(TT)
                self.rstd = m.take(TT)
                self.logits = m.take(TT, n)
                self.gl = m.take(TT, 8)
                self.gmax = m.take(TT, 8)
                self.gidx = m.take(TT, 8)
                self.gidx_f = m.take(TT)
                self.in_group = m.take(TT, N_EXP)
                self.el = m.take(TT, N_EXP)
                self.emax = m.take(TT, 8)
                self.eidx = m.take(TT, 8)
                self.eidx_f = m.take(TT, 2)
                self.pick = m.take(TT, 2, N_EXP)
                self.picks = m.take(TT, N_EXP)
                self.ranked = m.take(TT, 2, N_EXP)
                self.rank = m.take(TT, 2)
                self.route_rhs = m.take(TT, 2, N_EXP)
                self.place = m.take(TT, N_EXP)
                self.gexp = m.take(TT, N_GRP)
                self.gsum = m.take(TT)
                self.p_top = m.take(TT)
                self.ediff = m.take(TT)
                self.eexp = m.take(TT)
                self.gate = m.take(2, TT)
                self.cmax = m.take(1)
                self.over = m.take(T // SLOTS - 1)
                self.n_over = m.take(1)
                self.rounds = m.take(1)
                self.hot = m.take(TT * 2, P)
                self.far = m.take(N_EXP)
                self.idx = m.take(N_EXP)
                self.scatter_at = m.take(N_EXP)
                self.scatter_now = m.take(RING)
                self.back = [self.hnT.rearrange("p c t -> p (c t)")[:, 2 * D * b:2 * D * (b + 1)] for b in range(2)]
                s = f"{layer}"
                self.params_in = sem("moe_params_in" + s)
                self.squares = sem("squares" + s)
                self.rstd_step = sem("rstd_step" + s)
                self.hn_ready = sem("hn_ready" + s)
                self.place_ready = sem("place_ready" + s)
                self.takes_ready = sem("takes_ready" + s)
                self.hnT_in_psum = sem("hnT_in_psum" + s)
                self.hnT_ready = sem("hnT_ready" + s)
                self.logits_in_psum = sem("logits_in_psum" + s)
                self.route = sem("route" + s)
                self.exp_ready = sem("exp_ready" + s)
                self.rank_in_psum = sem("rank_in_psum" + s)
                self.rounds_ready = sem("rounds_ready" + s)
                self.hot_ready = sem("hot_ready" + s)
                self.slots_in_psum = sem("slots_in_psum" + s)
                self.slot_step = sem("slot_step" + s)
                self.tables_ready = sem("tables_ready" + s)
                self.round_done = sem("round_done" + s)
                self.w_in = [sem(f"w_in{j}_" + s) for j in range(RING)]
                self.index_ready = sem("index_ready" + s)
                self.xT_in_psum = sem("xT_in_psum" + s)
                self.xT_ready = sem("xT_ready" + s)
                self.gate_up_done = sem("gate_up_done" + s)
                self.silu_ready = sem("silu_ready" + s)
                self.z_ready = sem("z_ready" + s)
                self.zT_in_psum = sem("zT_in_psum" + s)
                self.zT_ready = sem("zT_ready" + s)
                self.down_done = sem("down_done" + s)
                self.y_ready = sem("y_ready" + s)
                self.y_stored = sem("y_stored" + s)
                self.y_free = sem("y_free" + s)
                self.back_in = [sem(f"back_in{b}_" + s) for b in range(2)]
                self.h_step = sem("h_step" + s)

        moe = [Moe(i) for i in range(DEPTH)]
        ROUTED = 18
        consts_ready = sem("consts_ready")
        const_step = sem("const_step")
        h_in = sem("h_in")
        out_stored = sem("out_stored")
        pool_tick = sem("pool_tick")


        def pool_constants():
            st = Steps(const_step)

            def wait():
                nc.gpsimd.wait_ge(const_step, st.n)

            st.done(nc.gpsimd.memset(ones[:], 1.0))
            st.done(nc.gpsimd.memset(half_shift[0:SLOTS, :], -2.0))
            wait()
            st.done(nc.gpsimd.memset(half_shift[SLOTS:P, :], -1.0))
            wait()
            st.done(nc.gpsimd.affine_select(out=ident[:], in_=ones[:], compare_op=ALU.is_equal, fill=0.0, base=0,
                                            pattern=[[-1, P]], channel_multiplier=1))
            st.done(nc.gpsimd.affine_select(out=earlier[:], in_=ones[:], compare_op=ALU.is_gt, fill=0.0, base=0,
                                            pattern=[[1, P]], channel_multiplier=-1))
            st.done(nc.gpsimd.iota(slot_of_col[:], pattern=[[0, 2], [1, SLOTS]], base=0, channel_multiplier=0,
                                   allow_small_or_imprecise_dtypes=True))
            st.done(nc.gpsimd.iota(expert_iota[:], pattern=[[1, N_EXP]], base=0, channel_multiplier=0,
                                   allow_small_or_imprecise_dtypes=True))
            st.done(nc.gpsimd.iota(group_iota[:], pattern=[[1, N_GRP], [0, PER_GRP]], base=0, channel_multiplier=0,
                                   allow_small_or_imprecise_dtypes=True))
            st.done(nc.gpsimd.iota(round_starts[:], pattern=[[SLOTS, T // SLOTS - 1]], base=SLOTS, channel_multiplier=0,
                                   allow_small_or_imprecise_dtypes=True))
            nc.gpsimd.iota(token_code[:].rearrange("p t k -> p (t k)"), pattern=[[2 * P, TT], [1, 2]], base=1,
                           channel_multiplier=2, allow_small_or_imprecise_dtypes=True).then_inc(consts_ready, 1)

        FREE2 = 2
        FREE1 = 1

        def sp_moe_params(m, sp):
            i = m.layer
            with nc.allow_non_contiguous_dma("small router tables"):
                sp.dma_start(m.g_row, a["norm2_g"][i:i + 1, :].broadcast_to([P, D])).then_inc(m.params_in, 16)
                sp.dma_start(m.w_route[:, :, 0:N_GRP],
                             a["moe_w_group"][i].rearrange("(p c) g -> p c g", p=P)).then_inc(m.params_in, 16)
                sp.dma_start(m.w_route[:, :, N_GRP:],
                             a["moe_w_expert"][i].rearrange("(p c) g -> p c g", p=P)).then_inc(m.params_in, 16)
                sp.dma_start(m.b_route[:, 0:N_GRP],
                             a["moe_b_group"][i:i + 1, :].broadcast_to([P, N_GRP])).then_inc(m.params_in, 16)
                sp.dma_start(m.b_route[:, N_GRP:],
                             a["moe_b_expert"][i:i + 1, :].broadcast_to([P, N_EXP])).then_inc(m.params_in, 16)

        def sp_load_expert(m, sp, j, e):
            n = m.layer * N_EXP + e
            for src, dst in ((wg_rows, ring[j]["up"][:, 0]), (wu_rows, ring[j]["up"][:, 1]), (wd_rows, ring[j]["down"])):
                s = src[n:n + 1] if isinstance(n, int) else src[bass.ds(n, 1)]
                sp.dma_start(dst, s.rearrange("o p k f -> (o p) k f")).then_inc(m.w_in[j], 16)

        def sp_moe_weights(m, sp, first_free):
            for j in range(RING):
                first_free(j)
                sp_load_expert(m, sp, j, j)
            with sp.Fori(1, NG) as g:
                for j in range(RING):
                    sp.wait_ge(m.down_done, FREE2 + 4 * g + (j - 3))
                    sp_load_expert(m, sp, j, g * RING + j)
            sp.wait_ge(m.rounds_ready, 1)
            rounds = sp.value_load(m.rounds[0:1, 0:1].bitcast(i32), min_val=1, max_val=T // SLOTS)
            with sp.If(rounds > 1):
                with sp.Fori(1, rounds) as r:
                    with sp.Fori(0, NG) as g:
                        for j in range(RING):
                            sp.wait_ge(m.down_done, FREE2 + N_EXP * r + 4 * g + (j - 3))
                            sp_load_expert(m, sp, j, g * RING + j)
            return rounds

        def act_norm(m, act):
            for t in range(TT):
                nc.scalar.activation(m.dump, h[:, t, :], ACT.Square,
                                     accum_out=m.ss[:, t:t + 1]).then_inc(m.squares, 1)
                act.wait_ge(m.squares, t + 1)
            act.wait_ge(m.rstd_step, 1)
            nc.scalar.activation(m.rstd, m.rstd, ACT.Ln).then_inc(m.rstd_step, 1)
            act.wait_ge(m.rstd_step, 2)
            nc.scalar.activation(m.rstd, m.rstd, ACT.Exp, scale=-0.5).then_inc(m.rstd_step, 1)
            for t in range(TT):
                act.wait_ge(m.hnT_in_psum, t + 1)
                for half in range(2):
                    nc.scalar.copy(m.hnT[:, 4 * half:4 * half + 4, t * P:(t + 1) * P],
                                   bank[half].rearrange("p (c t) -> p c t", t=P)).then_inc(m.hnT_ready, 1)

        def dve_norm(m, dve):
            dve.wait_ge(m.squares, TT)
            nc.vector.tensor_scalar(m.rstd, m.ss, 1.0 / D, RMS_EPS, ALU.mult, ALU.add).then_inc(m.rstd_step, 1)
            dve.wait_ge(m.rstd_step, 3)
            dve.wait_ge(m.params_in, 16 * m.n_params)
            for t in range(TT):
                if t >= len(m.hn):
                    dve.wait_ge(m.hnT_in_psum, t - 1)
                nc.vector.scalar_tensor_tensor(out=m.hn[t % len(m.hn)], in0=h[:, t, :], scalar=m.rstd[:, t:t + 1], in1=m.g_row,
                                               op0=ALU.mult, op1=ALU.mult).then_inc(m.hn_ready, 1)

        def pe_norm(m, pe):
            pe.wait_ge(consts_ready, 1)
            for t in range(TT):
                pe.wait_ge(m.hn_ready, t + 1)
                if t:
                    pe.wait_ge(m.hnT_ready, 2 * t)
                rows = m.hn[t % len(m.hn)].rearrange("p (f c) -> p c f", c=C)
                for c in range(C):
                    last = nc.tensor.transpose(bank[c // 4][:, (c % 4) * P:(c % 4 + 1) * P], rows[:, c, :], ident[:])
                last.then_inc(m.hnT_in_psum, 1)

        def pe_logits(m, pe):
            pe.wait_ge(m.params_in, 16 * m.n_params)
            n = N_GRP + N_EXP
            for t in range(TT):
                pe.wait_ge(m.hnT_ready, 2 * t + 2)
                for c in range(C):
                    last = nc.tensor.matmul(bank[2][:, t * n:(t + 1) * n], m.hnT[:, c, t * P:(t + 1) * P],
                                            m.w_route[:, c, :], start=(c == 0), stop=(c == C - 1))
            last.then_inc(m.logits_in_psum, 1)

        def dve_route(m, dve):
            st = Steps(m.route)

            def step(ins):
                dve.wait_ge(m.route, st.done(ins))

            n = N_GRP + N_EXP
            dve.wait_ge(consts_ready, 1)
            step(nc.vector.memset(m.gl, -3.0e38))
            dve.wait_ge(m.logits_in_psum, 1)
            step(nc.vector.tensor_tensor(m.logits, bank[2][:, 0:TT * n].rearrange("p (t n) -> p t n", n=n),
                                         m.b_route.unsqueeze(1).broadcast_to([P, TT, n]), ALU.add))
            step(nc.vector.tensor_copy(m.gl[:, :, 0:N_GRP], m.logits[:, :, 0:N_GRP]))
            for t in range(TT):
                last = nc.vector.max(m.gmax[:, t, :], m.gl[:, t, :])
            step(last)
            for t in range(TT):
                last = nc.vector.max_index(m.gidx[:, t, :].bitcast(u32), m.gmax[:, t, :], m.gl[:, t, :])
            step(last)
            step(nc.vector.tensor_copy(m.gidx_f, m.gidx[:, :, 0].bitcast(u32)))
            step(nc.vector.tensor_tensor(m.in_group, group_iota[:].unsqueeze(1).broadcast_to([P, TT, N_EXP]),
                                         m.gidx_f.unsqueeze(2).broadcast_to([P, TT, N_EXP]), ALU.is_equal))
            step(nc.vector.tensor_scalar(m.in_group, m.in_group, -1.0, 3.0e38, ALU.add, ALU.mult))
            step(nc.vector.tensor_tensor(m.el, m.in_group, m.logits[:, :, N_GRP:], ALU.add))
            for t in range(TT):
                last = nc.vector.max(m.emax[:, t, :], m.el[:, t, :])
            step(last)
            for t in range(TT):
                last = nc.vector.max_index(m.eidx[:, t, :].bitcast(u32), m.emax[:, t, :], m.el[:, t, :])
            step(last)
            step(nc.vector.tensor_copy(m.eidx_f, m.eidx[:, :, 0:2].bitcast(u32)))
            for k in range(2):
                last = nc.vector.tensor_tensor(m.pick[:, :, k, :], expert_iota[:].unsqueeze(1).broadcast_to([P, TT, N_EXP]),
                                               m.eidx_f[:, :, k:k + 1].broadcast_to([P, TT, N_EXP]), ALU.is_equal)
            step(last)
            step(nc.vector.tensor_tensor(m.picks, m.pick[:, :, 0, :], m.pick[:, :, 1, :], ALU.add))
            step(nc.vector.tensor_tensor(m.gexp, m.logits[:, :, 0:N_GRP], m.gmax[:, :, 0:1].broadcast_to([P, TT, N_GRP]),
                                         ALU.subtract))
            step(nc.vector.tensor_tensor(m.ediff, m.emax[:, :, 1], m.emax[:, :, 0], ALU.subtract))
            step(nc.vector.tensor_tensor(m.route_rhs, m.pick, token_code[:].unsqueeze(3).broadcast_to([P, TT, 2, N_EXP]),
                                         ALU.mult))
            dve.wait_ge(m.exp_ready, 2)
            step(nc.vector.tensor_reduce(m.gsum, m.gexp, AX.X, ALU.add))
            assert st.n == ROUTED
            step(nc.vector.reciprocal(m.p_top, m.gsum))
            step(nc.vector.tensor_scalar(m.ediff, m.eexp, 1.0, None, ALU.add))
            step(nc.vector.reciprocal(m.ediff, m.ediff))
            step(nc.vector.tensor_tensor(m.gate[:, 0, :], m.ediff, m.p_top, ALU.mult))
            step(nc.vector.tensor_tensor(m.gate[:, 1, :], m.gate[:, 0, :], m.eexp, ALU.mult))
            dve.wait_ge(m.rank_in_psum, 1)
            ranks = bank[3][:, 0:TT * N_EXP].rearrange("p (t e) -> p t e", e=N_EXP)
            step(nc.vector.scalar_tensor_tensor(out=m.place, in0=ranks, scalar=1.0, in1=m.picks, op0=ALU.add, op1=ALU.mult))
            nc.vector.tensor_scalar(m.place, m.place, -1.0, None, ALU.add).then_inc(m.place_ready, 1)
            for k in range(2):
                last = nc.vector.tensor_tensor(m.ranked[:, :, k, :], ranks, m.pick[:, :, k, :], ALU.mult)
            step(last)
            step(nc.vector.tensor_reduce(m.rank, m.ranked, AX.X, ALU.add))
            step(nc.vector.tensor_reduce(m.cmax, bank[3][:, TT * N_EXP:(TT + 1) * N_EXP], AX.X, ALU.max))
            step(nc.vector.tensor_scalar(m.over, round_starts[:], m.cmax, None, ALU.is_lt))
            step(nc.vector.tensor_reduce(m.n_over, m.over, AX.X, ALU.add))
            nc.vector.tensor_scalar(m.rounds.bitcast(i32), m.n_over, 1.0, None, ALU.add).then_inc(m.rounds_ready, 1)

        def act_route(m, act):
            act.wait_ge(m.route, 16)
            nc.scalar.activation(m.gexp, m.gexp, ACT.Exp).then_inc(m.exp_ready, 1)
            nc.scalar.activation(m.eexp, m.ediff, ACT.Exp).then_inc(m.exp_ready, 1)

        def pe_ranks(m, pe):
            pe.wait_ge(m.route, 14)
            for t in range(TT + 1):
                o = bank[3][:, t * N_EXP:(t + 1) * N_EXP]
                for u in range(min(t + 1, TT)):
                    last = nc.tensor.matmul(o, earlier[:] if u == t else ones[:], m.picks[:, u, :],
                                            start=(u == 0), stop=(u == min(t, TT - 1)))
            last.then_inc(m.rank_in_psum, 1)

        def load_rounds(m, eng):
            eng.wait_ge(m.rounds_ready, 1)
            return eng.value_load(m.rounds[0:1, 0:1].bitcast(i32), min_val=1, max_val=T // SLOTS)

        def dve_takes(m, dve, r, p, b):
            dve.wait_ge(m.place_ready, r + 1)
            place = m.place[:, :, bass.ds(2 * p, 2)]
            nc.vector.tensor_tensor(m.takes[b].rearrange("p t (e s) -> p t e s", s=SLOTS),
                                    slot_of_col[:].rearrange("p (e s) -> p e s", s=SLOTS).unsqueeze(1)
                                    .broadcast_to([P, TT, 2, SLOTS]),
                                    place.unsqueeze(3).broadcast_to([P, TT, 2, SLOTS]),
                                    ALU.is_equal).then_inc(m.takes_ready, 1)

        def dve_slots(m, dve, r):
            for i in range(TT * 2):
                nc.vector.tensor_scalar(m.hot[:, i, :], slot_of_col[:], m.rank[:, i // 2, i % 2:i % 2 + 1], None,
                                        ALU.is_equal).then_inc(m.hot_ready, 1)

        def dve_tables(m, dve, r):
            S = 4
            dve.wait_ge(m.hot_ready, TT * 2 * (r + 1))
            nc.vector.tensor_scalar(m.rank, m.rank, -float(SLOTS), None, ALU.add).then_inc(m.slot_step, 1)
            dve.wait_ge(m.slot_step, S * r + 1)
            dve.wait_ge(m.slots_in_psum, r + 1)
            dve.wait_ge(m.round_done, r + 1)
            v = bank[2][:, 0:N_EXP]
            nc.vector.tensor_scalar(m.far, v, 0.0, FAR, ALU.is_equal, ALU.mult).then_inc(m.slot_step, 1)
            nc.vector.tensor_scalar(m.idx, v, 2.0, half_shift[:, 0:1], ALU.mult, ALU.add).then_inc(m.slot_step, 1)
            dve.wait_ge(m.slot_step, S * r + 3)
            nc.vector.tensor_tensor(m.scatter_at.bitcast(i32), m.idx, m.far, ALU.add).then_inc(m.slot_step, 1)
            dve.wait_ge(m.slot_step, S * r + S)
            dve.sem_inc(m.tables_ready, 1)

        def pe_slots(m, pe, r):
            for i in range(TT * 2):
                pe.wait_ge(m.hot_ready, TT * 2 * r + i + 1)
                last = nc.tensor.matmul(bank[2][:, 0:N_EXP], m.hot[:, i, :], m.route_rhs[:, i // 2, i % 2, :],
                                        start=(i == 0), stop=(i == TT * 2 - 1))
            last.then_inc(m.slots_in_psum, 1)

        def pool_moe(m, pool):
            pool.sem_inc(m.z_ready, FREE2)
            pool.sem_inc(m.gate_up_done, FREE2)
            pool.sem_inc(m.down_done, FREE2)
            pool.sem_inc(m.y_ready, FREE2)
            pool.sem_inc(m.zT_ready, FREE1)
            pool.sem_inc(m.xT_ready, FREE1)
            pool.sem_inc(m.y_free, RING)
            pool.sem_inc(m.round_done, 1)
            rounds = load_rounds(m, pool)

            with pool.Fori(0, rounds) as r:
                pool.wait_ge(m.tables_ready, r + 1)
                pool.sem_inc(pool_tick)

                def scatter(n, j, e):
                    pool.wait_ge(m.y_ready, FREE2 + n + 1)
                    pool.sem_inc(pool_tick)
                    nc.gpsimd.tensor_copy(m.scatter_now[:, j:j + 1].bitcast(i32),
                                          m.scatter_at[:, bass.ds(e, 1)].bitcast(i32)).then_inc(m.index_ready, 1)
                    pool.wait_ge(m.index_ready, n + 1)
                    pool.sem_inc(pool_tick)
                    nc.gpsimd.indirect_dma_start(
                        chosen[m.layer],
                        bass.IndirectOffsetOnAxis(ap=m.scatter_now[:, j:j + 1].bitcast(u32), axis=0),
                        m.y[j], None, bounds_check=T * 4 - 1, oob_is_err=False).then_inc(m.y_stored, 16)

                def scattered(n):
                    pool.wait_ge(m.y_stored, 16 * n + 16)
                    pool.sem_inc(m.y_free)

                with pool.Fori(0, NG) as g:
                    for j in range(RING):
                        scatter(N_EXP * r + 4 * g + j, j, 4 * g + j)
                        scattered(N_EXP * r + 4 * g + j)
                pool.sem_inc(m.round_done, 1)
            return rounds

        def pe_moe(m, pe):
            rounds = load_rounds(m, pe)
            with pe.Fori(0, rounds) as r:

                def gather(p, b):
                    pair = NG * 2 * r + p
                    pe.wait_ge(m.takes_ready, pair + 1)
                    pe.wait_ge(m.xT_ready, FREE1 + pair)
                    for c in range(C):
                        for t in range(TT):
                            last = nc.tensor.matmul(bank[c // 4][:, (c % 4) * P:(c % 4 + 1) * P],
                                                    m.hn[t].rearrange("p (f c) -> p c f", c=C)[:, c, :],
                                                    m.takes[b][:, t, :], start=(t == 0), stop=(t == TT - 1))
                    last.then_inc(m.xT_in_psum, 1)

                def gate_up(g, j):
                    n = N_EXP * r + 4 * g + j
                    if j % 2 == 0:
                        pe.wait_ge(m.xT_ready, FREE1 + 1 + NG * 2 * r + 2 * g + j // 2)
                    pe.wait_ge(m.w_in[j], 48 * NG * r + 48 * g + 48)
                    pe.wait_ge(m.z_ready, n + 1)
                    o = bank[4 + j % 2]
                    for c in range(C):
                        for half in range(2):
                            last = nc.tensor.matmul(
                                o[half * SLOTS:(half + 1) * SLOTS, 0:F_EXP].rearrange("p (u f) -> p u f", u=2),
                                m.xT[j // 2][:, c, (j % 2) * SLOTS:(j % 2 + 1) * SLOTS],
                                ring[j]["up"][:, :, c, half * P:(half + 1) * P], start=(c == 0), stop=(c == C - 1))
                    last.then_inc(m.gate_up_done, 1)

                def down(g, j):
                    n = N_EXP * r + 4 * g + j
                    pe.wait_ge(m.z_ready, FREE2 + 1 + n)
                    pe.wait_ge(m.zT_ready, FREE1 + n)
                    nc.tensor.transpose(bank[3][:, 0:P], m.z[j % 2], ident[:]).then_inc(m.zT_in_psum, 1)
                    pe.wait_ge(m.zT_ready, FREE1 + 1 + n)
                    pe.wait_ge(m.y_ready, n + 1)
                    for k in range(2):
                        for half in range(2):
                            last = nc.tensor.matmul(bank[6 + j % 2][half * SLOTS:(half + 1) * SLOTS, :],
                                                    m.zT[j % 2][:, k, :],
                                                    ring[j]["down"][:, k, half * 512:(half + 1) * 512],
                                                    start=(k == 0), stop=(k == 1))
                    last.then_inc(m.down_done, 1)

                gather(0, 0)
                pe_slots(m, pe, r)
                gate_up(0, 0)
                with pe.Fori(0, NG - 1) as g:
                    for j in range(RING):
                        if j % 2 == 0:
                            gather(2 * g + (j // 2 + 1), 1 - j // 2)
                        gate_up(g + (j + 1) // RING, (j + 1) % RING)
                        down(g, j)
                gather(2 * NG - 1, 1)
                for j in range(RING):
                    if j + 1 < RING:
                        gate_up(NG - 1, j + 1)
                    down(NG - 1, j)

        def act_moe(m, act):
            rounds = load_rounds(m, act)
            with act.Fori(0, rounds) as r:
                with act.Fori(0, NG) as g:
                    for j in range(RING):
                        n = N_EXP * r + 4 * g + j
                        act.wait_ge(m.gate_up_done, FREE2 + 1 + n)
                        act.wait_ge(m.z_ready, n + 1)
                        nc.scalar.activation(m.silu[j % 2], bank[4 + j % 2][:, 0:P], ACT.Silu).then_inc(m.silu_ready, 1)
                        act.wait_ge(m.zT_in_psum, n + 1)
                        act.wait_ge(m.down_done, n + 1)
                        nc.scalar.copy(m.zT[j % 2].rearrange("p k s -> p (k s)"), bank[3][:, 0:P]).then_inc(m.zT_ready, 1)
                        act.wait_ge(m.down_done, FREE2 + 1 + n)
                        act.wait_ge(m.y_free, n + 1)
                        nc.scalar.copy(m.y[j], bank[6 + j % 2][:]).then_inc(m.y_ready, 1)
            return rounds

        def dve_moe(m, dve):
            rounds = load_rounds(m, dve)
            with dve.Fori(0, rounds) as r:

                def take_rows(p, b):
                    dve.wait_ge(m.xT_in_psum, NG * 2 * r + p + 1)
                    flat = m.xT[b].rearrange("p c s -> p (c s)")
                    nc.vector.tensor_copy(flat[:, 0:512], bank[0][:])
                    nc.vector.tensor_copy(flat[:, 512:1024], bank[1][:]).then_inc(m.xT_ready, 1)

                def gated(g, j):
                    n = N_EXP * r + 4 * g + j
                    dve.wait_ge(m.silu_ready, n + 1)
                    nc.vector.tensor_tensor(m.z[j % 2], m.silu[j % 2], bank[4 + j % 2][:, P:2 * P],
                                            ALU.mult).then_inc(m.z_ready, 1)

                dve_takes(m, dve, r, 0, 0)
                dve_takes(m, dve, r, 1, 1)
                dve_slots(m, dve, r)
                dve.wait_ge(m.down_done, FREE2 + N_EXP * r)
                take_rows(0, 0)
                dve_tables(m, dve, r)
                with dve.Fori(0, NG - 1) as g:
                    for j in range(RING):
                        gated(g, j)
                        if j % 2 == 0:
                            take_rows(2 * g + (j // 2 + 1), 1 - j // 2)
                            dve_takes(m, dve, r, 2 * g + (j // 2 + 2), j // 2)
                for j in range(RING):
                    gated(NG - 1, j)
                    if j == 0:
                        take_rows(2 * NG - 1, 1)
                dve.wait_ge(m.takes_ready, NG * 2 * (r + 1))
                nc.vector.tensor_scalar(m.place, m.place, -float(SLOTS), None, ALU.add).then_inc(m.place_ready, 1)
            return rounds

        def act_load_back(m, act, rounds):
            back = chosen[m.layer].rearrange("(t p c) n -> t p (c n)", p=P, c=4)
            act.wait_ge(m.round_done, rounds + 1)
            for t in range(TT):
                if t >= 2:
                    act.wait_ge(m.h_step, 2 * (t - 1))
                act.dma_start(m.back[t % 2], back[t]).then_inc(m.back_in[t % 2], 16)

        def dve_combine(m, dve):
            for t in range(TT):
                dve.wait_ge(m.back_in[t % 2], 16 * (t // 2 + 1))
                for k in range(2):
                    if k:
                        dve.wait_ge(m.h_step, 2 * t + 1)
                    nc.vector.scalar_tensor_tensor(out=h[:, t, :], in0=m.back[t % 2][:, k * D:(k + 1) * D],
                                                   scalar=m.gate[:, k, t:t + 1], in1=h[:, t, :], op0=ALU.mult,
                                                   op1=ALU.add).then_inc(m.h_step, 1)

        CH = 64
        HD = 64
        NCH = T // CH
        CP = NCH // 2
        PAIRS = D // P
        DECAY = float(np.exp(-0.5))
        N_VEC = 8
        W0, A0, KK, KA, RK, LNG, LNB, KA1 = range(N_VEC)


        class Rwkv:
            def __init__(self):
                m = Arena(big)
                self.layer = 0
                self.hnT = m.take(C, T)
                self.xr, self.xk, self.xv = (m.take(C, T) for _ in range(3))
                self.yg = m.take(PAIRS, T)
                self.w = m.take(3, C, P)
                self.w_lora = m.take(2, P)
                self.w_g2 = m.take(P)
                self.hid = m.take(3, T)
                self.vec = m.take(N_VEC, PAIRS)
                self.pv = m.take(N_VEC)
                self.pt = m.take(2)
                self.wend = m.take(NCH)
                hn_at = m.at
                self.hn = [m.take(D) for _ in range(2)]
                self.lora1 = m.take(C, 2 * 64 + P)
                self.mu = m.take(6, C)
                self.ss, self.rstd = m.take(TT), m.take(TT)
                self.keep = m.take(T)
                self.upper = m.take(CH)
                self.upper_incl = m.take(CH)
                self.u_in = m.take(CH)
                self.l_in, self.l_out = m.take(CH), m.take(CH)
                self.eye = m.take(CH)
                self.block16 = m.take(CH)
                self.tmp_mask = m.take(CH)
                self.heads = m.take(P)
                self.head_mean = m.take(P)
                tiles = m.at
                t = Arena(big, tiles)
                self.dump = big[:, tiles:tiles + D]
                self.g_row = big[:, tiles + D:tiles + 2 * D]
                self.xx = big[:, tiles + 2 * D:tiles + 2 * D + C * T].rearrange("p (c t) -> p c t", t=T)
                self.xw = self.yg
                self.xa = big[:, tiles + 6 * D:tiles + 6 * D + C * T].rearrange("p (c t) -> p c t", t=T)
                self.xg_ = self.xv
                f = Arena(big, tiles)
                lo = Arena(big, 0)
                (self.sig, self.a, self.cum, self.cprev, self.wc, self.winv, self.kraw, self.rraw, self.kk2, self.at,
                 self.kka, self.km, self.kt, self.rt, self.v) = (f.take(T) for _ in range(15))
                self.wprev, self.rs, self.kkn = self.cprev, self.kk2, self.kk2
                self.bt, self.k2, self.rk = self.kka, self.km, self.sig
                self.g, self.bv = f.take(T), f.take(T)
                (self.ud, self.ld, self.lo_, self.mrb, self.lak, self.mrk, self.lv,
                 self.gi) = (lo.take(2, CP, CH) for _ in range(8))
                dead = Arena(big, hn_at)
                (self.att, self.btt, self.ktt, self.vt) = (dead.take(CP, P) for _ in range(4))
                self.dr, self.x1 = (dead.take(2, CP, 2 * CH) for _ in range(2))
                self.wz = self.dr
                (self.v1, self.u2, self.l2, self.u4, self.v2, self.l4) = (f.take(2, CP, CH) for _ in range(6))
                self.v4, self.l8, self.dt, self.mm, self.mt, self.m2 = (self.v1, self.u2, self.u4, self.l2, self.v2,
                                                                        self.l4)
                self.rh = self.x1.rearrange("p h c t -> p (h c t)")[:, 0:T].rearrange(
                    "p (b c t) -> p b c t", b=2, t=CH)
                self.st = f.take(NCH, HD)
                self.y = self.ktt.rearrange("p c t -> p (c t)")
                self.yc = self.ud.rearrange("p b c t -> p (b c t)")
                self.ysq = self.gi.rearrange("p b c t -> p (b c t)")
                self.yr = self.x1.rearrange("p h c t -> p (h c t)")[:, T:2 * T]
                self.wo = big[:, C * T:C * T + PAIRS * D].rearrange("p (q d) -> p q d", d=D)
                self.n_params = 1
                (self.params_in, self.squares, self.rstd_step, self.hn_ready, self.hnT_in_psum, self.hnT_ready,
                 self.mask_step, self.masks_ready, self.vec_in, self.vec_ready, self.mu_in, self.lora_in,
                 self.w_in, self.g2_in, self.var_read, self.projected, self.s_ps, self.s_ready, self.pair_done,
                 self.wo_in, self.mix_ps, self.mixed) = (sem("rwkv_" + n) for n in (
                    "params_in squares rstd_step hn_ready hnT_in_psum hnT_ready mask_step masks_ready vec_in "
                    "vec_ready mu_in lora_in w_in g2_in var_read projected s_ps s_ready pair_done wo_in mix_ps "
                    "mixed").split())
                (self.xx_ready, self.xw_ready, self.xa_ready, self.xg_ready, self.xk_ready, self.xr_ready,
                 self.xv_ready) = signals(sem("rwkv_lerps"), 7)
                (self.hw_in_psum, self.ha_in_psum, self.hg_in_psum) = signals(sem("rwkv_hidden_in_psum"), 3)
                (self.hw_ready, self.ha_ready, self.hg_ready) = signals(sem("rwkv_hidden"), 3)
                (self.w_ps, self.a_ps, self.k_ps, self.r_ps, self.n2_ps, self.v_ps) = signals(sem("rwkv_prepared_tensor"), 6)
                (self.sig_ready, self.a_ready, self.kraw_ready, self.kk2_ready, self.rraw_ready, self.wc_ready,
                 self.winv_ready, self.wprev_ready, self.ln_ready, self.rs_ready, self.v_ready) = signals(sem("rwkv_prepared_scalar"), 11)
                (self.pv_ready, self.cum_ready, self.cprev_ready, self.km_ready, self.k2_ready, self.n2_ready,
                 self.kt_ready, self.kkn_ready, self.at_ready, self.kka_ready, self.bt_ready, self.rt_ready,
                 self.rk_ready) = signals(sem("rwkv_prepared_vector"), 13)
                (self.vt_ps, self.att_ps, self.btt_ps, self.ktt_ps, self.bonus_ps, self.ub_ps, self.lk_ps,
                 self.l_ps, self.u2_ps, self.l2_ps, self.u4_ps, self.v2_ps, self.l4_ps, self.lv_ps, self.v4_ps,
                 self.l8_ps, self.dt_ps, self.mm_ps, self.mt_ps, self.dr_ps, self.m2_ps, self.x1_ps, self.wz_ps,
                 self.rg_ps, self.z_ps, self.g_ps, self.y_ps, self.mean_ps, self.var_ps) = signals(sem("rwkv_tensor_results"), 29)
                (self.vt_ready, self.att_ready, self.btt_ready, self.ktt_ready, self.l2_ready, self.u4_ready,
                 self.l4_ready, self.lv_ready, self.l8_ready, self.mm_ready, self.dr_ready, self.m2_ready,
                 self.g_ready, self.y_ready, self.ysq_ready, self.yln_ready, self.yrstd) = signals(sem("rwkv_scalar_results"), 17)
                (self.pt_ready, self.bv_ready, self.ud_ready, self.masked_ub, self.masked_lk, self.masked_l,
                 self.v1_ready, self.u2_ready, self.v2_ready, self.v4_ready, self.dt_ready, self.mt_ready,
                 self.x1_ready, self.wz_ready, self.gi_ready, self.rh_ready, self.yc_ready, self.yn1_ready,
                 self.yn2_ready, self.yn3_ready) = signals(sem("rwkv_vector_results"), 20)

        rw = Rwkv()
        pe_tick = sem("pe_tick")

        def pe_wait(pe, s, value):
            pe.wait_ge(s, value)
            pe.sem_inc(pe_tick)

        def pool_rwkv_masks(m, pool):
            st = Steps(m.mask_step)

            def step(ins):
                pool.wait_ge(m.mask_step, st.done(ins))

            sel = nc.gpsimd.affine_select
            step(nc.gpsimd.memset(m.keep, 1.0))
            step(nc.gpsimd.memset(m.keep.rearrange("p (c t) -> p c t", t=CH)[:, :, 0:1], 0.0))
            step(nc.gpsimd.memset(m.heads, 0.0))
            step(nc.gpsimd.memset(m.head_mean, 0.0))
            for half in range(2):
                p = slice(half * CH, half * CH + CH)
                step(nc.gpsimd.memset(m.heads[p, half * HD:half * HD + HD], 1.0))
                step(nc.gpsimd.memset(m.head_mean[p, half * HD:half * HD + HD], 1.0 / HD))
                one = ones[p, 0:CH]
                step(sel(out=m.upper[p, :], in_=one, compare_op=ALU.is_gt, fill=0.0, base=0, pattern=[[1, CH]],
                         channel_multiplier=-1))
                step(sel(out=m.upper_incl[p, :], in_=one, compare_op=ALU.is_ge, fill=0.0, base=0, pattern=[[1, CH]],
                         channel_multiplier=-1))
                step(sel(out=m.eye[p, :], in_=one, compare_op=ALU.is_equal, fill=0.0, base=0, pattern=[[-1, CH]],
                         channel_multiplier=1))
                step(sel(out=m.tmp_mask[p, :], in_=one, compare_op=ALU.is_ge, fill=0.0, base=0,
                         pattern=[[-16, CH // 16], [0, 16]], channel_multiplier=1))
                step(sel(out=m.block16[p, :], in_=m.tmp_mask[p, :], compare_op=ALU.is_ge, fill=0.0, base=15,
                         pattern=[[16, CH // 16], [0, 16]], channel_multiplier=-1))
                step(sel(out=m.u_in[p, :], in_=m.block16[p, :], compare_op=ALU.is_gt, fill=0.0, base=0,
                         pattern=[[1, CH]], channel_multiplier=-1))
                step(sel(out=m.l_in[p, :], in_=m.block16[p, :], compare_op=ALU.is_gt, fill=0.0, base=0,
                         pattern=[[-1, CH]], channel_multiplier=1))
                step(sel(out=m.l_out[p, :], in_=one, compare_op=ALU.is_gt, fill=0.0, base=0, pattern=[[-1, CH]],
                         channel_multiplier=1))
            nc.gpsimd.tensor_tensor(m.l_out, m.l_out, m.l_in, ALU.subtract).then_inc(m.masks_ready, 1)
            pool.sem_inc(m.var_read, 1)

        def sp_rwkv(m, sp):
            i = 0
            sp.dma_start(h[:], a["x"].rearrange("b (t p) d -> (b p) t d", p=P)).then_inc(h_in, 16)
            sp.dma_start(m.g_row, a["norm1_g"][0:1, :].broadcast_to([P, D])).then_inc(m.params_in, 16)
            with nc.allow_non_contiguous_dma("per-channel vectors"):
                sp.dma_start(m.mu, a["rwkv_mu"][i].rearrange("n (p c) -> p n c", p=P)).then_inc(m.mu_in, 16)
                for n, src in ((W0, a["rwkv_w0"][i]), (A0, a["rwkv_a0"][i]), (KK, a["rwkv_k_k"][i]),
                               (KA, a["rwkv_k_a"][i]), (RK, a["rwkv_r_k"][i].rearrange("h n -> (h n)")),
                               (LNG, a["rwkv_ln_g"][i]), (LNB, a["rwkv_ln_b"][i])):
                    sp.dma_start(m.vec[:, n, :], src.rearrange("(q p) -> p q", p=P)).then_inc(m.vec_in, 16)
            col = 0
            for src, n in (("rwkv_w1", 64), ("rwkv_a1", 64), ("rwkv_g1", P)):
                sp.dma_start(m.lora1[:, :, col:col + n],
                             a[src][i].rearrange("(p c) n -> p c n", p=P)).then_inc(m.lora_in, 16)
                col += n
            w_rkv = a["rwkv_w_rkv"][i].rearrange("n (p c) d -> p n c d", p=P)

            def load_pair(q):
                for n in range(3):
                    sp.dma_start(m.w[:, n], w_rkv[:, n, :, bass.ds(q * P, P)]).then_inc(m.w_in, 16)
                for n, src in enumerate(("rwkv_w2", "rwkv_a2")):
                    sp.dma_start(m.w_lora[0:64, n], a[src][i][:, bass.ds(q * P, P)]).then_inc(m.w_in, 16)

            def load_g2(q):
                sp.dma_start(m.w_g2, a["rwkv_g2"][i][:, bass.ds(q * P, P)]).then_inc(m.g2_in, 16)

            load_pair(0)
            load_g2(0)
            sp.wait_ge(m.projected, 1)
            load_pair(1)
            with sp.Fori(1, PAIRS - 1) as q:
                sp.wait_ge(m.g_ps.sem, m.g_ps.by(q - 1))
                load_g2(q)
                sp.wait_ge(m.projected, q + 1)
                load_pair(q + 1)
            sp.wait_ge(m.g_ps.sem, m.g_ps.by(PAIRS - 2))
            load_g2(PAIRS - 1)
            sp.wait_ge(m.projected, PAIRS)
            sp.dma_start(m.wo, a["rwkv_w_o"][i].rearrange("(q p) d -> p q d", p=P)).then_inc(m.wo_in, 16)

        def dve_rwkv_lerps(m, dve):
            dve.wait_ge(m.hnT_ready, 2 * TT)
            nc.vector.tensor_scalar(m.xx[:, :, 0:1], m.hnT[:, :, 0:1], -1.0, None, ALU.mult)
            nc.vector.tensor_tensor(m.xx[:, :, 1:T], m.hnT[:, :, 0:T - 1], m.hnT[:, :, 1:T],
                                    ALU.subtract).then_inc(m.xx_ready.now(), 1)
            dve.wait_ge(m.xx_ready.sem, m.xx_ready.by(0))
            dve.wait_ge(m.mu_in, 16)
            for out_, n, s in ((m.xw, 1, m.xw_ready), (m.xa, 4, m.xa_ready), (m.xg_, 5, m.xg_ready),
                               (m.xk, 2, m.xk_ready), (m.xr, 0, m.xr_ready), (m.xv, 3, m.xv_ready)):
                if n == 3:
                    dve.wait_ge(m.hg_in_psum.sem, m.hg_in_psum.by(0))
                for c in range(C):
                    last = nc.vector.scalar_tensor_tensor(out=out_[:, c, :], in0=m.xx[:, c, :],
                                                          scalar=m.mu[:, n, c:c + 1], in1=m.hnT[:, c, :],
                                                          op0=ALU.mult, op1=ALU.add)
                last.then_inc(s.now(), 1)
            dve.wait_ge(m.vec_in, 16 * 7)
            nc.vector.tensor_scalar(m.vec[:, KA1, :], m.vec[:, KA, :], -1.0, 1.0, ALU.mult, ALU.add).then_inc(m.vec_ready, 1)

        def pe_rwkv_hidden(m, pe):
            pe.wait_ge(m.lora_in, 48)
            col = 0
            for x, rows, s, done, o in ((m.xw, 64, m.xw_ready, m.hw_in_psum, bank[2]),
                                        (m.xa, 64, m.xa_ready, m.ha_in_psum, bank[3]),
                                        (m.xg_, P, m.xg_ready, m.hg_in_psum, bank[4])):
                pe.wait_ge(s.sem, s.by(0))
                for c in range(C):
                    last = nc.tensor.matmul(o[0:rows, :], m.lora1[:, c, col:col + rows], x[:, c, :], start=(c == 0),
                                            stop=(c == C - 1))
                last.then_inc(done.now(), 1)
                col += rows

        def act_rwkv_hidden(m, act):
            act.wait_ge(m.hw_in_psum.sem, m.hw_in_psum.by(0))
            nc.scalar.activation(m.hid[0:64, 0, :], bank[2][0:64, :], ACT.Tanh).then_inc(m.hw_ready.now(), 1)
            act.wait_ge(m.ha_in_psum.sem, m.ha_in_psum.by(0))
            nc.scalar.copy(m.hid[0:64, 1, :], bank[3][0:64, :]).then_inc(m.ha_ready.now(), 1)
            act.wait_ge(m.hg_in_psum.sem, m.hg_in_psum.by(0))
            nc.scalar.activation(m.hid[:, 2, :], bank[4], ACT.Sigmoid).then_inc(m.hg_ready.now(), 1)

        def units():
            for hd in range(2):
                for cp in range(CP):
                    for par in range(2):
                        yield hd, cp, par

        def half(i):
            return slice(64 * i, 64 * i + 64)

        def two_banks(i, lo_, n):
            return psum[:, i * 512:(i + 2) * 512].rearrange("p (b n) -> p b n", b=2)[:, :, lo_:lo_ + n]

        def flat(x):
            return x.rearrange("p a b c -> p (a b c)") if len(x.shape) == 4 else x.rearrange("p a b -> p (a b)")

        def pe_prepare_low_rank(m, pe, q):
            pe_wait(pe, m.w_in, 80 * q + 80)
            nc.tensor.matmul(bank[0], m.w_lora[0:64, 0], m.hid[0:64, 0, :], start=True, stop=True).then_inc(m.w_ps.now(), 1)
            nc.tensor.matmul(bank[1], m.w_lora[0:64, 1], m.hid[0:64, 1, :], start=True, stop=True).then_inc(m.a_ps.now(), 1)

        def project(m, n, x, b, c0, c1):
            for c in range(c0, c1):
                last = nc.tensor.matmul(bank[b], m.w[:, n, c, :], x[:, c, :], start=(c == 0), stop=(c == C - 1))
            return last

        def pe_prepare_k(m, pe, q, c0, c1):
            if c0 == 0:
                pe_wait(pe, m.sig_ready.sem, m.sig_ready.by(q))
            last = project(m, 1, m.xk, 0, c0, c1)
            if c1 == C:
                last.then_inc(m.k_ps.now(), 1)

        def pe_prepare_r(m, pe, q, c0, c1):
            if c0 == 0:
                pe_wait(pe, m.a_ready.sem, m.a_ready.by(q))
            last = project(m, 0, m.xr, 1, c0, c1)
            if c1 == C:
                last.then_inc(m.r_ps.now(), 1)

        def pe_prepare_norm(m, pe, q):
            pe_wait(pe, m.kk2_ready.sem, m.kk2_ready.by(q))
            nc.tensor.matmul(bank[0], m.heads, m.kk2, start=True, stop=True).then_inc(m.n2_ps.now(), 1)

        def pe_prepare_v(m, pe, q, c0, c1):
            if c0 == 0:
                pe_wait(pe, m.rraw_ready.sem, m.rraw_ready.by(q))
            last = project(m, 2, m.xv, 1, c0, c1)
            if c1 == C:
                last.then_inc(m.v_ps.now(), 1)
                pe_wait(pe, m.v_ps.sem, m.v_ps.by(q))
                pe.sem_inc(m.projected)

        def act_prepare_sigmoids(m, act, q):
            act.wait_ge(m.pv_ready.sem, m.pv_ready.by(q))
            act.wait_ge(m.w_ps.sem, m.w_ps.by(q))
            nc.scalar.activation(m.sig, bank[0], ACT.Sigmoid, bias=m.pv[:, W0:W0 + 1]).then_inc(m.sig_ready.now(), 1)
            act.wait_ge(m.a_ps.sem, m.a_ps.by(q))
            nc.scalar.activation(m.a, bank[1], ACT.Sigmoid, bias=m.pv[:, A0:A0 + 1]).then_inc(m.a_ready.now(), 1)

        def act_prepare_k(m, act, q):
            act.wait_ge(m.k_ps.sem, m.k_ps.by(q))
            nc.scalar.copy(m.kraw, bank[0]).then_inc(m.kraw_ready.now(), 1)
            nc.scalar.activation(m.kk2, bank[0], ACT.Square, scale=m.pv[:, KK:KK + 1]).then_inc(m.kk2_ready.now(), 1)

        def act_prepare_r(m, act, q):
            act.wait_ge(m.r_ps.sem, m.r_ps.by(q))
            nc.scalar.copy(m.rraw, bank[1]).then_inc(m.rraw_ready.now(), 1)

        def act_prepare_decays(m, act, q):
            act.wait_ge(m.cum_ready.sem, m.cum_ready.by(q))
            nc.scalar.activation(m.wc, m.cum, ACT.Exp, scale=-DECAY).then_inc(m.wc_ready.now(), 1)
            nc.scalar.activation(m.winv, m.cum, ACT.Exp, scale=DECAY).then_inc(m.winv_ready.now(), 1)
            act.wait_ge(m.cprev_ready.sem, m.cprev_ready.by(q))
            nc.scalar.activation(m.wprev, m.cprev, ACT.Exp, scale=-DECAY).then_inc(m.wprev_ready.now(), 1)

        def act_prepare_norm(m, act, q):
            act.wait_ge(m.n2_ready.sem, m.n2_ready.by(q))
            nc.scalar.activation(m.rs, m.rs, ACT.Ln).then_inc(m.ln_ready.now(), 1)
            act.wait_ge(m.ln_ready.sem, m.ln_ready.by(q))
            nc.scalar.activation(m.rs, m.rs, ACT.Exp, scale=-0.5).then_inc(m.rs_ready.now(), 1)

        def act_prepare_v(m, act, q):
            act.wait_ge(m.v_ps.sem, m.v_ps.by(q))
            nc.scalar.copy(m.v, bank[1]).then_inc(m.v_ready.now(), 1)

        TTn, STT, TS = nc.vector.tensor_tensor, nc.vector.scalar_tensor_tensor, nc.vector.tensor_scalar

        def dve_wait(dve, q, *results):
            for s in results:
                dve.wait_ge(s.sem, s.by(q))

        def dve_prepare_vectors(m, dve, q):
            nc.vector.tensor_copy(m.pv, m.vec[:, :, bass.ds(q, 1)].rearrange("p n o -> p (n o)")
                                  ).then_inc(m.pv_ready.now(), 1)

        def dve_prepare_decays(m, dve, q):
            dve_wait(dve, q, m.sig_ready)
            nc.vector.tensor_tensor_scan(m.cum, m.keep, m.sig, 0.0, ALU.mult, ALU.add).then_inc(m.cum_ready.now(), 1)
            dve_wait(dve, q, m.cum_ready)
            TTn(m.cprev, m.cum, m.sig, ALU.subtract).then_inc(m.cprev_ready.now(), 1)

        def dve_prepare_k(m, dve, q):
            dve_wait(dve, q, m.a_ready, m.pv_ready)
            TS(m.km, m.a, m.pv[:, KA:KA + 1], m.pv[:, KA1:KA1 + 1], ALU.mult, ALU.add).then_inc(m.km_ready.now(), 1)
            dve_wait(dve, q, m.km_ready, m.kraw_ready)
            TTn(m.k2, m.kraw, m.km, ALU.mult).then_inc(m.k2_ready.now(), 1)

        def dve_prepare_norm(m, dve, q):
            dve_wait(dve, q, m.n2_ps)
            TS(m.rs, bank[0], 1e-24, None, ALU.max).then_inc(m.n2_ready.now(), 1)

        def dve_prepare_rest(m, dve, q):
            dve_wait(dve, q, m.k2_ready, m.winv_ready)
            TTn(m.kt, m.k2, m.winv, ALU.mult).then_inc(m.kt_ready.now(), 1)
            dve_wait(dve, q, m.rs_ready)
            STT(out=m.kkn, in0=m.kraw, scalar=m.pv[:, KK:KK + 1], in1=m.rs, op0=ALU.mult,
                op1=ALU.mult).then_inc(m.kkn_ready.now(), 1)
            dve_wait(dve, q, m.kkn_ready, m.wprev_ready)
            STT(out=m.at, in0=m.kkn, scalar=-1.0, in1=m.wprev, op0=ALU.mult, op1=ALU.mult).then_inc(m.at_ready.now(), 1)
            TTn(m.kka, m.kkn, m.a, ALU.mult).then_inc(m.kka_ready.now(), 1)
            dve_wait(dve, q, m.kka_ready)
            TTn(m.bt, m.kka, m.winv, ALU.mult).then_inc(m.bt_ready.now(), 1)
            dve_wait(dve, q, m.rraw_ready, m.wc_ready)
            TTn(m.rt, m.rraw, m.wc, ALU.mult).then_inc(m.rt_ready.now(), 1)
            dve_wait(dve, q, m.cprev_ready)
            STT(out=m.rk, in0=m.rraw, scalar=m.pv[:, RK:RK + 1], in1=m.k2, op0=ALU.mult,
                op1=ALU.mult).then_inc(m.rk_ready.now(), 1)

        def pe_rwkv_pair(m, pe, q, more):
            nq = q + 1

            def wait(*results):
                for s in results:
                    pe_wait(pe, s.sem, s.by(q))

            def flip(src, b, done):
                for i in range(CP):
                    last = nc.tensor.transpose(bank[b][:, i * P:(i + 1) * P], src[:, i * P:(i + 1) * P], ident[:])
                last.then_inc(done.now(), 1)

            wait(m.v_ready, m.rk_ready)
            pe_wait(pe, m.var_read, q + 1)
            flip(m.v, 2, m.vt_ps)
            flip(m.at, 3, m.att_ps)
            flip(m.bt, 4, m.btt_ps)
            flip(m.kt, 5, m.ktt_ps)
            nc.tensor.matmul(bank[7], m.heads, m.rk, start=True, stop=True).then_inc(m.bonus_ps.now(), 1)
            if more:
                pe_prepare_low_rank(m, pe, nq)

            def product(lhs, rhs, b, lo_):
                for hd, cp, par in units():
                    c = slice((2 * cp + par) * CH, (2 * cp + par + 1) * CH)
                    last = nc.tensor.matmul(bank[b + hd][half(par), lo_ + cp * CH:lo_ + (cp + 1) * CH],
                                            lhs[half(hd), c], rhs[half(hd), c], start=True, stop=True)
                return last

            wait(m.vt_ready, m.att_ready)
            product(m.bt, m.at, 2, 0)
            product(m.bt, m.rt, 2, 256).then_inc(m.ub_ps.now(), 1)
            wait(m.btt_ready, m.ktt_ready)
            product(m.kt, m.at, 4, 0)
            product(m.kt, m.rt, 4, 256).then_inc(m.lk_ps.now(), 1)
            wait(m.bv_ready)
            product(m.at, m.bt, 6, 0).then_inc(m.l_ps.now(), 1)
            if more:
                pe_prepare_k(m, pe, nq, 0, 4)

            def blocks(lhs, rhs, b, n=CH, lo_=0):
                for hd, cp, par in units():
                    o = bank[b] if n == CH else bank[b + hd]
                    at = (hd * CP + cp) * CH if n == CH else cp * 2 * CH + lo_
                    w = rhs(hd, cp, par)
                    last = nc.tensor.matmul(o[half(par), at:at + w.shape[1]], lhs(hd, cp, par), w, start=True, stop=True)
                return last

            def mat(x):
                return lambda hd, cp, par: x[half(par), hd, cp, :]

            def tok(x):
                return lambda hd, cp, par: x[half(par), cp, hd * HD:(hd + 1) * HD]

            wait(m.masked_l)
            blocks(mat(m.ld), mat(m.ud), 2).then_inc(m.u2_ps.now(), 1)
            blocks(mat(m.ud), mat(m.ld), 3).then_inc(m.l2_ps.now(), 1)
            if more:
                pe_prepare_k(m, pe, nq, 4, C)
            wait(m.l2_ready, m.u2_ready, m.v1_ready)
            blocks(mat(m.l2), mat(m.u2), 4).then_inc(m.u4_ps.now(), 1)
            blocks(mat(m.l2), mat(m.v1), 5).then_inc(m.v2_ps.now(), 1)
            blocks(mat(m.u2), mat(m.l2), 6).then_inc(m.l4_ps.now(), 1)
            blocks(mat(m.lak), tok(m.vt), 7).then_inc(m.lv_ps.now(), 1)
            if more:
                pe_prepare_r(m, pe, nq, 0, 2)
            wait(m.l4_ready, m.v2_ready)
            blocks(mat(m.l4), mat(m.v2), 2).then_inc(m.v4_ps.now(), 1)
            wait(m.u4_ready)
            blocks(mat(m.u4), mat(m.l4), 3).then_inc(m.l8_ps.now(), 1)
            if more:
                pe_prepare_r(m, pe, nq, 2, 4)
            wait(m.l8_ready, m.v4_ready)
            blocks(mat(m.l8), mat(m.v4), 4).then_inc(m.dt_ps.now(), 1)
            if more:
                pe_prepare_r(m, pe, nq, 4, 6)
            wait(m.dt_ready)
            blocks(mat(m.lo_), mat(m.dt), 5).then_inc(m.mm_ps.now(), 1)
            blocks(mat(m.dt), mat(m.lo_), 6).then_inc(m.mt_ps.now(), 1)
            wait(m.lv_ready)
            blocks(mat(m.dt), tok(m.att), 2, n=2 * CH)
            blocks(mat(m.dt), mat(m.lv), 2, n=2 * CH, lo_=CH).then_inc(m.dr_ps.now(), 1)
            wait(m.mm_ready, m.mt_ready)
            blocks(mat(m.mt), mat(m.mm), 7).then_inc(m.m2_ps.now(), 1)
            if more:
                pe_prepare_r(m, pe, nq, 6, C)
            wait(m.dr_ready)
            blocks(mat(m.mm), mat(m.dr), 4, n=2 * CH).then_inc(m.x1_ps.now(), 1)
            if more:
                pe_prepare_norm(m, pe, nq)
                pe_prepare_v(m, pe, nq, 0, 2)
            wait(m.m2_ready, m.x1_ready)
            blocks(mat(m.m2), mat(m.x1), 6, n=2 * CH).then_inc(m.wz_ps.now(), 1)
            if more:
                pe_prepare_v(m, pe, nq, 2, 4)
            wait(m.wz_ready)

            for hd, cp, par in units():
                w = m.wz[half(par), hd, cp, 0:CH]
                nc.tensor.matmul(bank[2 + par][half(hd), cp * CH:(cp + 1) * CH], w, m.mrb[half(par), hd, cp, :],
                                 start=True, stop=True)
                last = nc.tensor.matmul(bank[2 + par][half(hd), 256 + cp * CH:256 + (cp + 1) * CH], w,
                                        m.btt[half(par), cp, hd * HD:(hd + 1) * HD], start=True, stop=True)
            last.then_inc(m.rg_ps.now(), 1)
            for hd, cp, par in units():
                z = m.wz[half(par), hd, cp, CH:2 * CH]
                v = m.vt[half(par), cp, hd * HD:(hd + 1) * HD]
                o = bank[4 + par][half(hd), cp * CH:(cp + 1) * CH]
                nc.tensor.matmul(o, m.btt[half(par), cp, hd * HD:(hd + 1) * HD], z, start=(cp == 0), stop=False,
                                 skip_group_check=True)
                nc.tensor.matmul(o, m.ktt[half(par), cp, hd * HD:(hd + 1) * HD], v, start=False, stop=False,
                                 skip_group_check=True)
                o = bank[6 + par][half(hd), cp * CH:(cp + 1) * CH]
                nc.tensor.matmul(o, z, m.mrb[half(par), hd, cp, :], start=(cp == 0), stop=False, skip_group_check=True)
                last = nc.tensor.matmul(o, v, m.mrk[half(par), hd, cp, :], start=False, stop=False,
                                        skip_group_check=True)
            last.then_inc(m.z_ps.now(), 1)
            if more:
                pe_wait(pe, m.n2_ready.sem, m.n2_ready.by(nq))
            pe_wait(pe, m.g2_in, 16 * q + 16)
            nc.tensor.matmul(bank[0], m.w_g2, m.hid[:, 2, :], start=True, stop=True).then_inc(m.g_ps.now(), 1)
            wait(m.gi_ready, m.rh_ready)
            wait(m.z_ps)
            for c in range(NCH):
                cp, par = c // 2, c % 2
                pe_wait(pe, m.s_ready, NCH * q + c + 1)
                if c + 1 < NCH:
                    for hd in range(2):
                        last = nc.tensor.matmul(bank[4 + par][half(hd), cp * CH:(cp + 1) * CH],
                                                m.gi[half(hd), par, cp, :], m.st[half(hd), c, :], start=False, stop=True,
                                                skip_group_check=True)
                    last.then_inc(m.s_ps, 1)
                for hd in range(2):
                    last = nc.tensor.matmul(bank[6 + par][half(hd), cp * CH:(cp + 1) * CH], m.st[half(hd), c, :],
                                            m.rh[half(hd), par, cp, :], start=False, stop=True, skip_group_check=True)
                if c == NCH - 1:
                    last.then_inc(m.y_ps.now(), 1)
                if more and c < 4:
                    pe_prepare_v(m, pe, nq, 4 + c, 5 + c)
            wait(m.y_ready)
            nc.tensor.matmul(bank[2], m.head_mean, m.y, start=True, stop=True).then_inc(m.mean_ps.now(), 1)
            wait(m.ysq_ready)
            nc.tensor.matmul(bank[3], m.head_mean, m.ysq, start=True, stop=True).then_inc(m.var_ps.now(), 1)

        def act_rwkv_pair(m, act, q, more):
            nq = q + 1

            def take(s, dst, src, done):
                act.wait_ge(s.sem, s.by(q))
                nc.scalar.copy(dst, src).then_inc(done.now(), 1)

            take(m.vt_ps, flat(m.vt), bank[2], m.vt_ready)
            take(m.att_ps, flat(m.att), bank[3], m.att_ready)
            take(m.btt_ps, flat(m.btt), bank[4], m.btt_ready)
            take(m.ktt_ps, flat(m.ktt), bank[5], m.ktt_ready)
            if more:
                act.wait_ge(m.ud_ready.sem, m.ud_ready.by(q))
                act_prepare_sigmoids(m, act, nq)
            take(m.l2_ps, flat(m.l2), bank[3], m.l2_ready)
            if more:
                act_prepare_k(m, act, nq)
            take(m.u4_ps, flat(m.u4), bank[4], m.u4_ready)
            take(m.l4_ps, flat(m.l4), bank[6], m.l4_ready)
            take(m.lv_ps, flat(m.lv), bank[7], m.lv_ready)
            take(m.l8_ps, flat(m.l8), bank[3], m.l8_ready)
            take(m.mm_ps, flat(m.mm), bank[5], m.mm_ready)
            take(m.dr_ps, flat(m.dr), psum[:, 2 * 512:4 * 512], m.dr_ready)
            take(m.m2_ps, flat(m.m2), bank[7], m.m2_ready)
            if more:
                act_prepare_r(m, act, nq)
                act_prepare_decays(m, act, nq)
                act_prepare_norm(m, act, nq)
            take(m.g_ps, m.g, bank[0], m.g_ready)
            for c in range(NCH - 1):
                cp, par = c // 2, c % 2
                act.wait_ge(m.s_ps, (NCH - 1) * q + c + 1)
                nc.scalar.activation(m.st[:, c + 1, :], bank[4 + par][:, cp * CH:(cp + 1) * CH], ACT.Copy,
                                     scale=m.wend[:, c:c + 1]).then_inc(m.s_ready, 1)
            act.wait_ge(m.y_ps.sem, m.y_ps.by(q))
            nc.scalar.copy(m.y.rearrange("p (c b t) -> p b c t", b=2, t=CH),
                           two_banks(6, 0, 256).rearrange("p b (c t) -> p b c t", t=CH)).then_inc(m.y_ready.now(), 1)
            if more:
                act_prepare_v(m, act, nq)
            act.wait_ge(m.yc_ready.sem, m.yc_ready.by(q))
            nc.scalar.activation(m.ysq, m.yc, ACT.Square).then_inc(m.ysq_ready.now(), 1)
            act.wait_ge(m.var_read, q + 2)
            nc.scalar.activation(m.yr, m.yr, ACT.Ln).then_inc(m.yln_ready.now(), 1)
            act.wait_ge(m.yln_ready.sem, m.yln_ready.by(q))
            nc.scalar.activation(m.yr, m.yr, ACT.Exp, scale=-0.5).then_inc(m.yrstd.now(), 1)

        def dve_rwkv_pair(m, dve, q, more):
            nq = q + 1

            def w(*results):
                dve_wait(dve, q, *results)

            nc.vector.tensor_copy(m.pt, m.vec[:, LNG:LNB + 1, bass.ds(q, 1)].rearrange("p n o -> p (n o)"))
            w(m.wc_ready)
            nc.vector.tensor_copy(m.wend, m.wc.rearrange("p (c t) -> p c t", t=CH)[:, :, CH - 1]
                                  ).then_inc(m.pt_ready.now(), 1)
            w(m.bonus_ps, m.v_ready)
            TTn(m.bv, bank[7], m.v, ALU.mult).then_inc(m.bv_ready.now(), 1)
            if more:
                dve_prepare_vectors(m, dve, nq)

            def mask(x):
                return x.unsqueeze(1).unsqueeze(1).broadcast_to([P, 2, CP, CH])

            def four(x):
                return x.rearrange("p b (c t) -> p b c t", t=CH)

            w(m.ub_ps)
            TTn(m.ud, four(two_banks(2, 0, 256)), mask(m.u_in), ALU.mult).then_inc(m.ud_ready.now(), 1)
            TTn(m.mrb, four(two_banks(2, 256, 256)), mask(m.upper_incl), ALU.mult).then_inc(m.masked_ub.now(), 1)
            w(m.lk_ps)
            TTn(m.lak, four(two_banks(4, 0, 256)), mask(m.upper), ALU.mult)
            TTn(m.mrk, four(two_banks(4, 256, 256)), mask(m.upper_incl), ALU.mult).then_inc(m.masked_lk.now(), 1)
            w(m.l_ps)
            lb = four(two_banks(6, 0, 256))
            TTn(m.ld, lb, mask(m.l_in), ALU.mult)
            TTn(m.lo_, lb, mask(m.l_out), ALU.mult).then_inc(m.masked_l.now(), 1)
            w(m.ud_ready)
            TTn(m.v1, m.ud, mask(m.eye), ALU.add).then_inc(m.v1_ready.now(), 1)
            w(m.u2_ps)
            nc.vector.tensor_copy(flat(m.u2), bank[2]).then_inc(m.u2_ready.now(), 1)
            if more:
                dve_prepare_decays(m, dve, nq)
            w(m.v1_ready, m.v2_ps)
            TTn(flat(m.v2), bank[5], flat(m.v1), ALU.add).then_inc(m.v2_ready.now(), 1)
            w(m.v2_ready, m.v4_ps)
            TTn(flat(m.v4), bank[2], flat(m.v2), ALU.add).then_inc(m.v4_ready.now(), 1)
            if more:
                dve_prepare_k(m, dve, nq)
            w(m.v4_ready, m.dt_ps)
            TTn(flat(m.dt), bank[4], flat(m.v4), ALU.add).then_inc(m.dt_ready.now(), 1)
            w(m.mt_ps)
            nc.vector.tensor_copy(flat(m.mt), bank[6]).then_inc(m.mt_ready.now(), 1)
            w(m.x1_ps, m.dr_ready)
            TTn(flat(m.x1), psum[:, 4 * 512:6 * 512], flat(m.dr), ALU.add).then_inc(m.x1_ready.now(), 1)
            if more:
                dve_prepare_norm(m, dve, nq)
            w(m.wz_ps, m.x1_ready)
            TTn(flat(m.wz), psum[:, 6 * 512:8 * 512], flat(m.x1), ALU.add).then_inc(m.wz_ready.now(), 1)
            w(m.rg_ps, m.wz_ready)
            TTn(m.gi, four(two_banks(2, 256, 256)), mask(m.eye), ALU.add).then_inc(m.gi_ready.now(), 1)
            TTn(m.rh, four(two_banks(2, 0, 256)), m.rt.rearrange("p (c b t) -> p b c t", b=2, t=CH),
                ALU.add).then_inc(m.rh_ready.now(), 1)
            nc.vector.memset(m.st[:, 0, :], 0.0).then_inc(m.s_ready, 1)
            if more:
                w(m.rh_ready)
                dve_prepare_rest(m, dve, nq)
            w(m.y_ready, m.mean_ps)
            TTn(m.yc, m.y, bank[2], ALU.subtract).then_inc(m.yc_ready.now(), 1)
            w(m.var_ps)
            TS(m.yr, bank[3], 1.0, LNX_EPS, ALU.mult, ALU.add).then_inc(m.var_read, 1)
            w(m.yrstd)
            TTn(m.yc, m.yc, m.yr, ALU.mult).then_inc(m.yn1_ready.now(), 1)
            w(m.yn1_ready)
            TS(m.yc, m.yc, m.pt[:, 0:1], m.pt[:, 1:2], ALU.mult, ALU.add).then_inc(m.yn2_ready.now(), 1)
            w(m.yn2_ready)
            TTn(m.yc, m.yc, m.bv, ALU.add).then_inc(m.yn3_ready.now(), 1)
            w(m.yn3_ready)
            TTn(m.yg[:, bass.ds(q, 1), :].rearrange("p o t -> p (o t)"), m.yc, m.g, ALU.mult).then_inc(m.pair_done, 1)
            dve.wait_ge(m.pair_done, q + 1)

        def pe_mix_out(m, pe, src, wts, wts_in, src_ready):
            pe.wait_ge(wts_in, 16)

            def add(t, c):
                for nh in range(2):
                    last = nc.tensor.matmul(bank[4 * (t % 2) + nh], src[:, c, t * P:(t + 1) * P],
                                            wts[:, c, nh * 512:(nh + 1) * 512], start=(c == 0), stop=(c == C - 1))
                if c == C - 1:
                    last.then_inc(m.mix_ps, 1)

            for c in range(C):
                pe.wait_ge(src_ready, c + 1)
                add(0, c)
                add(1, c)
            for t in range(2, TT):
                pe.wait_ge(m.mixed, t - 1)
                for c in range(C):
                    add(t, c)

        def dve_mix_out(m, dve):
            for t in range(TT):
                dve.wait_ge(m.mix_ps, t + 1)
                b = 4 * (t % 2)
                nc.vector.tensor_tensor(h[:, t, :], psum[:, b * 512:(b + 2) * 512], h[:, t, :],
                                        ALU.add).then_inc(m.mixed, 1)

        def pe_rwkv(m, pe):
            pe_norm(m, pe)
            pe_rwkv_hidden(m, pe)
            pe.wait_ge(m.masks_ready, 1)
            pe.wait_ge(m.hg_ready.sem, m.hg_ready.by(0))
            pe.wait_ge(m.xk_ready.sem, m.xk_ready.by(0))
            pe_prepare_low_rank(m, pe, 0)
            pe_prepare_k(m, pe, 0, 0, C)
            pe.wait_ge(m.xr_ready.sem, m.xr_ready.by(0))
            pe_prepare_r(m, pe, 0, 0, C)
            pe_prepare_norm(m, pe, 0)
            pe.wait_ge(m.xv_ready.sem, m.xv_ready.by(0))
            pe_prepare_v(m, pe, 0, 0, C)
            with pe.Fori(0, PAIRS - 1) as q:
                pe_rwkv_pair(m, pe, q, True)
            pe_rwkv_pair(m, pe, PAIRS - 1, False)
            pe_mix_out(m, pe, m.yg, m.wo, m.wo_in, m.pair_done)

        def act_rwkv(m, act):
            act.wait_ge(h_in, 16)
            act_norm(m, act)
            act_rwkv_hidden(m, act)
            act_prepare_sigmoids(m, act, 0)
            act_prepare_k(m, act, 0)
            act_prepare_r(m, act, 0)
            act_prepare_decays(m, act, 0)
            act_prepare_norm(m, act, 0)
            act_prepare_v(m, act, 0)
            with act.Fori(0, PAIRS - 1) as q:
                act_rwkv_pair(m, act, q, True)
            act_rwkv_pair(m, act, PAIRS - 1, False)

        def dve_rwkv(m, dve):
            dve.wait_ge(h_in, 16)
            dve_norm(m, dve)
            dve_rwkv_lerps(m, dve)
            dve.wait_ge(m.masks_ready, 1)
            dve.wait_ge(m.vec_ready, 1)
            dve_prepare_vectors(m, dve, 0)
            dve_prepare_decays(m, dve, 0)
            dve_prepare_k(m, dve, 0)
            dve_prepare_norm(m, dve, 0)
            dve_prepare_rest(m, dve, 0)
            with dve.Fori(0, PAIRS - 1) as q:
                dve_rwkv_pair(m, dve, q, True)
            dve_rwkv_pair(m, dve, PAIRS - 1, False)
            dve_mix_out(m, dve)

        TAPS = a["conv_w_dw"].shape[1]
        PAD = TAPS - 1
        PE_TAPS = 4
        DVE_TAPS = TAPS - PE_TAPS
        B1A, B1B, BDW, CLG, CLB = range(5)
        CONV_RING = RING // 2

        def top_of_ring(places):
            return places * (2 * C * F_EXP + 2 * D)

        class Conv:
            def __init__(self):
                m = Arena(big, top_of_ring(CONV_RING))
                self.layer = 1
                self.n_params = 1
                self.w2 = m.take(C, D)
                self.w1 = [m.take(C, 2, P) for _ in range(2)]
                m.at = max(m.at, stage_base)
                self.hn = [m.take(D) for _ in range(2)]
                self.dump = self.hn[0]
                self.g_row = m.take(D)
                self.hnT = m.take(C, T)
                self.u = [m.take(PAD + T) for _ in range(2)]
                self.sig = [m.take(T) for _ in range(2)]
                self.co = m.take(C, T)
                self.odd = [m.take(T) for _ in range(2)]
                self.diag = [m.take(PE_TAPS, P) for _ in range(2)]
                self.vec = m.take(5, C)
                self.taps = m.take(C, TAPS)
                self.ss, self.rstd = m.take(TT), m.take(TT)
                self.mean_of = m.take(P)
                self.mean = m.take(T)
                self.rs = m.take(T)
                self.sq = [self.u[b][:, 0:T] for b in range(2)]
                (self.params_in, self.squares, self.rstd_step, self.hn_ready, self.hnT_in_psum, self.hnT_ready,
                 self.vec_in, self.w1_in0, self.w1_in1, self.w2_in, self.pads_ready, self.up_ps, self.sig_ready,
                 self.gated, self.tap, self.co_ready, self.mean_ps, self.centred, self.sq_ready, self.var_ps,
                 self.rs_step, self.normed_, self.act_ready, self.mix_ps, self.mixed, self.bias_in, self.biased,
                 self.mean_of_ready, self.diag_ready, self.taps_ps) = (sem("conv_" + n) for n in (
                    "params_in squares rstd_step hn_ready hnT_in_psum hnT_ready vec_in w1_in0 w1_in1 "
                    "w2_in pads_ready up_ps sig_ready gated tap co_ready mean_ps centred sq_ready "
                    "var_ps rs_step normed_ act_ready mix_ps mixed bias_in biased mean_of_ready "
                    "diag_ready taps_ps").split())

        cv = Conv()

        def sp_conv(m, sp, memory_free):
            memory_free()
            sp.dma_start(m.g_row, a["norm1_g"][1:2, :].broadcast_to([P, D])).then_inc(m.params_in, 16)
            w1 = a["conv_w_pw1"][0].rearrange("(p c) (u q n) -> p c u q n", p=P, u=2, n=P)

            def load_w1(q, b):
                for u in range(2):
                    src = w1[:, :, u, q, :] if isinstance(q, int) else \
                        w1[:, :, u, bass.ds(q, 1), :].rearrange("p c o n -> p c (o n)")
                    sp.dma_start(m.w1[b][:, :, u, :], src).then_inc(m.w1_in0 if b == 0 else m.w1_in1, 16)

            for b in range(2):
                load_w1(b, b)
            with nc.allow_non_contiguous_dma("per-channel vectors"):
                for n, src in ((B1A, a["conv_b_pw1"][0][0:D]), (B1B, a["conv_b_pw1"][0][D:2 * D]),
                               (BDW, a["conv_b_dw"][0]), (CLG, a["conv_ln_g"][0]), (CLB, a["conv_ln_b"][0])):
                    sp.dma_start(m.vec[:, n, :], src.rearrange("(q p) -> p q", p=P)).then_inc(m.vec_in, 16)
                for q in range(C):
                    sp.dma_start(m.taps[:, q, :],
                                 a["conv_w_dw"][0][:, q * P:(q + 1) * P].rearrange("k p -> p k")).then_inc(m.vec_in, 16)
            sp.dma_start(m.w2, a["conv_w_pw2"][0].rearrange("(q p) d -> p q d", p=P)).then_inc(m.w2_in, 16)
            with sp.Fori(1, C // 2) as g:
                for b in range(2):
                    sp.wait_ge(m.up_ps, 2 * g + (b - 1))
                    load_w1(2 * g + b, b)
            sp.wait_ge(m.hn_ready, TT)
            sp.dma_start(m.g_row, a["conv_b_pw2"][0:1, :].broadcast_to([P, D])).then_inc(m.bias_in, 16)

        def pool_conv(m, pool, memory_free):
            memory_free()
            nc.gpsimd.memset(m.u[0][:, 0:PAD], 0.0).then_inc(m.pads_ready, 1)
            nc.gpsimd.memset(m.u[1][:, 0:PAD], 0.0).then_inc(m.pads_ready, 1)
            nc.gpsimd.memset(m.mean_of, 1.0 / D).then_inc(m.mean_of_ready, 1)
            pool.sem_inc(m.gated, FREE2)
            pool.sem_inc(m.co_ready, FREE2)

        def pe_conv(m, pe):
            pe_norm(m, pe)
            pe.wait_ge(m.hnT_ready, 2 * TT)

            def up(g, b):
                q = 2 * g + b
                pe_wait(pe, m.w1_in0 if b == 0 else m.w1_in1, 32 * g + 32)
                pe_wait(pe, m.gated, q + 1)
                for u in range(2):
                    for c in range(C):
                        last = nc.tensor.matmul(bank[2 + 2 * b + u], m.w1[b][:, c, u, :], m.hnT[:, c, :],
                                                start=(c == 0), stop=(c == C - 1))
                last.then_inc(m.up_ps, 1)

            def last_taps(q, b):
                pe_wait(pe, m.gated, FREE2 + q + 1)
                pe_wait(pe, m.diag_ready, q + 1)
                pe_wait(pe, m.co_ready, q + 1)
                for k in range(PE_TAPS):
                    at = DVE_TAPS + k
                    last = nc.tensor.matmul(bank[6 + b], m.diag[b][:, k, :], m.u[b][:, at:at + T], start=(k == 0),
                                            stop=(k == PE_TAPS - 1))
                last.then_inc(m.taps_ps, 1)

            up(0, 0)
            with pe.Fori(0, C // 2 - 1) as g:
                up(g, 1)
                last_taps(2 * g, 0)
                up(g + 1, 0)
                last_taps(2 * g + 1, 1)
            up(C // 2 - 1, 1)
            last_taps(C - 2, 0)
            last_taps(C - 1, 1)
            pe.wait_ge(m.mean_of_ready, 1)
            for q in range(C):
                pe.wait_ge(m.co_ready, FREE2 + q + 1)
                last = nc.tensor.matmul(bank[0], m.mean_of, m.co[:, q, :], start=(q == 0), stop=(q == C - 1))
            last.then_inc(m.mean_ps, 1)
            for q in range(C):
                pe.wait_ge(m.sq_ready, q + 1)
                nc.tensor.matmul(bank[1], m.mean_of, m.sq[q % 2], start=(q == 0),
                                 stop=(q == C - 1)).then_inc(m.var_ps, 1)
            pe.wait_ge(m.rs_step, 1)
            pe_mix_out(m, pe, m.co, m.w2, m.w2_in, m.act_ready)

        def act_conv(m, act, memory_free):
            memory_free()
            act_norm(m, act)
            act.wait_ge(m.vec_in, 16 * (5 + C))
            with act.Fori(0, C // 2) as g:
                for b in range(2):
                    q = 2 * g + b
                    act.wait_ge(m.up_ps, q + 1)
                    act.wait_ge(m.gated, q + 1)
                    nc.scalar.activation(m.sig[b], bank[3 + 2 * b], ACT.Sigmoid,
                                         bias=m.vec[:, B1B, bass.ds(q, 1)]).then_inc(m.sig_ready, 1)
                    act.wait_ge(m.co_ready, q + 1)
                    for k in range(PE_TAPS):
                        w = m.taps[:, bass.ds(q, 1), DVE_TAPS + k:DVE_TAPS + k + 1].rearrange("p o k -> p (o k)")
                        last = nc.scalar.activation(m.diag[b][:, k, :], ident[:], ACT.Copy, scale=w)
                    last.then_inc(m.diag_ready, 1)
            for q in range(C):
                act.wait_ge(m.centred, q + 1)
                if q >= 2:
                    act.wait_ge(m.var_ps, q - 1)
                nc.scalar.activation(m.sq[q % 2], m.co[:, q, :], ACT.Square).then_inc(m.sq_ready, 1)
            act.wait_ge(m.rs_step, 1)
            nc.scalar.activation(m.rs, m.rs, ACT.Ln).then_inc(m.rs_step, 1)
            act.wait_ge(m.rs_step, 2)
            nc.scalar.activation(m.rs, m.rs, ACT.Exp, scale=-0.5).then_inc(m.rs_step, 1)
            for q in range(C):
                act.wait_ge(m.normed_, q + 1)
                nc.scalar.activation(m.co[:, q, :], m.co[:, q, :], ACT.Silu, bias=m.vec[:, CLB, q:q + 1],
                                     scale=m.vec[:, CLG, q:q + 1]).then_inc(m.act_ready, 1)

        def dve_conv(m, dve, memory_free):
            memory_free()
            dve_norm(m, dve)
            dve.wait_ge(m.vec_in, 16 * (5 + C))
            dve.wait_ge(m.pads_ready, 2)

            def gate(q, b):
                dve.wait_ge(m.sig_ready, q + 1)
                dve.wait_ge(m.co_ready, q + 1)
                nc.vector.scalar_tensor_tensor(out=m.u[b][:, PAD:], in0=bank[2 + 2 * b],
                                               scalar=m.vec[:, B1A, bass.ds(q, 1)], in1=m.sig[b], op0=ALU.add,
                                               op1=ALU.mult).then_inc(m.gated, 1)

            def convolve(q, b, more):
                dve.wait_ge(m.gated, FREE2 + q + 1)
                even = m.co[:, bass.ds(q, 1), :].rearrange("p o t -> p (o t)")
                w = m.taps[:, bass.ds(q, 1), :].rearrange("p o k -> p (o k)")
                nc.vector.tensor_scalar(even, m.u[b][:, 0:T], w[:, 0:1], m.vec[:, BDW, bass.ds(q, 1)], ALU.mult,
                                        ALU.add).then_inc(m.tap, 1)
                dve.wait_ge(m.taps_ps, q + 1)
                dve.wait_ge(m.co_ready, q + 1)
                nc.vector.scalar_tensor_tensor(out=m.odd[b], in0=m.u[b][:, 1:1 + T], scalar=w[:, 1:2], in1=bank[6 + b],
                                               op0=ALU.mult, op1=ALU.add).then_inc(m.tap, 1)
                for k in range(2, DVE_TAPS):
                    if more and k == DVE_TAPS // 2:
                        gate(q + 1, 1 - b)
                    o = even if k % 2 == 0 else m.odd[b]
                    dve.wait_ge(m.tap, DVE_TAPS * q + k - 1)
                    nc.vector.scalar_tensor_tensor(out=o, in0=m.u[b][:, k:k + T], scalar=w[:, k:k + 1], in1=o,
                                                   op0=ALU.mult, op1=ALU.add).then_inc(m.tap, 1)
                dve.wait_ge(m.tap, DVE_TAPS * q + DVE_TAPS)
                nc.vector.tensor_tensor(even, even, m.odd[b], ALU.add).then_inc(m.co_ready, 1)

            gate(0, 0)
            with dve.Fori(0, C // 2 - 1) as g:
                convolve(2 * g, 0, True)
                convolve(2 * g + 1, 1, True)
            convolve(C - 2, 0, True)
            convolve(C - 1, 1, False)
            dve.wait_ge(m.bias_in, 16)
            for t in range(TT):
                nc.vector.tensor_tensor(h[:, t, :], h[:, t, :], m.g_row, ALU.add).then_inc(m.biased, 1)
            dve.wait_ge(m.mean_ps, 1)
            nc.vector.tensor_copy(m.mean, bank[0]).then_inc(m.mean_of_ready, 1)
            dve.wait_ge(m.mean_of_ready, 2)
            for q in range(C):
                nc.vector.tensor_tensor(m.co[:, q, :], m.co[:, q, :], m.mean, ALU.subtract).then_inc(m.centred, 1)
            dve.wait_ge(m.var_ps, C)
            nc.vector.tensor_scalar(m.rs, bank[1], LN_EPS, None, ALU.add).then_inc(m.rs_step, 1)
            dve.wait_ge(m.rs_step, 3)
            for q in range(C):
                nc.vector.tensor_tensor(m.co[:, q, :], m.co[:, q, :], m.rs, ALU.mult).then_inc(m.normed_, 1)
            dve.wait_ge(m.biased, TT)
            dve_mix_out(m, dve)

        block = ctx.enter_context(nc.Block())

        class Final:

            def __init__(self):
                m = Arena(big)
                self.n_params = 1
                self.hn = [m.take(D) for _ in range(2)]
                self.dump = m.take(D)
                self.g_row = m.take(D)
                self.ss, self.rstd = m.take(TT), m.take(TT)
                (self.params_in, self.squares, self.rstd_step, self.hn_ready, self.stored0, self.stored1) = (sem("final_" + n) for n in (
                    "params_in squares rstd_step hn_ready stored0 stored1").split())
                self.hn_stored = [self.stored0, self.stored1]

        fin = Final()

        @block.sync
        def _(sp):
            sp_rwkv(rw, sp)
            sp.wait_ge(rw.mixed, TT)
            sp_moe_params(moe[0], sp)
            sp_moe_weights(moe[0], sp, lambda j: None)
            sp_conv(cv, sp, lambda: sp.wait_ge(moe[0].h_step, 2 * TT))

            def place_free(j):
                if j == CONV_RING:
                    sp.wait_ge(cv.mixed, TT)
                    sp_moe_params(moe[1], sp)

            sp_moe_weights(moe[1], sp, place_free)
            sp.wait_ge(moe[1].h_step, 2 * TT)
            sp.dma_start(fin.g_row, a["final_g"].rearrange("(o d) -> o d", o=1).broadcast_to([P, D])
                         ).then_inc(fin.params_in, 16)
            out_tiles = out.rearrange("b (t p) d -> (b t) p d", p=P)
            for t in range(TT):
                sp.wait_ge(fin.hn_ready, t + 1)
                sp.dma_start(out_tiles[t], fin.hn[t % 2]).then_inc(fin.hn_stored[t % 2], 16)
            for b in range(2):
                sp.wait_ge(fin.hn_stored[b], 16 * TT // 2)

        @block.gpsimd
        def _(pool):
            pool_constants()
            pool.wait_ge(consts_ready, 1)
            pool_rwkv_masks(rw, pool)
            pool_moe(moe[0], pool)
            pool_conv(cv, pool, lambda: pool.wait_ge(moe[0].h_step, 2 * TT))
            pool_moe(moe[1], pool)

        @block.scalar
        def _(act):
            act_rwkv(rw, act)
            for m, before in ((moe[0], rw.mixed), (moe[1], cv.mixed)):
                act.wait_ge(before, TT)
                act_norm(m, act)
                act_route(m, act)
                rounds = act_moe(m, act)
                act_load_back(m, act, rounds)
                if m is moe[0]:
                    act_conv(cv, act, lambda: act.wait_ge(moe[0].h_step, 2 * TT))
            act.wait_ge(moe[1].h_step, 2 * TT)
            for t in range(TT):
                nc.scalar.activation(fin.dump, h[:, t, :], ACT.Square,
                                     accum_out=fin.ss[:, t:t + 1]).then_inc(fin.squares, 1)
                act.wait_ge(fin.squares, t + 1)
            act.wait_ge(fin.rstd_step, 1)
            nc.scalar.activation(fin.rstd, fin.rstd, ACT.Ln).then_inc(fin.rstd_step, 1)
            act.wait_ge(fin.rstd_step, 2)
            nc.scalar.activation(fin.rstd, fin.rstd, ACT.Exp, scale=-0.5).then_inc(fin.rstd_step, 1)

        @block.vector
        def _(dve):
            dve_rwkv(rw, dve)
            for m, before in ((moe[0], rw.mixed), (moe[1], cv.mixed)):
                dve.wait_ge(before, TT)
                dve_norm(m, dve)
                dve_route(m, dve)
                dve_moe(m, dve)
                dve_combine(m, dve)
                if m is moe[0]:
                    dve_conv(cv, dve, lambda: dve.wait_ge(moe[0].h_step, 2 * TT))
            dve.wait_ge(fin.squares, TT)
            nc.vector.tensor_scalar(fin.rstd, fin.ss, 1.0 / D, RMS_EPS, ALU.mult, ALU.add).then_inc(fin.rstd_step, 1)
            dve.wait_ge(fin.rstd_step, 3)
            dve.wait_ge(fin.params_in, 16)
            for t in range(TT):
                if t >= 2:
                    dve.wait_ge(fin.hn_stored[t % 2], 16)
                nc.vector.scalar_tensor_tensor(out=fin.hn[t % 2], in0=h[:, t, :], scalar=fin.rstd[:, t:t + 1],
                                               in1=fin.g_row, op0=ALU.mult, op1=ALU.mult).then_inc(fin.hn_ready, 1)

        @block.tensor
        def _(pe):
            pe_rwkv(rw, pe)
            for m in moe:
                pe_norm(m, pe)
                pe_logits(m, pe)
                pe_ranks(m, pe)
                pe_moe(m, pe)
                if m is moe[0]:
                    pe_conv(cv, pe)


_INS = ["x", "norm1_g", "norm2_g", "final_g", "rwkv_mu", "rwkv_w_rkv", "rwkv_w0", "rwkv_w1", "rwkv_w2", "rwkv_a0",
        "rwkv_a1", "rwkv_a2", "rwkv_g1", "rwkv_g2", "rwkv_k_k", "rwkv_k_a", "rwkv_r_k", "rwkv_ln_g", "rwkv_ln_b",
        "rwkv_w_o", "conv_w_pw1", "conv_b_pw1", "conv_w_dw", "conv_b_dw", "conv_ln_g", "conv_ln_b", "conv_w_pw2",
        "conv_b_pw2", "moe_w_group", "moe_b_group", "moe_w_expert", "moe_b_expert", "moe_w_gate", "moe_w_up",
        "moe_w_down"]


def kernel(**inputs):
    import numpy as _np
    import concourse.bacc as _bacc
    from concourse import mybir as _mybir
    from concourse.bass_utils import run_bass_kernel_spmd as _run

    nc = _bacc.Bacc("TRN2", target_bir_lowering=False, num_devices=1)
    arrays, args = {}, {}
    for name in _INS:
        v = _np.ascontiguousarray(inputs[name])
        arrays[f"in_{name}_dram"] = v
        args[name] = nc.dram_tensor(f"in_{name}_dram", v.shape, _mybir.dt.from_np(v.dtype), kind="ExternalInput").ap()
    out = nc.dram_tensor("out_dram", (1, T, D), _mybir.dt.float32, kind="ExternalOutput").ap()
    bass_hybrid_rwkv7_conformer_hmoe(nc, args, out)
    r = _run(nc, [arrays], core_ids=[0])
    return r.results[0]["out_dram"]
```

```python
import numpy as np

import concourse.bass as bass
from concourse import mybir
from contextlib import ExitStack

D = 1024
T = 512
DEPTH = 2
P = 128
TT = T // P
C = D // P
N_EXP = 32
N_GRP = 4
PER_GRP = N_EXP // N_GRP
F_EXP = 256
SLOTS = 64
RING = 4
NG = N_EXP // RING
RMS_EPS = 1e-6
FAR = 60000.0
LNX_EPS = 64e-5
LN_EPS = 1e-5


class Arena:

    def __init__(self, tensor, start=0):
        self.tensor, self.at = tensor, start

    def take(self, *shape, parts=P):
        n = 1
        for s in shape:
            n *= s
        v = self.tensor[0:parts, self.at:self.at + n]
        self.at += n
        assert self.at <= self.tensor.shape[1], (self.at, self.tensor.shape)
        if len(shape) == 2:
            v = v.rearrange("p (a b) -> p a b", b=shape[1])
        if len(shape) == 3:
            v = v.rearrange("p (a b c) -> p a b c", b=shape[1], c=shape[2])
        return v


class Steps:

    def __init__(self, sem):
        self.sem, self.n = sem, 0

    def done(self, ins):
        self.n += 1
        ins.then_inc(self.sem, 1)
        return self.n


class Signal:

    def __init__(self, made, sem, at, per_trip):
        self.made, self.sem, self.at, self.per_trip = made, sem, at, per_trip

    def by(self, trip):
        return self.per_trip * trip + self.at

    def now(self):
        assert self.made[0] % self.per_trip == self.at - 1, self.at
        self.made[0] += 1
        return self.sem


def signals(sem, n):
    made = [0]
    return [Signal(made, sem, i + 1, n) for i in range(n)]


def bass_hybrid_rwkv7_conformer_hmoe(nc, a, out):
    fp32 = mybir.dt.float32
    bf16 = mybir.dt.bfloat16
    u32 = mybir.dt.uint32
    i32 = mybir.dt.int32
    ALU = mybir.AluOpType
    ACT = mybir.ActivationFunctionType
    AX = mybir.AxisListType
    ctx = ExitStack()
    with ctx:
        def sb(name, shape, dt=fp32):
            return ctx.enter_context(nc.sbuf_tensor(name, shape, dt))

        def sem(name):
            return ctx.enter_context(nc.semaphore(name))

        h = sb("h", [P, TT, D])
        ident = sb("ident", [P, P])
        ones = sb("ones", [P, P])
        earlier = sb("earlier", [P, P])
        slot_of_col = sb("slot_of_col", [P, P])
        expert_iota = sb("expert_iota", [P, N_EXP])
        group_iota = sb("group_iota", [P, N_EXP])
        round_starts = sb("round_starts", [P, T // SLOTS - 1])
        token_code = sb("token_code", [P, TT, 2])
        half_shift = sb("half_shift", [P, 1])
        big = sb("big", [P, 48500 - TT * D])

        psum = ctx.enter_context(nc.psum_tensor("psum", [P, 8 * 512], fp32))
        bank = [psum[:, i * 512:(i + 1) * 512] for i in range(8)]
        NORM_BANKS = (6, 7)
        dump = psum[:, 2 * 512:4 * 512]

        chosen = [nc.dram_tensor(f"chosen{i}", [T * 4, D // 2], fp32, kind="Internal").ap() for i in range(DEPTH)]

        wg_rows = a["moe_w_gate"].rearrange("l e (p c) f -> (l e) p c f", p=P)
        wu_rows = a["moe_w_up"].rearrange("l e (p c) f -> (l e) p c f", p=P)
        wd_rows = a["moe_w_down"].rearrange("l e (k p) d -> (l e) p k d", p=P)

        top = Arena(big)
        ring = [dict(up=top.take(2, C, F_EXP), down=top.take(2, D)) for _ in range(RING)]
        stage_base = top.at

        class Moe:

            def __init__(self, layer):
                m = Arena(big, stage_base)
                self.layer = layer
                self.n_params = 5
                self.g_row = m.take(D)
                self.w_route = m.take(C, N_GRP + N_EXP)
                self.b_route = m.take(N_GRP + N_EXP)
                self.ss, self.rstd = m.take(TT), m.take(TT)
                self.hn = [m.take(D) for _ in range(2)]
                self.parts = [m.take(TT * D // 2).bitcast(bf16).rearrange("p (t d) -> p t d", d=D) for _ in range(3)]
                self.rest = m.take(D)
                hnT_at = m.at
                self.hnT = m.take(C, T)
                self.dead_at_end = m.at
                self.takes = [m.take(TT * 2 * SLOTS // 2).bitcast(bf16).rearrange("p (t s) -> p t s", t=TT)
                              for _ in range(2)]
                over = Arena(big, hnT_at)
                self.xT = [over.take(C, P) for _ in range(2)]
                self.silu = [m.take(P) for _ in range(2)]
                self.z = [m.take(P) for _ in range(2)]
                self.zT = [m.take(2, SLOTS) for _ in range(2)]
                self.y = [over.take(D // 2) for _ in range(RING)]
                n = N_GRP + N_EXP
                self.logits = m.take(TT, n)
                self.gl = m.take(TT, 8)
                self.gmax = m.take(TT, 8)
                self.gidx = m.take(TT, 8)
                self.gidx_f = m.take(TT)
                self.in_group = m.take(TT, N_EXP)
                self.el = m.take(TT, N_EXP)
                self.emax = m.take(TT, 8)
                self.eidx = m.take(TT, 8)
                self.eidx_f = m.take(TT, 2)
                self.pick = m.take(TT, 2, N_EXP)
                self.picks = m.take(TT, N_EXP)
                self.ranked = m.take(TT, 2, N_EXP)
                self.rank = m.take(TT, 2)
                self.route_rhs = m.take(TT, 2, N_EXP)
                self.place = m.take(TT, N_EXP)
                self.gexp = m.take(TT, N_GRP)
                self.gsum = m.take(TT)
                self.p_top = m.take(TT)
                self.ediff = m.take(TT)
                self.eexp = m.take(TT)
                self.gate = m.take(2, TT)
                self.cmax = m.take(1)
                self.over = m.take(T // SLOTS - 1)
                self.n_over = m.take(1)
                self.rounds = m.take(1)
                self.hot = m.take(TT * 2, P)
                self.far = m.take(N_EXP)
                self.idx = m.take(N_EXP)
                self.scatter_at = m.take(N_EXP)
                self.scatter_now = m.take(RING)
                self.back = [big[:, stage_base // 2 + 2 * D * t:stage_base // 2 + 2 * D * (t + 1)] for t in range(TT)]
                s = f"{layer}"
                self.params_in = sem("moe_params_in" + s)
                self.squares = sem("squares" + s)
                self.rstd_step = sem("rstd_step" + s)
                self.hn_ready = sem("hn_ready" + s)
                self.place_ready = sem("place_ready" + s)
                self.takes_ready = sem("takes_ready" + s)
                self.split = sem("split" + s)
                self.hnT_in_psum = sem("hnT_in_psum" + s)
                self.hnT_ready = sem("hnT_ready" + s)
                self.logits_in_psum = sem("logits_in_psum" + s)
                self.route = sem("route" + s)
                self.exp_ready = sem("exp_ready" + s)
                self.rank_in_psum = sem("rank_in_psum" + s)
                self.rounds_ready = sem("rounds_ready" + s)
                self.hot_ready = sem("hot_ready" + s)
                self.slots_in_psum = sem("slots_in_psum" + s)
                self.slot_step = sem("slot_step" + s)
                self.tables_ready = sem("tables_ready" + s)
                self.round_done = sem("round_done" + s)
                self.w_in = [sem(f"w_in{j}_" + s) for j in range(RING)]
                self.index_ready = sem("index_ready" + s)
                self.xT_in_psum = sem("xT_in_psum" + s)
                self.xT_ready = sem("xT_ready" + s)
                self.gate_up_done = sem("gate_up_done" + s)
                self.silu_ready = sem("silu_ready" + s)
                self.z_ready = sem("z_ready" + s)
                self.zT_in_psum = sem("zT_in_psum" + s)
                self.zT_ready = sem("zT_ready" + s)
                self.down_done = sem("down_done" + s)
                self.y_ready = sem("y_ready" + s)
                self.y_stored = [sem(f"y_stored{b}_" + s) for b in range(2)]
                self.y_free = sem("y_free" + s)
                self.back_in = [sem(f"back_in{t}_" + s) for t in range(TT)]
                self.h_step = sem("h_step" + s)

        moe = [Moe(i) for i in range(DEPTH)]
        ROUTED = 18
        consts_ready = sem("consts_ready")
        const_step = sem("const_step")
        h_in = [sem(f"h_in{t}") for t in range(TT)]
        out_stored = sem("out_stored")
        pool_tick = sem("pool_tick")


        def pool_constants():
            st = Steps(const_step)

            def wait():
                nc.gpsimd.wait_ge(const_step, st.n)

            st.done(nc.gpsimd.memset(ones[:], 1.0))
            st.done(nc.gpsimd.memset(half_shift[0:SLOTS, :], -2.0))
            wait()
            st.done(nc.gpsimd.memset(half_shift[SLOTS:P, :], -1.0))
            wait()
            st.done(nc.gpsimd.affine_select(out=ident[:], in_=ones[:], compare_op=ALU.is_equal, fill=0.0, base=0,
                                            pattern=[[-1, P]], channel_multiplier=1))
            st.done(nc.gpsimd.affine_select(out=earlier[:], in_=ones[:], compare_op=ALU.is_gt, fill=0.0, base=0,
                                            pattern=[[1, P]], channel_multiplier=-1))
            st.done(nc.gpsimd.iota(slot_of_col[:], pattern=[[0, 2], [1, SLOTS]], base=0, channel_multiplier=0,
                                   allow_small_or_imprecise_dtypes=True))
            st.done(nc.gpsimd.iota(expert_iota[:], pattern=[[1, N_EXP]], base=0, channel_multiplier=0,
                                   allow_small_or_imprecise_dtypes=True))
            st.done(nc.gpsimd.iota(group_iota[:], pattern=[[1, N_GRP], [0, PER_GRP]], base=0, channel_multiplier=0,
                                   allow_small_or_imprecise_dtypes=True))
            st.done(nc.gpsimd.iota(round_starts[:], pattern=[[SLOTS, T // SLOTS - 1]], base=SLOTS, channel_multiplier=0,
                                   allow_small_or_imprecise_dtypes=True))
            nc.gpsimd.iota(token_code[:].rearrange("p t k -> p (t k)"), pattern=[[2 * P, TT], [1, 2]], base=1,
                           channel_multiplier=2, allow_small_or_imprecise_dtypes=True).then_inc(consts_ready, 1)

        FREE2 = 2
        FREE1 = 1

        def sp_moe_params(m, sp):
            i = m.layer
            with nc.allow_non_contiguous_dma("small router tables"):
                sp.dma_start(m.g_row, a["norm2_g"][i:i + 1, :].broadcast_to([P, D])).then_inc(m.params_in, 16)
                sp.dma_start(m.w_route[:, :, 0:N_GRP],
                             a["moe_w_group"][i].rearrange("(p c) g -> p c g", p=P)).then_inc(m.params_in, 16)
                sp.dma_start(m.w_route[:, :, N_GRP:],
                             a["moe_w_expert"][i].rearrange("(p c) g -> p c g", p=P)).then_inc(m.params_in, 16)
                sp.dma_start(m.b_route[:, 0:N_GRP],
                             a["moe_b_group"][i:i + 1, :].broadcast_to([P, N_GRP])).then_inc(m.params_in, 16)
                sp.dma_start(m.b_route[:, N_GRP:],
                             a["moe_b_expert"][i:i + 1, :].broadcast_to([P, N_EXP])).then_inc(m.params_in, 16)

        def sp_load_expert(m, sp, j, e):
            n = m.layer * N_EXP + e
            for src, dst in ((wg_rows, ring[j]["up"][:, 0]), (wu_rows, ring[j]["up"][:, 1]), (wd_rows, ring[j]["down"])):
                s = src[n:n + 1] if isinstance(n, int) else src[bass.ds(n, 1)]
                sp.dma_start(dst, s.rearrange("o p k f -> (o p) k f")).then_inc(m.w_in[j], 16)

        def sp_moe_weights(m, sp, first):
            for j, free in first:
                free()
                sp_load_expert(m, sp, j, j)
            with sp.Fori(1, NG) as g:
                for j in range(RING):
                    sp.wait_ge(m.down_done, FREE2 + 4 * g + (j - 3))
                    sp_load_expert(m, sp, j, g * RING + j)
            sp.wait_ge(m.rounds_ready, 1)
            rounds = sp.value_load(m.rounds[0:1, 0:1].bitcast(i32), min_val=1, max_val=T // SLOTS)
            with sp.If(rounds > 1):
                with sp.Fori(1, rounds) as r:
                    with sp.Fori(0, NG) as g:
                        for j in range(RING):
                            sp.wait_ge(m.down_done, FREE2 + N_EXP * r + 4 * g + (j - 3))
                            sp_load_expert(m, sp, j, g * RING + j)
            return rounds

        EACH_TILE = tuple((t, t + 1) for t in range(TT))
        LAST_ALONE = ((0, TT - 1), (TT - 1, TT))
        ALL_TILES = ((0, TT),)

        def act_norm_rows(m, act, tile_ready, groups, g):
            first, end = groups[g]
            for t in range(first, end):
                tile_ready(t)
                if t:
                    act.wait_ge(m.squares, t)
                nc.scalar.activation(dump, h[:, t, :], ACT.Square, accum_out=m.ss[:, t:t + 1]).then_inc(m.squares, 1)
            rstd = m.rstd[:, first:end]
            act.wait_ge(m.rstd_step, 3 * g + 1)
            nc.scalar.activation(rstd, rstd, ACT.Ln).then_inc(m.rstd_step, 1)
            act.wait_ge(m.rstd_step, 3 * g + 2)
            nc.scalar.activation(rstd, rstd, ACT.Exp, scale=-0.5).then_inc(m.rstd_step, 1)

        def act_norm(m, act, tile_ready, groups):

            def columns(g):
                for t in range(*groups[g]):
                    act.wait_ge(m.hnT_in_psum, t + 1)
                    for half in range(2):
                        nc.scalar.copy(m.hnT[:, 4 * half:4 * half + 4, t * P:(t + 1) * P],
                                       bank[NORM_BANKS[half]].rearrange("p (c t) -> p c t", t=P)).then_inc(m.hnT_ready, 1)

            for g in range(len(groups)):
                act_norm_rows(m, act, tile_ready, groups, g)
                if g:
                    columns(g - 1)
            columns(len(groups) - 1)

        def dve_split(m, dve, t):
            high, mid, low = (x[:, t, :] for x in m.parts)
            hn, n = m.hn[t % 2], 4 * t
            nc.vector.tensor_copy(high, hn).then_inc(m.split, 1)
            dve.wait_ge(m.split, n + 1)
            nc.vector.tensor_tensor(m.rest, hn, high, ALU.subtract).then_inc(m.split, 1)
            dve.wait_ge(m.split, n + 2)
            nc.vector.tensor_copy(mid, m.rest).then_inc(m.split, 1)
            dve.wait_ge(m.split, n + 3)
            nc.vector.tensor_tensor(low, m.rest, mid, ALU.subtract).then_inc(m.split, 1)
            dve.wait_ge(m.split, n + 4)

        def dve_norm(m, dve, tile_ready, groups, after=lambda t: None):

            def rows(g):
                dve.wait_ge(m.rstd_step, 3 * g + 3)
                if g == 0:
                    dve.wait_ge(m.params_in, 16 * m.n_params)
                for t in range(*groups[g]):
                    if t >= len(m.hn):
                        dve.wait_ge(m.hnT_in_psum, t - 1)
                    nc.vector.scalar_tensor_tensor(out=m.hn[t % len(m.hn)], in0=h[:, t, :], scalar=m.rstd[:, t:t + 1],
                                                   in1=m.g_row, op0=ALU.mult, op1=ALU.mult).then_inc(m.hn_ready, 1)
                    dve.wait_ge(m.hn_ready, t + 1)
                    after(t)

            for g, (first, end) in enumerate(groups):
                for t in range(first, end):
                    tile_ready(t)
                if g and groups is LAST_ALONE:
                    rows(g - 1)
                dve.wait_ge(m.squares, end)
                nc.vector.tensor_scalar(m.rstd[:, first:end], m.ss[:, first:end], 1.0 / D, RMS_EPS, ALU.mult,
                                        ALU.add).then_inc(m.rstd_step, 1)
                if groups is not LAST_ALONE or end == TT:
                    rows(g)

        def pe_norm_columns(m, pe, t):
            pe.wait_ge(m.hn_ready, t + 1)
            if t:
                pe.wait_ge(m.hnT_ready, 2 * t)
            rows = m.hn[t % len(m.hn)].rearrange("p (f c) -> p c f", c=C)
            for c in range(C):
                last = nc.tensor.transpose(bank[NORM_BANKS[c // 4]][:, (c % 4) * P:(c % 4 + 1) * P], rows[:, c, :],
                                           ident[:])
            last.then_inc(m.hnT_in_psum, 1)

        def pe_norm(m, pe):
            pe.wait_ge(consts_ready, 1)
            for t in range(TT):
                pe_norm_columns(m, pe, t)

        def pe_logits(m, pe):
            pe.wait_ge(m.params_in, 16 * m.n_params)
            n = N_GRP + N_EXP
            for t in range(TT):
                pe.wait_ge(m.hnT_ready, 2 * t + 2)
                for c in range(C):
                    last = nc.tensor.matmul(bank[2][:, t * n:(t + 1) * n], m.hnT[:, c, t * P:(t + 1) * P],
                                            m.w_route[:, c, :], start=(c == 0), stop=(c == C - 1))
            last.then_inc(m.logits_in_psum, 1)

        def dve_route(m, dve):
            st = Steps(m.route)

            def step(ins):
                dve.wait_ge(m.route, st.done(ins))

            n = N_GRP + N_EXP
            dve.wait_ge(consts_ready, 1)
            step(nc.vector.memset(m.gl, -3.0e38))
            dve.wait_ge(m.logits_in_psum, 1)
            step(nc.vector.tensor_tensor(m.logits, bank[2][:, 0:TT * n].rearrange("p (t n) -> p t n", n=n),
                                         m.b_route.unsqueeze(1).broadcast_to([P, TT, n]), ALU.add))
            step(nc.vector.tensor_copy(m.gl[:, :, 0:N_GRP], m.logits[:, :, 0:N_GRP]))
            for t in range(TT):
                last = nc.vector.max(m.gmax[:, t, :], m.gl[:, t, :])
            step(last)
            for t in range(TT):
                last = nc.vector.max_index(m.gidx[:, t, :].bitcast(u32), m.gmax[:, t, :], m.gl[:, t, :])
            step(last)
            step(nc.vector.tensor_copy(m.gidx_f, m.gidx[:, :, 0].bitcast(u32)))
            step(nc.vector.tensor_tensor(m.in_group, group_iota[:].unsqueeze(1).broadcast_to([P, TT, N_EXP]),
                                         m.gidx_f.unsqueeze(2).broadcast_to([P, TT, N_EXP]), ALU.is_equal))
            step(nc.vector.tensor_scalar(m.in_group, m.in_group, -1.0, 3.0e38, ALU.add, ALU.mult))
            step(nc.vector.tensor_tensor(m.el, m.in_group, m.logits[:, :, N_GRP:], ALU.add))
            for t in range(TT):
                last = nc.vector.max(m.emax[:, t, :], m.el[:, t, :])
            step(last)
            for t in range(TT):
                last = nc.vector.max_index(m.eidx[:, t, :].bitcast(u32), m.emax[:, t, :], m.el[:, t, :])
            step(last)
            step(nc.vector.tensor_copy(m.eidx_f, m.eidx[:, :, 0:2].bitcast(u32)))
            for k in range(2):
                last = nc.vector.tensor_tensor(m.pick[:, :, k, :], expert_iota[:].unsqueeze(1).broadcast_to([P, TT, N_EXP]),
                                               m.eidx_f[:, :, k:k + 1].broadcast_to([P, TT, N_EXP]), ALU.is_equal)
            step(last)
            step(nc.vector.tensor_tensor(m.picks, m.pick[:, :, 0, :], m.pick[:, :, 1, :], ALU.add))
            step(nc.vector.tensor_tensor(m.gexp, m.logits[:, :, 0:N_GRP], m.gmax[:, :, 0:1].broadcast_to([P, TT, N_GRP]),
                                         ALU.subtract))
            step(nc.vector.tensor_tensor(m.ediff, m.emax[:, :, 1], m.emax[:, :, 0], ALU.subtract))
            step(nc.vector.tensor_tensor(m.route_rhs, m.pick, token_code[:].unsqueeze(3).broadcast_to([P, TT, 2, N_EXP]),
                                         ALU.mult))
            dve.wait_ge(m.exp_ready, 2)
            step(nc.vector.tensor_reduce(m.gsum, m.gexp, AX.X, ALU.add))
            assert st.n == ROUTED
            step(nc.vector.reciprocal(m.p_top, m.gsum))
            step(nc.vector.tensor_scalar(m.ediff, m.eexp, 1.0, None, ALU.add))
            step(nc.vector.reciprocal(m.ediff, m.ediff))
            step(nc.vector.tensor_tensor(m.gate[:, 0, :], m.ediff, m.p_top, ALU.mult))
            step(nc.vector.tensor_tensor(m.gate[:, 1, :], m.gate[:, 0, :], m.eexp, ALU.mult))
            dve.wait_ge(m.rank_in_psum, 1)
            ranks = bank[3][:, 0:TT * N_EXP].rearrange("p (t e) -> p t e", e=N_EXP)
            step(nc.vector.scalar_tensor_tensor(out=m.place, in0=ranks, scalar=1.0, in1=m.picks, op0=ALU.add, op1=ALU.mult))
            nc.vector.tensor_scalar(m.place, m.place, -1.0, None, ALU.add).then_inc(m.place_ready, 1)
            for k in range(2):
                last = nc.vector.tensor_tensor(m.ranked[:, :, k, :], ranks, m.pick[:, :, k, :], ALU.mult)
            step(last)
            step(nc.vector.tensor_reduce(m.rank, m.ranked, AX.X, ALU.add))
            step(nc.vector.tensor_reduce(m.cmax, bank[3][:, TT * N_EXP:(TT + 1) * N_EXP], AX.X, ALU.max))
            step(nc.vector.tensor_scalar(m.over, round_starts[:], m.cmax, None, ALU.is_lt))
            step(nc.vector.tensor_reduce(m.n_over, m.over, AX.X, ALU.add))
            nc.vector.tensor_scalar(m.rounds.bitcast(i32), m.n_over, 1.0, None, ALU.add).then_inc(m.rounds_ready, 1)

        def act_route(m, act):
            act.wait_ge(m.route, 16)
            nc.scalar.activation(m.gexp, m.gexp, ACT.Exp).then_inc(m.exp_ready, 1)
            nc.scalar.activation(m.eexp, m.ediff, ACT.Exp).then_inc(m.exp_ready, 1)

        def pe_ranks(m, pe):
            pe.wait_ge(m.route, 14)
            for t in range(TT + 1):
                o = bank[3][:, t * N_EXP:(t + 1) * N_EXP]
                for u in range(min(t + 1, TT)):
                    last = nc.tensor.matmul(o, earlier[:] if u == t else ones[:], m.picks[:, u, :],
                                            start=(u == 0), stop=(u == min(t, TT - 1)))
            last.then_inc(m.rank_in_psum, 1)

        def load_rounds(m, eng):
            eng.wait_ge(m.rounds_ready, 1)
            return eng.value_load(m.rounds[0:1, 0:1].bitcast(i32), min_val=1, max_val=T // SLOTS)

        def dve_takes(m, dve, r, p, b):
            dve.wait_ge(m.place_ready, r + 1)
            place = m.place[:, :, bass.ds(2 * p, 2)]
            nc.vector.tensor_tensor(m.takes[b].rearrange("p t (e s) -> p t e s", s=SLOTS),
                                    slot_of_col[:].rearrange("p (e s) -> p e s", s=SLOTS).unsqueeze(1)
                                    .broadcast_to([P, TT, 2, SLOTS]),
                                    place.unsqueeze(3).broadcast_to([P, TT, 2, SLOTS]),
                                    ALU.is_equal).then_inc(m.takes_ready, 1)

        def dve_slots(m, dve, r):
            for i in range(TT * 2):
                nc.vector.tensor_scalar(m.hot[:, i, :], slot_of_col[:], m.rank[:, i // 2, i % 2:i % 2 + 1], None,
                                        ALU.is_equal).then_inc(m.hot_ready, 1)

        def dve_tables(m, dve, r):
            S = 4
            dve.wait_ge(m.hot_ready, TT * 2 * (r + 1))
            nc.vector.tensor_scalar(m.rank, m.rank, -float(SLOTS), None, ALU.add).then_inc(m.slot_step, 1)
            dve.wait_ge(m.slot_step, S * r + 1)
            dve.wait_ge(m.slots_in_psum, r + 1)
            dve.wait_ge(m.round_done, r + 1)
            v = bank[2][:, 0:N_EXP]
            nc.vector.tensor_scalar(m.far, v, 0.0, FAR, ALU.is_equal, ALU.mult).then_inc(m.slot_step, 1)
            nc.vector.tensor_scalar(m.idx, v, 2.0, half_shift[:, 0:1], ALU.mult, ALU.add).then_inc(m.slot_step, 1)
            dve.wait_ge(m.slot_step, S * r + 3)
            nc.vector.tensor_tensor(m.scatter_at.bitcast(i32), m.idx, m.far, ALU.add).then_inc(m.slot_step, 1)
            dve.wait_ge(m.slot_step, S * r + S)
            dve.sem_inc(m.tables_ready, 1)

        def pe_slots(m, pe, r):
            for i in range(TT * 2):
                pe.wait_ge(m.hot_ready, TT * 2 * r + i + 1)
                last = nc.tensor.matmul(bank[2][:, 0:N_EXP], m.hot[:, i, :], m.route_rhs[:, i // 2, i % 2, :],
                                        start=(i == 0), stop=(i == TT * 2 - 1))
            last.then_inc(m.slots_in_psum, 1)

        def pool_moe(m, pool):
            pool.sem_inc(m.z_ready, FREE2)
            pool.sem_inc(m.gate_up_done, FREE2)
            pool.sem_inc(m.down_done, FREE2)
            pool.sem_inc(m.y_ready, FREE2)
            pool.sem_inc(m.zT_ready, FREE1)
            pool.sem_inc(m.xT_ready, FREE1)
            pool.sem_inc(m.y_free, RING)
            pool.sem_inc(m.round_done, 1)
            rounds = load_rounds(m, pool)

            with pool.Fori(0, rounds) as r:
                pool.wait_ge(m.tables_ready, r + 1)
                pool.sem_inc(pool_tick)

                def scatter(g, j):
                    n, e = N_EXP * r + 4 * g + j, 4 * g + j
                    pool.wait_ge(m.y_ready, FREE2 + n + 1)
                    pool.sem_inc(pool_tick)
                    nc.gpsimd.tensor_copy(m.scatter_now[:, j:j + 1].bitcast(i32),
                                          m.scatter_at[:, bass.ds(e, 1)].bitcast(i32)).then_inc(m.index_ready, 1)
                    pool.wait_ge(m.index_ready, n + 1)
                    pool.sem_inc(pool_tick)
                    nc.gpsimd.indirect_dma_start(
                        chosen[m.layer],
                        bass.IndirectOffsetOnAxis(ap=m.scatter_now[:, j:j + 1].bitcast(u32), axis=0),
                        m.y[j], None, bounds_check=T * 4 - 1, oob_is_err=False).then_inc(m.y_stored[j % 2], 16)

                def scattered(g, j):
                    pool.wait_ge(m.y_stored[j % 2], 16 * (NG * 2 * r + 2 * g + j // 2) + 16)
                    pool.sem_inc(m.y_free)

                scatter(0, 0)
                with pool.Fori(0, NG - 1) as g:
                    for j in range(RING):
                        scatter(g + (j + 1) // RING, (j + 1) % RING)
                        scattered(g, j)
                for j in range(RING):
                    if j + 1 < RING:
                        scatter(NG - 1, j + 1)
                    scattered(NG - 1, j)
                pool.sem_inc(m.round_done, 1)
            return rounds

        def pe_moe(m, pe):
            rounds = load_rounds(m, pe)
            pe.wait_ge(m.split, 4 * TT)
            with pe.Fori(0, rounds) as r:

                def gather(p, b):
                    pair = NG * 2 * r + p
                    pe.wait_ge(m.takes_ready, pair + 1)
                    pe.wait_ge(m.xT_ready, FREE1 + pair)
                    for c in range(C):
                        for t in range(TT):
                            for n, part in enumerate(m.parts):
                                last = nc.tensor.matmul(bank[c // 4][:, (c % 4) * P:(c % 4 + 1) * P],
                                                        part[:, t, :].rearrange("p (f c) -> p c f", c=C)[:, c, :],
                                                        m.takes[b][:, t, :], start=(t == 0 and n == 0),
                                                        stop=(t == TT - 1 and n == 2))
                    last.then_inc(m.xT_in_psum, 1)

                def gate_up(g, j):
                    n = N_EXP * r + 4 * g + j
                    if j % 2 == 0:
                        pe.wait_ge(m.xT_ready, FREE1 + 1 + NG * 2 * r + 2 * g + j // 2)
                    pe.wait_ge(m.w_in[j], 48 * NG * r + 48 * g + 48)
                    pe.wait_ge(m.z_ready, n + 1)
                    o = bank[4 + j % 2]
                    for c in range(C):
                        for half in range(2):
                            last = nc.tensor.matmul(
                                o[half * SLOTS:(half + 1) * SLOTS, 0:F_EXP].rearrange("p (u f) -> p u f", u=2),
                                m.xT[j // 2][:, c, (j % 2) * SLOTS:(j % 2 + 1) * SLOTS],
                                ring[j]["up"][:, :, c, half * P:(half + 1) * P], start=(c == 0), stop=(c == C - 1))
                    last.then_inc(m.gate_up_done, 1)

                def down(g, j):
                    n = N_EXP * r + 4 * g + j
                    pe.wait_ge(m.z_ready, FREE2 + 1 + n)
                    pe.wait_ge(m.zT_ready, FREE1 + n)
                    nc.tensor.transpose(bank[3][:, 0:P], m.z[j % 2], ident[:]).then_inc(m.zT_in_psum, 1)
                    pe.wait_ge(m.zT_ready, FREE1 + 1 + n)
                    pe.wait_ge(m.y_ready, n + 1)
                    for k in range(2):
                        for half in range(2):
                            last = nc.tensor.matmul(bank[6 + j % 2][half * SLOTS:(half + 1) * SLOTS, :],
                                                    m.zT[j % 2][:, k, :],
                                                    ring[j]["down"][:, k, half * 512:(half + 1) * 512],
                                                    start=(k == 0), stop=(k == 1))
                    last.then_inc(m.down_done, 1)

                gather(0, 0)
                pe_slots(m, pe, r)
                gate_up(0, 0)
                with pe.Fori(0, NG - 1) as g:
                    for j in range(RING):
                        if j % 2 == 0:
                            gather(2 * g + (j // 2 + 1), 1 - j // 2)
                        gate_up(g + (j + 1) // RING, (j + 1) % RING)
                        down(g, j)
                gather(2 * NG - 1, 1)
                for j in range(RING):
                    if j + 1 < RING:
                        gate_up(NG - 1, j + 1)
                    down(NG - 1, j)

        def act_moe(m, act):
            rounds = load_rounds(m, act)
            with act.Fori(0, rounds) as r:
                with act.Fori(0, NG) as g:
                    for j in range(RING):
                        n = N_EXP * r + 4 * g + j
                        act.wait_ge(m.gate_up_done, FREE2 + 1 + n)
                        act.wait_ge(m.z_ready, n + 1)
                        nc.scalar.activation(m.silu[j % 2], bank[4 + j % 2][:, 0:P], ACT.Silu).then_inc(m.silu_ready, 1)
                        act.wait_ge(m.zT_in_psum, n + 1)
                        act.wait_ge(m.down_done, n + 1)
                        nc.scalar.copy(m.zT[j % 2].rearrange("p k s -> p (k s)"), bank[3][:, 0:P]).then_inc(m.zT_ready, 1)
                        act.wait_ge(m.down_done, FREE2 + 1 + n)
                        act.wait_ge(m.y_free, n + 1)
                        nc.scalar.copy(m.y[j], bank[6 + j % 2][:]).then_inc(m.y_ready, 1)
            return rounds

        def dve_moe(m, dve):
            rounds = load_rounds(m, dve)
            with dve.Fori(0, rounds) as r:

                def take_rows(p, b):
                    dve.wait_ge(m.xT_in_psum, NG * 2 * r + p + 1)
                    flat = m.xT[b].rearrange("p c s -> p (c s)")
                    nc.vector.tensor_copy(flat[:, 0:512], bank[0][:])
                    nc.vector.tensor_copy(flat[:, 512:1024], bank[1][:]).then_inc(m.xT_ready, 1)

                def gated(g, j):
                    n = N_EXP * r + 4 * g + j
                    dve.wait_ge(m.silu_ready, n + 1)
                    nc.vector.tensor_tensor(m.z[j % 2], m.silu[j % 2], bank[4 + j % 2][:, P:2 * P],
                                            ALU.mult).then_inc(m.z_ready, 1)

                dve_takes(m, dve, r, 0, 0)
                dve_takes(m, dve, r, 1, 1)
                dve_slots(m, dve, r)
                dve.wait_ge(m.down_done, FREE2 + N_EXP * r)
                take_rows(0, 0)
                dve_tables(m, dve, r)
                with dve.Fori(0, NG - 1) as g:
                    for j in range(RING):
                        gated(g, j)
                        if j % 2 == 0:
                            take_rows(2 * g + (j // 2 + 1), 1 - j // 2)
                            dve_takes(m, dve, r, 2 * g + (j // 2 + 2), j // 2)
                for j in range(RING):
                    gated(NG - 1, j)
                    if j == 0:
                        take_rows(2 * NG - 1, 1)
                dve.wait_ge(m.takes_ready, NG * 2 * (r + 1))
                nc.vector.tensor_scalar(m.place, m.place, -float(SLOTS), None, ALU.add).then_inc(m.place_ready, 1)
            return rounds

        def act_load_back(m, act, rounds):
            back = chosen[m.layer].rearrange("(t p c) n -> t p (c n)", p=P, c=4)

            act.wait_ge(m.round_done, rounds + 1)
            for t in range(TT):
                act.dma_start(m.back[t], back[t]).then_inc(m.back_in[t], 16)
            return lambda t: act.wait_ge(m.h_step, 2 * (t + 1))

        def dve_combine(m, dve, t):
            dve.wait_ge(m.back_in[t], 16)
            for k in range(2):
                if k:
                    dve.wait_ge(m.h_step, 2 * t + 1)
                nc.vector.scalar_tensor_tensor(out=h[:, t, :], in0=m.back[t][:, k * D:(k + 1) * D],
                                               scalar=m.gate[:, k, t:t + 1], in1=h[:, t, :], op0=ALU.mult,
                                               op1=ALU.add).then_inc(m.h_step, 1)
            dve.wait_ge(m.h_step, 2 * t + 2)

        CH = 64
        HD = 64
        NCH = T // CH
        CP = NCH // 2
        PAIRS = D // P
        DECAY = float(np.exp(-0.5))
        N_VEC = 8
        W0, A0, KK, KA, RK, LNG, LNB, KA1 = range(N_VEC)


        class Rwkv:
            def __init__(self):
                m = Arena(big)
                self.layer = 0
                self.hnT = m.take(C, T)
                self.xr, self.xk, self.xv = (m.take(C, T) for _ in range(3))
                yg_at = big.shape[1] - PAIRS * T
                self.yg = big[:, yg_at:].rearrange("p (q t) -> p q t", t=T)
                assert yg_at >= moe[0].dead_at_end
                self.w = m.take(3, C, P)
                self.w_lora = m.take(2, P)
                self.w_g2 = m.take(P)
                self.hid = m.take(3, T)
                self.vec = m.take(N_VEC, PAIRS)
                self.pv = m.take(N_VEC)
                self.pt = m.take(2)
                self.wend = m.take(NCH)
                hn_at = m.at
                self.hn = [m.take(D) for _ in range(2)]
                self.lora1 = m.take(C, 2 * 64 + P)
                self.mu = m.take(6, C)
                self.ss, self.rstd = m.take(TT), m.take(TT)
                self.keep = m.take(T)
                self.upper = m.take(CH)
                self.upper_incl = m.take(CH)
                self.u_in = m.take(CH)
                self.l_in, self.l_out = m.take(CH), m.take(CH)
                self.eye = m.take(CH)
                self.block16 = m.take(CH)
                self.tmp_mask = m.take(CH)
                self.heads = m.take(P)
                self.head_mean = m.take(P)
                tiles = m.at
                t = Arena(big, tiles)
                self.g_row = big[:, tiles + D:tiles + 2 * D]
                self.xx = big[:, tiles + 2 * D:tiles + 2 * D + C * T].rearrange("p (c t) -> p c t", t=T)
                self.xw = self.yg
                self.xa = big[:, tiles + 6 * D:tiles + 6 * D + C * T].rearrange("p (c t) -> p c t", t=T)
                self.xg_ = self.xv
                f = Arena(big, tiles)
                lo = Arena(big, 0)
                (self.sig, self.a, self.cum, self.cprev, self.wc, self.winv, self.kraw, self.rraw, self.kk2, self.at,
                 self.kka, self.km, self.kt, self.rt, self.v) = (f.take(T) for _ in range(15))
                self.wprev, self.rs, self.kkn = self.cprev, self.kk2, self.kk2
                self.bt, self.k2, self.rk = self.kka, self.km, self.sig
                self.g, self.bv = f.take(T), f.take(T)
                (self.ud, self.ld, self.lo_, self.mrb, self.lak, self.mrk, self.lv,
                 self.gi) = (lo.take(2, CP, CH) for _ in range(8))
                dead = Arena(big, hn_at)
                (self.att, self.btt, self.ktt, self.vt) = (dead.take(CP, P) for _ in range(4))
                self.dr, self.x1 = (dead.take(2, CP, 2 * CH) for _ in range(2))
                self.wz = self.dr
                (self.v1, self.u2, self.l2, self.u4, self.v2, self.l4) = (f.take(2, CP, CH) for _ in range(6))
                self.v4, self.l8, self.dt, self.mm, self.mt, self.m2 = (self.v1, self.u2, self.u4, self.l2, self.v2,
                                                                        self.l4)
                self.rh = self.x1.rearrange("p h c t -> p (h c t)")[:, 0:T].rearrange(
                    "p (b c t) -> p b c t", b=2, t=CH)
                self.st = f.take(NCH, HD)
                assert f.at <= yg_at
                self.y = self.ktt.rearrange("p c t -> p (c t)")
                self.yc = self.ud.rearrange("p b c t -> p (b c t)")
                self.ysq = self.gi.rearrange("p b c t -> p (b c t)")
                self.yr = self.x1.rearrange("p h c t -> p (h c t)")[:, T:2 * T]
                self.wo = big[:, C * T:C * T + PAIRS * D].rearrange("p (q d) -> p q d", d=D)
                self.n_params = 2
                (self.params_in, self.squares, self.rstd_step, self.hn_ready, self.hnT_in_psum, self.hnT_ready,
                 self.mask_step, self.masks_ready, self.vec_in, self.vec_ready, self.lora_in,
                 self.w_in, self.g2_in, self.var_read, self.projected, self.s_ps, self.s_ready, self.pair_done,
                 self.wo_in, self.mix_ps, self.mixed) = (sem("rwkv_" + n) for n in (
                    "params_in squares rstd_step hn_ready hnT_in_psum hnT_ready mask_step masks_ready vec_in "
                    "vec_ready lora_in w_in g2_in var_read projected s_ps s_ready pair_done wo_in mix_ps "
                    "mixed").split())
                (self.xx_ready, self.xw_ready, self.xa_ready, self.xg_ready, self.xk_ready, self.xr_ready,
                 self.xv_ready) = signals(sem("rwkv_lerps"), 7)
                (self.hw_in_psum, self.ha_in_psum, self.hg_in_psum) = signals(sem("rwkv_hidden_in_psum"), 3)
                (self.hw_ready, self.ha_ready, self.hg_ready) = signals(sem("rwkv_hidden"), 3)
                (self.w_ps, self.a_ps, self.k_ps, self.r_ps, self.n2_ps, self.v_ps) = signals(sem("rwkv_prepared_tensor"), 6)
                (self.sig_ready, self.a_ready, self.kraw_ready, self.kk2_ready, self.rraw_ready, self.wc_ready,
                 self.winv_ready, self.wprev_ready, self.ln_ready, self.rs_ready, self.v_ready) = signals(sem("rwkv_prepared_scalar"), 11)
                (self.pv_ready, self.cum_ready, self.cprev_ready, self.km_ready, self.k2_ready, self.n2_ready,
                 self.kt_ready, self.kkn_ready, self.at_ready, self.kka_ready, self.bt_ready, self.rt_ready,
                 self.rk_ready) = signals(sem("rwkv_prepared_vector"), 13)
                (self.vt_ps, self.att_ps, self.btt_ps, self.ktt_ps, self.bonus_ps, self.ub_ps, self.lk_ps,
                 self.l_ps, self.u2_ps, self.l2_ps, self.u4_ps, self.v2_ps, self.l4_ps, self.lv_ps, self.v4_ps,
                 self.l8_ps, self.dt_ps, self.mm_ps, self.mt_ps, self.dr_ps, self.m2_ps, self.x1_ps, self.wz_ps,
                 self.rg_ps, self.z_ps, self.g_ps, self.y_ps, self.mean_ps, self.var_ps) = signals(sem("rwkv_tensor_results"), 29)
                (self.vt_ready, self.att_ready, self.btt_ready, self.ktt_ready, self.l2_ready, self.u4_ready,
                 self.l4_ready, self.lv_ready, self.l8_ready, self.mm_ready, self.dr_ready, self.m2_ready,
                 self.g_ready, self.y_ready, self.ysq_ready, self.yln_ready, self.yrstd) = signals(sem("rwkv_scalar_results"), 17)
                (self.pt_ready, self.bv_ready, self.ud_ready, self.masked_ub, self.masked_lk, self.masked_l,
                 self.v1_ready, self.u2_ready, self.v2_ready, self.v4_ready, self.dt_ready, self.mt_ready,
                 self.x1_ready, self.wz_ready, self.gi_ready, self.rh_ready, self.yc_ready, self.yn1_ready,
                 self.yn2_ready, self.yn3_ready) = signals(sem("rwkv_vector_results"), 20)

        rw = Rwkv()
        pe_tick = sem("pe_tick")

        def pe_wait(pe, s, value):
            pe.wait_ge(s, value)
            pe.sem_inc(pe_tick)

        def pool_rwkv_masks(m, pool):
            st = Steps(m.mask_step)

            def step(ins):
                pool.wait_ge(m.mask_step, st.done(ins))

            sel = nc.gpsimd.affine_select
            step(nc.gpsimd.memset(m.keep, 1.0))
            step(nc.gpsimd.memset(m.keep.rearrange("p (c t) -> p c t", t=CH)[:, :, 0:1], 0.0))
            step(nc.gpsimd.memset(m.heads, 0.0))
            step(nc.gpsimd.memset(m.head_mean, 0.0))
            for half in range(2):
                p = slice(half * CH, half * CH + CH)
                step(nc.gpsimd.memset(m.heads[p, half * HD:half * HD + HD], 1.0))
                step(nc.gpsimd.memset(m.head_mean[p, half * HD:half * HD + HD], 1.0 / HD))
                one = ones[p, 0:CH]
                step(sel(out=m.upper[p, :], in_=one, compare_op=ALU.is_gt, fill=0.0, base=0, pattern=[[1, CH]],
                         channel_multiplier=-1))
                step(sel(out=m.upper_incl[p, :], in_=one, compare_op=ALU.is_ge, fill=0.0, base=0, pattern=[[1, CH]],
                         channel_multiplier=-1))
                step(sel(out=m.eye[p, :], in_=one, compare_op=ALU.is_equal, fill=0.0, base=0, pattern=[[-1, CH]],
                         channel_multiplier=1))
                step(sel(out=m.tmp_mask[p, :], in_=one, compare_op=ALU.is_ge, fill=0.0, base=0,
                         pattern=[[-16, CH // 16], [0, 16]], channel_multiplier=1))
                step(sel(out=m.block16[p, :], in_=m.tmp_mask[p, :], compare_op=ALU.is_ge, fill=0.0, base=15,
                         pattern=[[16, CH // 16], [0, 16]], channel_multiplier=-1))
                step(sel(out=m.u_in[p, :], in_=m.block16[p, :], compare_op=ALU.is_gt, fill=0.0, base=0,
                         pattern=[[1, CH]], channel_multiplier=-1))
                step(sel(out=m.l_in[p, :], in_=m.block16[p, :], compare_op=ALU.is_gt, fill=0.0, base=0,
                         pattern=[[-1, CH]], channel_multiplier=1))
                step(sel(out=m.l_out[p, :], in_=one, compare_op=ALU.is_gt, fill=0.0, base=0, pattern=[[-1, CH]],
                         channel_multiplier=1))
            nc.gpsimd.tensor_tensor(m.l_out, m.l_out, m.l_in, ALU.subtract).then_inc(m.masks_ready, 1)
            pool.sem_inc(m.var_read, 1)

        def sp_rwkv(m, sp):
            i = 0
            for t in range(TT):
                sp.dma_start(h[:, t, :], a["x"].rearrange("b (t p) d -> (b t) p d", p=P)[t]).then_inc(h_in[t], 16)
            sp.dma_start(m.g_row, a["norm1_g"][0:1, :].broadcast_to([P, D])).then_inc(m.params_in, 16)
            with nc.allow_non_contiguous_dma("per-channel vectors"):
                sp.dma_start(m.mu, a["rwkv_mu"][i].rearrange("n (p c) -> p n c", p=P)).then_inc(m.params_in, 16)
                for n, src in ((W0, a["rwkv_w0"][i]), (A0, a["rwkv_a0"][i]), (KK, a["rwkv_k_k"][i]),
                               (KA, a["rwkv_k_a"][i]), (RK, a["rwkv_r_k"][i].rearrange("h n -> (h n)")),
                               (LNG, a["rwkv_ln_g"][i]), (LNB, a["rwkv_ln_b"][i])):
                    sp.dma_start(m.vec[:, n, :], src.rearrange("(q p) -> p q", p=P)).then_inc(m.vec_in, 16)
            col = 0
            for src, n in (("rwkv_w1", 64), ("rwkv_a1", 64), ("rwkv_g1", P)):
                sp.dma_start(m.lora1[:, :, col:col + n],
                             a[src][i].rearrange("(p c) n -> p c n", p=P)).then_inc(m.lora_in, 16)
                col += n
            w_rkv = a["rwkv_w_rkv"][i].rearrange("n (p c) d -> p n c d", p=P)

            def load_pair(q):
                for n in range(3):
                    sp.dma_start(m.w[:, n], w_rkv[:, n, :, bass.ds(q * P, P)]).then_inc(m.w_in, 16)
                for n, src in enumerate(("rwkv_w2", "rwkv_a2")):
                    sp.dma_start(m.w_lora[0:64, n], a[src][i][:, bass.ds(q * P, P)]).then_inc(m.w_in, 16)

            def load_g2(q):
                sp.dma_start(m.w_g2, a["rwkv_g2"][i][:, bass.ds(q * P, P)]).then_inc(m.g2_in, 16)

            load_pair(0)
            load_g2(0)
            sp.wait_ge(m.projected, 1)
            load_pair(1)
            with sp.Fori(1, PAIRS - 1) as q:
                sp.wait_ge(m.g_ps.sem, m.g_ps.by(q - 1))
                load_g2(q)
                sp.wait_ge(m.projected, q + 1)
                load_pair(q + 1)
            sp.wait_ge(m.g_ps.sem, m.g_ps.by(PAIRS - 2))
            load_g2(PAIRS - 1)
            sp.wait_ge(m.projected, PAIRS)
            sp.dma_start(m.wo, a["rwkv_w_o"][i].rearrange("(q p) d -> p q d", p=P)).then_inc(m.wo_in, 16)

        def dve_rwkv_lerps(m, dve):
            dve.wait_ge(m.hnT_ready, 2 * TT)
            nc.vector.tensor_scalar(m.xx[:, :, 0:1], m.hnT[:, :, 0:1], -1.0, None, ALU.mult)
            nc.vector.tensor_tensor(m.xx[:, :, 1:T], m.hnT[:, :, 0:T - 1], m.hnT[:, :, 1:T],
                                    ALU.subtract).then_inc(m.xx_ready.now(), 1)
            dve.wait_ge(m.xx_ready.sem, m.xx_ready.by(0))
            for out_, n, s in ((m.xw, 1, m.xw_ready), (m.xa, 4, m.xa_ready), (m.xg_, 5, m.xg_ready),
                               (m.xk, 2, m.xk_ready), (m.xr, 0, m.xr_ready), (m.xv, 3, m.xv_ready)):
                if n == 3:
                    dve.wait_ge(m.hg_in_psum.sem, m.hg_in_psum.by(0))
                for c in range(C):
                    last = nc.vector.scalar_tensor_tensor(out=out_[:, c, :], in0=m.xx[:, c, :],
                                                          scalar=m.mu[:, n, c:c + 1], in1=m.hnT[:, c, :],
                                                          op0=ALU.mult, op1=ALU.add)
                last.then_inc(s.now(), 1)
            dve.wait_ge(m.vec_in, 16 * 7)
            nc.vector.tensor_scalar(m.vec[:, KA1, :], m.vec[:, KA, :], -1.0, 1.0, ALU.mult, ALU.add).then_inc(m.vec_ready, 1)

        def pe_rwkv_hidden(m, pe):
            pe.wait_ge(m.lora_in, 48)
            col = 0
            for x, rows, s, done, o in ((m.xw, 64, m.xw_ready, m.hw_in_psum, bank[2]),
                                        (m.xa, 64, m.xa_ready, m.ha_in_psum, bank[3]),
                                        (m.xg_, P, m.xg_ready, m.hg_in_psum, bank[4])):
                pe.wait_ge(s.sem, s.by(0))
                for c in range(C):
                    last = nc.tensor.matmul(o[0:rows, :], m.lora1[:, c, col:col + rows], x[:, c, :], start=(c == 0),
                                            stop=(c == C - 1))
                last.then_inc(done.now(), 1)
                col += rows

        def act_rwkv_hidden(m, act):
            act.wait_ge(m.hw_in_psum.sem, m.hw_in_psum.by(0))
            nc.scalar.activation(m.hid[0:64, 0, :], bank[2][0:64, :], ACT.Tanh).then_inc(m.hw_ready.now(), 1)
            act.wait_ge(m.ha_in_psum.sem, m.ha_in_psum.by(0))
            nc.scalar.copy(m.hid[0:64, 1, :], bank[3][0:64, :]).then_inc(m.ha_ready.now(), 1)
            act.wait_ge(m.hg_in_psum.sem, m.hg_in_psum.by(0))
            nc.scalar.activation(m.hid[:, 2, :], bank[4], ACT.Sigmoid).then_inc(m.hg_ready.now(), 1)

        def units():
            for hd in range(2):
                for cp in range(CP):
                    for par in range(2):
                        yield hd, cp, par

        def half(i):
            return slice(64 * i, 64 * i + 64)

        def two_banks(i, lo_, n):
            return psum[:, i * 512:(i + 2) * 512].rearrange("p (b n) -> p b n", b=2)[:, :, lo_:lo_ + n]

        def flat(x):
            return x.rearrange("p a b c -> p (a b c)") if len(x.shape) == 4 else x.rearrange("p a b -> p (a b)")

        def pe_prepare_low_rank(m, pe, q):
            pe_wait(pe, m.w_in, 80 * q + 80)
            nc.tensor.matmul(bank[0], m.w_lora[0:64, 0], m.hid[0:64, 0, :], start=True, stop=True).then_inc(m.w_ps.now(), 1)
            nc.tensor.matmul(bank[1], m.w_lora[0:64, 1], m.hid[0:64, 1, :], start=True, stop=True).then_inc(m.a_ps.now(), 1)

        def project(m, n, x, b, c0, c1):
            for c in range(c0, c1):
                last = nc.tensor.matmul(bank[b], m.w[:, n, c, :], x[:, c, :], start=(c == 0), stop=(c == C - 1))
            return last

        def pe_prepare_k(m, pe, q, c0, c1):
            if c0 == 0:
                pe_wait(pe, m.sig_ready.sem, m.sig_ready.by(q))
            last = project(m, 1, m.xk, 0, c0, c1)
            if c1 == C:
                last.then_inc(m.k_ps.now(), 1)

        def pe_prepare_r(m, pe, q, c0, c1):
            if c0 == 0:
                pe_wait(pe, m.a_ready.sem, m.a_ready.by(q))
            last = project(m, 0, m.xr, 1, c0, c1)
            if c1 == C:
                last.then_inc(m.r_ps.now(), 1)

        def pe_prepare_norm(m, pe, q):
            pe_wait(pe, m.kk2_ready.sem, m.kk2_ready.by(q))
            nc.tensor.matmul(bank[0], m.heads, m.kk2, start=True, stop=True).then_inc(m.n2_ps.now(), 1)

        def pe_prepare_v(m, pe, q, c0, c1):
            if c0 == 0:
                pe_wait(pe, m.rraw_ready.sem, m.rraw_ready.by(q))
            last = project(m, 2, m.xv, 1, c0, c1)
            if c1 == C:
                last.then_inc(m.v_ps.now(), 1)
                pe_wait(pe, m.v_ps.sem, m.v_ps.by(q))
                pe.sem_inc(m.projected)

        def act_prepare_sigmoids(m, act, q):
            act.wait_ge(m.pv_ready.sem, m.pv_ready.by(q))
            act.wait_ge(m.w_ps.sem, m.w_ps.by(q))
            nc.scalar.activation(m.sig, bank[0], ACT.Sigmoid, bias=m.pv[:, W0:W0 + 1]).then_inc(m.sig_ready.now(), 1)
            act.wait_ge(m.a_ps.sem, m.a_ps.by(q))
            nc.scalar.activation(m.a, bank[1], ACT.Sigmoid, bias=m.pv[:, A0:A0 + 1]).then_inc(m.a_ready.now(), 1)

        def act_prepare_k(m, act, q):
            act.wait_ge(m.k_ps.sem, m.k_ps.by(q))
            nc.scalar.copy(m.kraw, bank[0]).then_inc(m.kraw_ready.now(), 1)
            nc.scalar.activation(m.kk2, bank[0], ACT.Square, scale=m.pv[:, KK:KK + 1]).then_inc(m.kk2_ready.now(), 1)

        def act_prepare_r(m, act, q):
            act.wait_ge(m.r_ps.sem, m.r_ps.by(q))
            nc.scalar.copy(m.rraw, bank[1]).then_inc(m.rraw_ready.now(), 1)

        def act_prepare_decays(m, act, q):
            act.wait_ge(m.cum_ready.sem, m.cum_ready.by(q))
            nc.scalar.activation(m.wc, m.cum, ACT.Exp, scale=-DECAY).then_inc(m.wc_ready.now(), 1)
            nc.scalar.activation(m.winv, m.cum, ACT.Exp, scale=DECAY).then_inc(m.winv_ready.now(), 1)
            act.wait_ge(m.cprev_ready.sem, m.cprev_ready.by(q))
            nc.scalar.activation(m.wprev, m.cprev, ACT.Exp, scale=-DECAY).then_inc(m.wprev_ready.now(), 1)

        def act_prepare_norm(m, act, q):
            act.wait_ge(m.n2_ready.sem, m.n2_ready.by(q))
            nc.scalar.activation(m.rs, m.rs, ACT.Ln).then_inc(m.ln_ready.now(), 1)
            act.wait_ge(m.ln_ready.sem, m.ln_ready.by(q))
            nc.scalar.activation(m.rs, m.rs, ACT.Exp, scale=-0.5).then_inc(m.rs_ready.now(), 1)

        def act_prepare_v(m, act, q):
            act.wait_ge(m.v_ps.sem, m.v_ps.by(q))
            nc.scalar.copy(m.v, bank[1]).then_inc(m.v_ready.now(), 1)

        TTn, STT, TS = nc.vector.tensor_tensor, nc.vector.scalar_tensor_tensor, nc.vector.tensor_scalar

        def dve_wait(dve, q, *results):
            for s in results:
                dve.wait_ge(s.sem, s.by(q))

        def dve_prepare_vectors(m, dve, q):
            nc.vector.tensor_copy(m.pv, m.vec[:, :, bass.ds(q, 1)].rearrange("p n o -> p (n o)")
                                  ).then_inc(m.pv_ready.now(), 1)

        def dve_prepare_decays(m, dve, q):
            dve_wait(dve, q, m.sig_ready)
            nc.vector.tensor_tensor_scan(m.cum, m.keep, m.sig, 0.0, ALU.mult, ALU.add).then_inc(m.cum_ready.now(), 1)
            dve_wait(dve, q, m.cum_ready)
            TTn(m.cprev, m.cum, m.sig, ALU.subtract).then_inc(m.cprev_ready.now(), 1)

        def dve_prepare_k(m, dve, q):
            dve_wait(dve, q, m.a_ready, m.pv_ready)
            TS(m.km, m.a, m.pv[:, KA:KA + 1], m.pv[:, KA1:KA1 + 1], ALU.mult, ALU.add).then_inc(m.km_ready.now(), 1)
            dve_wait(dve, q, m.km_ready, m.kraw_ready)
            TTn(m.k2, m.kraw, m.km, ALU.mult).then_inc(m.k2_ready.now(), 1)

        def dve_prepare_norm(m, dve, q):
            dve_wait(dve, q, m.n2_ps)
            TS(m.rs, bank[0], 1e-24, None, ALU.max).then_inc(m.n2_ready.now(), 1)

        def dve_prepare_rest(m, dve, q):
            dve_wait(dve, q, m.k2_ready, m.winv_ready)
            TTn(m.kt, m.k2, m.winv, ALU.mult).then_inc(m.kt_ready.now(), 1)
            dve_wait(dve, q, m.rs_ready)
            STT(out=m.kkn, in0=m.kraw, scalar=m.pv[:, KK:KK + 1], in1=m.rs, op0=ALU.mult,
                op1=ALU.mult).then_inc(m.kkn_ready.now(), 1)
            dve_wait(dve, q, m.kkn_ready, m.wprev_ready)
            STT(out=m.at, in0=m.kkn, scalar=-1.0, in1=m.wprev, op0=ALU.mult, op1=ALU.mult).then_inc(m.at_ready.now(), 1)
            TTn(m.kka, m.kkn, m.a, ALU.mult).then_inc(m.kka_ready.now(), 1)
            dve_wait(dve, q, m.kka_ready)
            TTn(m.bt, m.kka, m.winv, ALU.mult).then_inc(m.bt_ready.now(), 1)
            dve_wait(dve, q, m.rraw_ready, m.wc_ready)
            TTn(m.rt, m.rraw, m.wc, ALU.mult).then_inc(m.rt_ready.now(), 1)
            dve_wait(dve, q, m.cprev_ready)
            STT(out=m.rk, in0=m.rraw, scalar=m.pv[:, RK:RK + 1], in1=m.k2, op0=ALU.mult,
                op1=ALU.mult).then_inc(m.rk_ready.now(), 1)

        def pe_rwkv_pair(m, pe, q, more):
            nq = q + 1

            def wait(*results):
                for s in results:
                    pe_wait(pe, s.sem, s.by(q))

            def mix_first(nh, c0, c1):
                for c in range(c0, c1):
                    mix_add(m.yg, m.wo[:, c], 0, c, nh)

            def flip(src, b, done):
                for i in range(CP):
                    last = nc.tensor.transpose(bank[b][:, i * P:(i + 1) * P], src[:, i * P:(i + 1) * P], ident[:])
                last.then_inc(done.now(), 1)

            wait(m.v_ready, m.rk_ready)
            pe_wait(pe, m.var_read, q + 1)
            flip(m.v, 2, m.vt_ps)
            flip(m.at, 3, m.att_ps)
            flip(m.bt, 4, m.btt_ps)
            flip(m.kt, 5, m.ktt_ps)
            nc.tensor.matmul(bank[7], m.heads, m.rk, start=True, stop=True).then_inc(m.bonus_ps.now(), 1)
            if more:
                pe_prepare_low_rank(m, pe, nq)

            def product(lhs, rhs, b, lo_):
                for hd, cp, par in units():
                    c = slice((2 * cp + par) * CH, (2 * cp + par + 1) * CH)
                    last = nc.tensor.matmul(bank[b + hd][half(par), lo_ + cp * CH:lo_ + (cp + 1) * CH],
                                            lhs[half(hd), c], rhs[half(hd), c], start=True, stop=True)
                return last

            wait(m.vt_ready, m.att_ready)
            product(m.bt, m.at, 2, 0)
            product(m.bt, m.rt, 2, 256).then_inc(m.ub_ps.now(), 1)
            wait(m.btt_ready, m.ktt_ready)
            product(m.kt, m.at, 4, 0)
            product(m.kt, m.rt, 4, 256).then_inc(m.lk_ps.now(), 1)
            wait(m.bv_ready)
            product(m.at, m.bt, 6, 0).then_inc(m.l_ps.now(), 1)
            if more:
                pe_prepare_k(m, pe, nq, 0, 4)

            def blocks(lhs, rhs, b, n=CH, lo_=0):
                for hd, cp, par in units():
                    o = bank[b] if n == CH else bank[b + hd]
                    at = (hd * CP + cp) * CH if n == CH else cp * 2 * CH + lo_
                    w = rhs(hd, cp, par)
                    last = nc.tensor.matmul(o[half(par), at:at + w.shape[1]], lhs(hd, cp, par), w, start=True, stop=True)
                return last

            def mat(x):
                return lambda hd, cp, par: x[half(par), hd, cp, :]

            def tok(x):
                return lambda hd, cp, par: x[half(par), cp, hd * HD:(hd + 1) * HD]

            wait(m.masked_l)
            blocks(mat(m.ld), mat(m.ud), 2).then_inc(m.u2_ps.now(), 1)
            blocks(mat(m.ud), mat(m.ld), 3).then_inc(m.l2_ps.now(), 1)
            if more:
                pe_prepare_k(m, pe, nq, 4, C)
            wait(m.l2_ready, m.u2_ready, m.v1_ready)
            blocks(mat(m.l2), mat(m.u2), 4).then_inc(m.u4_ps.now(), 1)
            blocks(mat(m.l2), mat(m.v1), 5).then_inc(m.v2_ps.now(), 1)
            blocks(mat(m.u2), mat(m.l2), 6).then_inc(m.l4_ps.now(), 1)
            blocks(mat(m.lak), tok(m.vt), 7).then_inc(m.lv_ps.now(), 1)
            if more:
                pe_prepare_r(m, pe, nq, 0, 2)
            else:
                pe.wait_ge(m.pair_done, PAIRS - 1)
                pe.wait_ge(m.wo_in, 16)
                mix_first(1, 0, 2)
            wait(m.l4_ready, m.v2_ready)
            blocks(mat(m.l4), mat(m.v2), 2).then_inc(m.v4_ps.now(), 1)
            wait(m.u4_ready)
            blocks(mat(m.u4), mat(m.l4), 3).then_inc(m.l8_ps.now(), 1)
            if more:
                pe_prepare_r(m, pe, nq, 2, 4)
            else:
                mix_first(1, 2, 3)
            wait(m.l8_ready, m.v4_ready)
            blocks(mat(m.l8), mat(m.v4), 4).then_inc(m.dt_ps.now(), 1)
            if more:
                pe_prepare_r(m, pe, nq, 4, 6)
            else:
                mix_first(1, 3, 4)
            wait(m.dt_ready)
            blocks(mat(m.lo_), mat(m.dt), 5).then_inc(m.mm_ps.now(), 1)
            blocks(mat(m.dt), mat(m.lo_), 6).then_inc(m.mt_ps.now(), 1)
            wait(m.lv_ready)
            blocks(mat(m.dt), tok(m.att), 2, n=2 * CH)
            blocks(mat(m.dt), mat(m.lv), 2, n=2 * CH, lo_=CH).then_inc(m.dr_ps.now(), 1)
            wait(m.mm_ready, m.mt_ready)
            blocks(mat(m.mt), mat(m.mm), 7).then_inc(m.m2_ps.now(), 1)
            if more:
                pe_prepare_r(m, pe, nq, 6, C)
            else:
                mix_first(1, 4, 5)
            wait(m.dr_ready)
            blocks(mat(m.mm), mat(m.dr), 4, n=2 * CH).then_inc(m.x1_ps.now(), 1)
            if more:
                pe_prepare_norm(m, pe, nq)
                pe_prepare_v(m, pe, nq, 0, 2)
            else:
                mix_first(1, 5, 6)
            wait(m.m2_ready, m.x1_ready)
            blocks(mat(m.m2), mat(m.x1), 6, n=2 * CH).then_inc(m.wz_ps.now(), 1)
            if more:
                pe_prepare_v(m, pe, nq, 2, 4)
            else:
                mix_first(1, 6, PAIRS - 1)
            wait(m.wz_ready)

            for hd, cp, par in units():
                w = m.wz[half(par), hd, cp, 0:CH]
                nc.tensor.matmul(bank[2 + par][half(hd), cp * CH:(cp + 1) * CH], w, m.mrb[half(par), hd, cp, :],
                                 start=True, stop=True)
                last = nc.tensor.matmul(bank[2 + par][half(hd), 256 + cp * CH:256 + (cp + 1) * CH], w,
                                        m.btt[half(par), cp, hd * HD:(hd + 1) * HD], start=True, stop=True)
            last.then_inc(m.rg_ps.now(), 1)
            for hd, cp, par in units():
                z = m.wz[half(par), hd, cp, CH:2 * CH]
                v = m.vt[half(par), cp, hd * HD:(hd + 1) * HD]
                o = bank[4 + par][half(hd), cp * CH:(cp + 1) * CH]
                nc.tensor.matmul(o, m.btt[half(par), cp, hd * HD:(hd + 1) * HD], z, start=(cp == 0), stop=False,
                                 skip_group_check=True)
                nc.tensor.matmul(o, m.ktt[half(par), cp, hd * HD:(hd + 1) * HD], v, start=False, stop=False,
                                 skip_group_check=True)
                o = bank[6 + par][half(hd), cp * CH:(cp + 1) * CH]
                nc.tensor.matmul(o, z, m.mrb[half(par), hd, cp, :], start=(cp == 0), stop=False, skip_group_check=True)
                last = nc.tensor.matmul(o, v, m.mrk[half(par), hd, cp, :], start=False, stop=False,
                                        skip_group_check=True)
            last.then_inc(m.z_ps.now(), 1)
            if more:
                pe_wait(pe, m.n2_ready.sem, m.n2_ready.by(nq))
            pe_wait(pe, m.g2_in, 16 * q + 16)
            nc.tensor.matmul(bank[0], m.w_g2, m.hid[:, 2, :], start=True, stop=True).then_inc(m.g_ps.now(), 1)
            wait(m.gi_ready, m.rh_ready)
            wait(m.z_ps)
            for c in range(NCH):
                cp, par = c // 2, c % 2
                pe_wait(pe, m.s_ready, NCH * q + c + 1)
                if c + 1 < NCH:
                    for hd in range(2):
                        last = nc.tensor.matmul(bank[4 + par][half(hd), cp * CH:(cp + 1) * CH],
                                                m.gi[half(hd), par, cp, :], m.st[half(hd), c, :], start=False, stop=True,
                                                skip_group_check=True)
                    last.then_inc(m.s_ps, 1)
                for hd in range(2):
                    last = nc.tensor.matmul(bank[6 + par][half(hd), cp * CH:(cp + 1) * CH], m.st[half(hd), c, :],
                                            m.rh[half(hd), par, cp, :], start=False, stop=True, skip_group_check=True)
                if c == NCH - 1:
                    last.then_inc(m.y_ps.now(), 1)
                if more and c < 4:
                    pe_prepare_v(m, pe, nq, 4 + c, 5 + c)
                if not more and c == 0:
                    wait(m.g_ready)
                if not more and c < PAIRS - 1:
                    mix_first(0, c, c + 1)
            wait(m.y_ready)
            nc.tensor.matmul(bank[2], m.head_mean, m.y, start=True, stop=True).then_inc(m.mean_ps.now(), 1)
            wait(m.ysq_ready)
            nc.tensor.matmul(bank[3], m.head_mean, m.ysq, start=True, stop=True).then_inc(m.var_ps.now(), 1)

        def act_rwkv_pair(m, act, q, more):
            nq = q + 1

            def take(s, dst, src, done):
                act.wait_ge(s.sem, s.by(q))
                nc.scalar.copy(dst, src).then_inc(done.now(), 1)

            take(m.vt_ps, flat(m.vt), bank[2], m.vt_ready)
            take(m.att_ps, flat(m.att), bank[3], m.att_ready)
            take(m.btt_ps, flat(m.btt), bank[4], m.btt_ready)
            take(m.ktt_ps, flat(m.ktt), bank[5], m.ktt_ready)
            if more:
                act.wait_ge(m.ud_ready.sem, m.ud_ready.by(q))
                act_prepare_sigmoids(m, act, nq)
            take(m.l2_ps, flat(m.l2), bank[3], m.l2_ready)
            if more:
                act_prepare_k(m, act, nq)
            take(m.u4_ps, flat(m.u4), bank[4], m.u4_ready)
            take(m.l4_ps, flat(m.l4), bank[6], m.l4_ready)
            take(m.lv_ps, flat(m.lv), bank[7], m.lv_ready)
            take(m.l8_ps, flat(m.l8), bank[3], m.l8_ready)
            take(m.mm_ps, flat(m.mm), bank[5], m.mm_ready)
            take(m.dr_ps, flat(m.dr), psum[:, 2 * 512:4 * 512], m.dr_ready)
            take(m.m2_ps, flat(m.m2), bank[7], m.m2_ready)
            if more:
                act_prepare_r(m, act, nq)
                act_prepare_decays(m, act, nq)
                act_prepare_norm(m, act, nq)
            take(m.g_ps, m.g, bank[0], m.g_ready)
            for c in range(NCH - 1):
                cp, par = c // 2, c % 2
                act.wait_ge(m.s_ps, (NCH - 1) * q + c + 1)
                nc.scalar.activation(m.st[:, c + 1, :], bank[4 + par][:, cp * CH:(cp + 1) * CH], ACT.Copy,
                                     scale=m.wend[:, c:c + 1]).then_inc(m.s_ready, 1)
            act.wait_ge(m.y_ps.sem, m.y_ps.by(q))
            nc.scalar.copy(m.y.rearrange("p (c b t) -> p b c t", b=2, t=CH),
                           two_banks(6, 0, 256).rearrange("p b (c t) -> p b c t", t=CH)).then_inc(m.y_ready.now(), 1)
            if more:
                act_prepare_v(m, act, nq)
            act.wait_ge(m.yc_ready.sem, m.yc_ready.by(q))
            nc.scalar.activation(m.ysq, m.yc, ACT.Square).then_inc(m.ysq_ready.now(), 1)
            act.wait_ge(m.var_read, q + 2)
            nc.scalar.activation(m.yr, m.yr, ACT.Ln).then_inc(m.yln_ready.now(), 1)
            act.wait_ge(m.yln_ready.sem, m.yln_ready.by(q))
            nc.scalar.activation(m.yr, m.yr, ACT.Exp, scale=-0.5).then_inc(m.yrstd.now(), 1)

        def dve_rwkv_pair(m, dve, q, more):
            nq = q + 1

            def w(*results):
                dve_wait(dve, q, *results)

            nc.vector.tensor_copy(m.pt, m.vec[:, LNG:LNB + 1, bass.ds(q, 1)].rearrange("p n o -> p (n o)"))
            w(m.wc_ready)
            nc.vector.tensor_copy(m.wend, m.wc.rearrange("p (c t) -> p c t", t=CH)[:, :, CH - 1]
                                  ).then_inc(m.pt_ready.now(), 1)
            w(m.bonus_ps, m.v_ready)
            TTn(m.bv, bank[7], m.v, ALU.mult).then_inc(m.bv_ready.now(), 1)
            if more:
                dve_prepare_vectors(m, dve, nq)

            def mask(x):
                return x.unsqueeze(1).unsqueeze(1).broadcast_to([P, 2, CP, CH])

            def four(x):
                return x.rearrange("p b (c t) -> p b c t", t=CH)

            w(m.ub_ps)
            TTn(m.ud, four(two_banks(2, 0, 256)), mask(m.u_in), ALU.mult).then_inc(m.ud_ready.now(), 1)
            TTn(m.mrb, four(two_banks(2, 256, 256)), mask(m.upper_incl), ALU.mult).then_inc(m.masked_ub.now(), 1)
            w(m.lk_ps)
            TTn(m.lak, four(two_banks(4, 0, 256)), mask(m.upper), ALU.mult)
            TTn(m.mrk, four(two_banks(4, 256, 256)), mask(m.upper_incl), ALU.mult).then_inc(m.masked_lk.now(), 1)
            w(m.l_ps)
            lb = four(two_banks(6, 0, 256))
            TTn(m.ld, lb, mask(m.l_in), ALU.mult)
            TTn(m.lo_, lb, mask(m.l_out), ALU.mult).then_inc(m.masked_l.now(), 1)
            w(m.ud_ready)
            TTn(m.v1, m.ud, mask(m.eye), ALU.add).then_inc(m.v1_ready.now(), 1)
            w(m.u2_ps)
            nc.vector.tensor_copy(flat(m.u2), bank[2]).then_inc(m.u2_ready.now(), 1)
            if more:
                dve_prepare_decays(m, dve, nq)
            w(m.v1_ready, m.v2_ps)
            TTn(flat(m.v2), bank[5], flat(m.v1), ALU.add).then_inc(m.v2_ready.now(), 1)
            w(m.v2_ready, m.v4_ps)
            TTn(flat(m.v4), bank[2], flat(m.v2), ALU.add).then_inc(m.v4_ready.now(), 1)
            if more:
                dve_prepare_k(m, dve, nq)
            w(m.v4_ready, m.dt_ps)
            TTn(flat(m.dt), bank[4], flat(m.v4), ALU.add).then_inc(m.dt_ready.now(), 1)
            w(m.mt_ps)
            nc.vector.tensor_copy(flat(m.mt), bank[6]).then_inc(m.mt_ready.now(), 1)
            w(m.x1_ps, m.dr_ready)
            TTn(flat(m.x1), psum[:, 4 * 512:6 * 512], flat(m.dr), ALU.add).then_inc(m.x1_ready.now(), 1)
            if more:
                dve_prepare_norm(m, dve, nq)
            w(m.wz_ps, m.x1_ready)
            TTn(flat(m.wz), psum[:, 6 * 512:8 * 512], flat(m.x1), ALU.add).then_inc(m.wz_ready.now(), 1)
            w(m.rg_ps, m.wz_ready)
            TTn(m.gi, four(two_banks(2, 256, 256)), mask(m.eye), ALU.add).then_inc(m.gi_ready.now(), 1)
            TTn(m.rh, four(two_banks(2, 0, 256)), m.rt.rearrange("p (c b t) -> p b c t", b=2, t=CH),
                ALU.add).then_inc(m.rh_ready.now(), 1)
            nc.vector.memset(m.st[:, 0, :], 0.0).then_inc(m.s_ready, 1)
            if more:
                w(m.rh_ready)
                dve_prepare_rest(m, dve, nq)
            w(m.y_ready, m.mean_ps)
            TTn(m.yc, m.y, bank[2], ALU.subtract).then_inc(m.yc_ready.now(), 1)
            w(m.var_ps)
            TS(m.yr, bank[3], 1.0, LNX_EPS, ALU.mult, ALU.add).then_inc(m.var_read, 1)
            w(m.yrstd)
            TTn(m.yc, m.yc, m.yr, ALU.mult).then_inc(m.yn1_ready.now(), 1)
            w(m.yn1_ready)
            TS(m.yc, m.yc, m.pt[:, 0:1], m.pt[:, 1:2], ALU.mult, ALU.add).then_inc(m.yn2_ready.now(), 1)
            w(m.yn2_ready)
            TTn(m.yc, m.yc, m.bv, ALU.add).then_inc(m.yn3_ready.now(), 1)
            w(m.yn3_ready)
            TTn(m.yg[:, bass.ds(q, 1), :].rearrange("p o t -> p (o t)"), m.yc, m.g, ALU.mult).then_inc(m.pair_done, 1)
            dve.wait_ge(m.pair_done, q + 1)

        def mix_add(src, wts, t, c, nh):
            return nc.tensor.matmul(bank[4 * (t % 2) + nh], src[:, c, t * P:(t + 1) * P],
                                    wts[:, nh * 512:(nh + 1) * 512], start=(c == 0), stop=(c == C - 1))

        def pe_mix_out(m, pe, src, wts, src_ready, after, begun=0):

            def add(t, c):
                for nh in range(2):
                    last = mix_add(src, wts[c], t, c, nh)
                if c == C - 1:
                    last.then_inc(m.mix_ps, 1)

            for c in range(C):
                pe.wait_ge(src_ready, c + 1)
                if c >= begun:
                    add(0, c)
                add(1, c)
            for t in range(2, TT):
                pe.wait_ge(m.mixed, t - 1)
                for c in range(C):
                    add(t, c)
                if t == 2:
                    pe_norm_columns(after, pe, 0)
                pe_norm_columns(after, pe, t - 1)
            pe_norm_columns(after, pe, TT - 1)

        def dve_mix(m, dve, t):
            dve.wait_ge(m.mix_ps, t + 1)
            b = 4 * (t % 2)
            nc.vector.tensor_tensor(h[:, t, :], psum[:, b * 512:(b + 2) * 512], h[:, t, :], ALU.add).then_inc(m.mixed, 1)

        def dve_mixed(m, dve, t):
            if t != 1:
                dve_mix(m, dve, t)
            if t == 0:
                dve_mix(m, dve, 1)
            dve.wait_ge(m.mixed, t + 1)

        def pe_rwkv(m, pe):
            pe_norm(m, pe)
            pe_rwkv_hidden(m, pe)
            pe.wait_ge(m.masks_ready, 1)
            pe.wait_ge(m.hg_ready.sem, m.hg_ready.by(0))
            pe.wait_ge(m.xk_ready.sem, m.xk_ready.by(0))
            pe_prepare_low_rank(m, pe, 0)
            pe_prepare_k(m, pe, 0, 0, C)
            pe.wait_ge(m.xr_ready.sem, m.xr_ready.by(0))
            pe_prepare_r(m, pe, 0, 0, C)
            pe_prepare_norm(m, pe, 0)
            pe.wait_ge(m.xv_ready.sem, m.xv_ready.by(0))
            pe_prepare_v(m, pe, 0, 0, C)
            with pe.Fori(0, PAIRS - 1) as q:
                pe_rwkv_pair(m, pe, q, True)
            pe_rwkv_pair(m, pe, PAIRS - 1, False)
            pe_mix_out(m, pe, m.yg, [m.wo[:, c] for c in range(C)], m.pair_done, moe[0], begun=PAIRS - 1)

        def act_rwkv(m, act):
            act_norm(m, act, lambda t: act.wait_ge(h_in[t], 16), ALL_TILES)
            act_rwkv_hidden(m, act)
            act_prepare_sigmoids(m, act, 0)
            act_prepare_k(m, act, 0)
            act_prepare_r(m, act, 0)
            act_prepare_decays(m, act, 0)
            act_prepare_norm(m, act, 0)
            act_prepare_v(m, act, 0)
            with act.Fori(0, PAIRS - 1) as q:
                act_rwkv_pair(m, act, q, True)
            act_rwkv_pair(m, act, PAIRS - 1, False)

        def dve_rwkv(m, dve):
            dve_norm(m, dve, lambda t: dve.wait_ge(h_in[t], 16), ALL_TILES)
            dve_rwkv_lerps(m, dve)
            dve.wait_ge(m.masks_ready, 1)
            dve.wait_ge(m.vec_ready, 1)
            dve_prepare_vectors(m, dve, 0)
            dve_prepare_decays(m, dve, 0)
            dve_prepare_k(m, dve, 0)
            dve_prepare_norm(m, dve, 0)
            dve_prepare_rest(m, dve, 0)
            with dve.Fori(0, PAIRS - 1) as q:
                dve_rwkv_pair(m, dve, q, True)
            dve_rwkv_pair(m, dve, PAIRS - 1, False)

        TAPS = a["conv_w_dw"].shape[1]
        PAD = TAPS - 1
        PE_TAPS = 5
        DVE_TAPS = TAPS - PE_TAPS
        B1A, B1B, BDW, CLG, CLB = range(5)
        CONV_RING = RING // 2

        def top_of_ring(places):
            return places * (2 * C * F_EXP + 2 * D)

        class Conv:
            def __init__(self):
                m = Arena(big, top_of_ring(CONV_RING))
                self.layer = 1
                self.n_params = 1
                self.w2 = m.take(C, D)
                self.w1 = [m.take(C, 2, P) for _ in range(2)]
                m.at = max(m.at, stage_base)
                self.hn = [m.take(D) for _ in range(2)]
                self.g_row = m.take(D)
                self.ss, self.rstd = m.take(TT), m.take(TT)
                self.vec = m.take(5, C)
                self.taps = m.take(C, TAPS)
                self.mean_of = m.take(P)
                self.hnT = m.take(C, T)
                assert m.at <= moe[0].dead_at_end
                self.u = [m.take(PAD + T) for _ in range(2)]
                self.sig = [m.take(T) for _ in range(2)]
                self.odd = [m.take(T) for _ in range(2)]
                self.diag = [m.take(PE_TAPS, P) for _ in range(2)]
                self.mean = m.take(T)
                self.rs = m.take(T)
                m.at = max(m.at, moe[1].dead_at_end)
                self.co = m.take(C, T)
                self.sq = [self.u[b][:, 0:T] for b in range(2)]
                (self.params_in, self.squares, self.rstd_step, self.hn_ready, self.hnT_in_psum, self.hnT_ready,
                 self.vec_in, self.w1_in0, self.w1_in1, self.w2_in, self.pads_ready, self.up_ps, self.sig_ready,
                 self.gated, self.tap, self.co_ready, self.mean_ps, self.centred, self.sq_ready, self.var_ps,
                 self.rs_step, self.normed_, self.act_ready, self.mix_ps, self.mixed, self.bias_in, self.biased,
                 self.mean_of_ready, self.diag_ready, self.taps_ps) = (sem("conv_" + n) for n in (
                    "params_in squares rstd_step hn_ready hnT_in_psum hnT_ready vec_in w1_in0 w1_in1 "
                    "w2_in pads_ready up_ps sig_ready gated tap co_ready mean_ps centred sq_ready "
                    "var_ps rs_step normed_ act_ready mix_ps mixed bias_in biased mean_of_ready "
                    "diag_ready taps_ps").split())

        cv = Conv()

        def sp_conv(m, sp, memory_free):
            memory_free()
            before = moe[0]
            sp.dma_start(m.g_row, a["norm1_g"][1:2, :].broadcast_to([P, D])).then_inc(m.params_in, 16)
            w1 = a["conv_w_pw1"][0].rearrange("(p c) (u q n) -> p c u q n", p=P, u=2, n=P)

            def load_w1(q, b):
                for u in range(2):
                    src = w1[:, :, u, q, :] if isinstance(q, int) else \
                        w1[:, :, u, bass.ds(q, 1), :].rearrange("p c o n -> p c (o n)")
                    sp.dma_start(m.w1[b][:, :, u, :], src).then_inc(m.w1_in0 if b == 0 else m.w1_in1, 16)

            sp.wait_ge(before.h_step, 2)
            for b in range(2):
                load_w1(b, b)
            with nc.allow_non_contiguous_dma("per-channel vectors"):
                for n, src in ((B1A, a["conv_b_pw1"][0][0:D]), (B1B, a["conv_b_pw1"][0][D:2 * D]),
                               (BDW, a["conv_b_dw"][0]), (CLG, a["conv_ln_g"][0]), (CLB, a["conv_ln_b"][0])):
                    sp.dma_start(m.vec[:, n, :], src.rearrange("(q p) -> p q", p=P)).then_inc(m.vec_in, 16)
                for q in range(C):
                    sp.dma_start(m.taps[:, q, :],
                                 a["conv_w_dw"][0][:, q * P:(q + 1) * P].rearrange("k p -> p k")).then_inc(m.vec_in, 16)
            sp.wait_ge(before.h_step, 2 * TT)
            sp.dma_start(m.w2, a["conv_w_pw2"][0].rearrange("(q p) d -> p q d", p=P)).then_inc(m.w2_in, 16)
            with sp.Fori(1, C // 2) as g:
                for b in range(2):
                    sp.wait_ge(m.up_ps, 2 * g + (b - 1))
                    load_w1(2 * g + b, b)
            sp.wait_ge(m.hn_ready, TT)
            sp.dma_start(m.g_row, a["conv_b_pw2"][0:1, :].broadcast_to([P, D])).then_inc(m.bias_in, 16)

        def pool_conv(m, pool, memory_free):
            memory_free()
            nc.gpsimd.memset(m.u[0][:, 0:PAD], 0.0).then_inc(m.pads_ready, 1)
            nc.gpsimd.memset(m.u[1][:, 0:PAD], 0.0).then_inc(m.pads_ready, 1)
            nc.gpsimd.memset(m.mean_of, 1.0 / D).then_inc(m.mean_of_ready, 1)
            pool.sem_inc(m.gated, FREE2)
            pool.sem_inc(m.co_ready, FREE2)

        def pe_conv(m, pe):
            pe_norm(m, pe)
            pe.wait_ge(m.hnT_ready, 2 * TT)

            def up(g, b):
                q = 2 * g + b
                pe_wait(pe, m.w1_in0 if b == 0 else m.w1_in1, 32 * g + 32)
                pe_wait(pe, m.gated, q + 1)
                for u in range(2):
                    for c in range(C):
                        last = nc.tensor.matmul(bank[2 + 2 * b + u], m.w1[b][:, c, u, :], m.hnT[:, c, :],
                                                start=(c == 0), stop=(c == C - 1))
                last.then_inc(m.up_ps, 1)

            def last_taps(q, b):
                pe_wait(pe, m.gated, FREE2 + q + 1)
                pe_wait(pe, m.diag_ready, q + 1)
                pe_wait(pe, m.co_ready, q + 1)
                for k in range(PE_TAPS):
                    at = DVE_TAPS + k
                    last = nc.tensor.matmul(bank[6 + b], m.diag[b][:, k, :], m.u[b][:, at:at + T], start=(k == 0),
                                            stop=(k == PE_TAPS - 1))
                last.then_inc(m.taps_ps, 1)

            up(0, 0)
            with pe.Fori(0, C // 2 - 1) as g:
                up(g, 1)
                last_taps(2 * g, 0)
                up(g + 1, 0)
                last_taps(2 * g + 1, 1)
            up(C // 2 - 1, 1)
            last_taps(C - 2, 0)
            last_taps(C - 1, 1)
            pe.wait_ge(m.mean_of_ready, 1)
            for q in range(C):
                pe.wait_ge(m.co_ready, FREE2 + q + 1)
                last = nc.tensor.matmul(bank[0], m.mean_of, m.co[:, q, :], start=(q == 0), stop=(q == C - 1))
            last.then_inc(m.mean_ps, 1)
            for q in range(C):
                pe.wait_ge(m.sq_ready, q + 1)
                nc.tensor.matmul(bank[1], m.mean_of, m.sq[q % 2], start=(q == 0),
                                 stop=(q == C - 1)).then_inc(m.var_ps, 1)
            pe.wait_ge(m.rs_step, 1)
            pe.wait_ge(m.w2_in, 16)
            pe_mix_out(m, pe, m.co, [m.w2[:, c] for c in range(C)], m.act_ready, moe[1])

        def act_conv(m, act, tile_ready):
            act_norm(m, act, tile_ready, LAST_ALONE)
            act.wait_ge(m.vec_in, 16 * (5 + C))
            with act.Fori(0, C // 2) as g:
                for b in range(2):
                    q = 2 * g + b
                    act.wait_ge(m.up_ps, q + 1)
                    act.wait_ge(m.gated, q + 1)
                    nc.scalar.activation(m.sig[b], bank[3 + 2 * b], ACT.Sigmoid,
                                         bias=m.vec[:, B1B, bass.ds(q, 1)]).then_inc(m.sig_ready, 1)
                    act.wait_ge(m.co_ready, q + 1)
                    for k in range(PE_TAPS):
                        w = m.taps[:, bass.ds(q, 1), DVE_TAPS + k:DVE_TAPS + k + 1].rearrange("p o k -> p (o k)")
                        last = nc.scalar.activation(m.diag[b][:, k, :], ident[:], ACT.Copy, scale=w)
                    last.then_inc(m.diag_ready, 1)
            for q in range(C):
                act.wait_ge(m.centred, q + 1)
                if q >= 2:
                    act.wait_ge(m.var_ps, q - 1)
                nc.scalar.activation(m.sq[q % 2], m.co[:, q, :], ACT.Square).then_inc(m.sq_ready, 1)
            act.wait_ge(m.rs_step, 1)
            nc.scalar.activation(m.rs, m.rs, ACT.Ln).then_inc(m.rs_step, 1)
            act.wait_ge(m.rs_step, 2)
            nc.scalar.activation(m.rs, m.rs, ACT.Exp, scale=-0.5).then_inc(m.rs_step, 1)
            for q in range(C):
                act.wait_ge(m.normed_, q + 1)
                nc.scalar.activation(m.co[:, q, :], m.co[:, q, :], ACT.Silu, bias=m.vec[:, CLB, q:q + 1],
                                     scale=m.vec[:, CLG, q:q + 1]).then_inc(m.act_ready, 1)

        def dve_conv(m, dve, tile_ready):
            dve_norm(m, dve, tile_ready, LAST_ALONE)
            dve.wait_ge(m.vec_in, 16 * (5 + C))
            dve.wait_ge(m.pads_ready, 2)

            def gate(q, b):
                dve.wait_ge(m.sig_ready, q + 1)
                dve.wait_ge(m.co_ready, q + 1)
                nc.vector.scalar_tensor_tensor(out=m.u[b][:, PAD:], in0=bank[2 + 2 * b],
                                               scalar=m.vec[:, B1A, bass.ds(q, 1)], in1=m.sig[b], op0=ALU.add,
                                               op1=ALU.mult).then_inc(m.gated, 1)

            def convolve(q, b, more):
                dve.wait_ge(m.gated, FREE2 + q + 1)
                even = m.co[:, bass.ds(q, 1), :].rearrange("p o t -> p (o t)")
                w = m.taps[:, bass.ds(q, 1), :].rearrange("p o k -> p (o k)")
                nc.vector.tensor_scalar(even, m.u[b][:, 0:T], w[:, 0:1], m.vec[:, BDW, bass.ds(q, 1)], ALU.mult,
                                        ALU.add).then_inc(m.tap, 1)
                dve.wait_ge(m.taps_ps, q + 1)
                dve.wait_ge(m.co_ready, q + 1)
                nc.vector.scalar_tensor_tensor(out=m.odd[b], in0=m.u[b][:, 1:1 + T], scalar=w[:, 1:2], in1=bank[6 + b],
                                               op0=ALU.mult, op1=ALU.add).then_inc(m.tap, 1)
                for k in range(2, DVE_TAPS):
                    if more and k == DVE_TAPS // 2:
                        gate(q + 1, 1 - b)
                    o = even if k % 2 == 0 else m.odd[b]
                    dve.wait_ge(m.tap, DVE_TAPS * q + k - 1)
                    nc.vector.scalar_tensor_tensor(out=o, in0=m.u[b][:, k:k + T], scalar=w[:, k:k + 1], in1=o,
                                                   op0=ALU.mult, op1=ALU.add).then_inc(m.tap, 1)
                dve.wait_ge(m.tap, DVE_TAPS * q + DVE_TAPS)
                nc.vector.tensor_tensor(even, even, m.odd[b], ALU.add).then_inc(m.co_ready, 1)

            gate(0, 0)
            with dve.Fori(0, C // 2 - 1) as g:
                convolve(2 * g, 0, True)
                convolve(2 * g + 1, 1, True)
            convolve(C - 2, 0, True)
            convolve(C - 1, 1, False)
            dve.wait_ge(m.mean_ps, 1)
            nc.vector.tensor_copy(m.mean, bank[0]).then_inc(m.mean_of_ready, 1)
            dve.wait_ge(m.mean_of_ready, 2)
            for q in range(C):
                nc.vector.tensor_tensor(m.co[:, q, :], m.co[:, q, :], m.mean, ALU.subtract).then_inc(m.centred, 1)
            dve.wait_ge(m.bias_in, 16)
            for t in range(TT):
                nc.vector.tensor_tensor(h[:, t, :], h[:, t, :], m.g_row, ALU.add).then_inc(m.biased, 1)
            dve.wait_ge(m.var_ps, C)
            nc.vector.tensor_scalar(m.rs, bank[1], LN_EPS, None, ALU.add).then_inc(m.rs_step, 1)
            dve.wait_ge(m.rs_step, 3)
            for q in range(C):
                nc.vector.tensor_tensor(m.co[:, q, :], m.co[:, q, :], m.rs, ALU.mult).then_inc(m.normed_, 1)
            dve.wait_ge(m.biased, TT)

        block = ctx.enter_context(nc.Block())

        class Final:

            def __init__(self):
                m = Arena(big)
                self.n_params = 1
                self.hn = [m.take(D) for _ in range(TT)]
                self.g_row = m.take(D)
                self.ss, self.rstd = m.take(TT), m.take(TT)
                (self.params_in, self.squares, self.rstd_step, self.hn_ready, self.stored) = (sem("final_" + n) for n in (
                    "params_in squares rstd_step hn_ready stored").split())

        fin = Final()

        @block.sync
        def _(sp):
            sp_rwkv(rw, sp)

            def pairs_done():
                sp.wait_ge(rw.pair_done, PAIRS)
                sp_moe_params(moe[0], sp)

            rounds = sp_moe_weights(moe[0], sp, ((2, lambda: None), (3, pairs_done),
                                                 (0, lambda: sp.wait_ge(rw.mixed, TT)), (1, lambda: None)))
            sp_conv(cv, sp, lambda: sp.wait_ge(moe[0].down_done, FREE2 + N_EXP * rounds))

            def conv_done():
                sp.wait_ge(cv.act_ready, C)
                sp_moe_params(moe[1], sp)
                sp.wait_ge(cv.mixed, TT)

            rounds = sp_moe_weights(moe[1], sp, ((0, lambda: None), (1, lambda: None), (2, conv_done),
                                                 (3, lambda: None)))
            sp.wait_ge(moe[1].down_done, FREE2 + N_EXP * rounds)
            sp.dma_start(fin.g_row, a["final_g"].rearrange("(o d) -> o d", o=1).broadcast_to([P, D])
                         ).then_inc(fin.params_in, 16)
            out_tiles = out.rearrange("b (t p) d -> (b t) p d", p=P)
            for t in range(TT):
                sp.wait_ge(fin.hn_ready, t + 1)
                sp.dma_start(out_tiles[t], fin.hn[t]).then_inc(fin.stored, 16)
            sp.wait_ge(fin.stored, 16 * TT)

        @block.gpsimd
        def _(pool):
            pool_constants()
            pool.wait_ge(consts_ready, 1)
            pool_rwkv_masks(rw, pool)
            pool_moe(moe[0], pool)
            pool_conv(cv, pool, lambda: pool.wait_ge(moe[0].h_step, 2 * TT))
            pool_moe(moe[1], pool)

        @block.scalar
        def _(act):
            act_rwkv(rw, act)
            for m, mixer in ((moe[0], rw), (moe[1], cv)):
                act_norm(m, act, lambda t: act.wait_ge(mixer.mixed, t + 1), EACH_TILE)
                act_route(m, act)
                rounds = act_moe(m, act)
                tile_ready = act_load_back(m, act, rounds)
                if m is moe[0]:
                    act_conv(cv, act, tile_ready)
            for g in range(len(LAST_ALONE)):
                act_norm_rows(fin, act, tile_ready, LAST_ALONE, g)

        @block.vector
        def _(dve):
            dve_rwkv(rw, dve)
            for m, mixer in ((moe[0], rw), (moe[1], cv)):
                dve_norm(m, dve, lambda t: dve_mixed(mixer, dve, t), EACH_TILE, lambda t: dve_split(m, dve, t))
                dve_route(m, dve)
                dve_moe(m, dve)
                if m is moe[0]:
                    dve_conv(cv, dve, lambda t: dve_combine(moe[0], dve, t))
            dve_norm(fin, dve, lambda t: dve_combine(moe[1], dve, t), LAST_ALONE)

        @block.tensor
        def _(pe):
            pe_rwkv(rw, pe)
            for m in moe:
                pe_logits(m, pe)
                pe_ranks(m, pe)
                pe_moe(m, pe)
                if m is moe[0]:
                    pe_conv(cv, pe)


_INS = ["x", "norm1_g", "norm2_g", "final_g", "rwkv_mu", "rwkv_w_rkv", "rwkv_w0", "rwkv_w1", "rwkv_w2", "rwkv_a0",
        "rwkv_a1", "rwkv_a2", "rwkv_g1", "rwkv_g2", "rwkv_k_k", "rwkv_k_a", "rwkv_r_k", "rwkv_ln_g", "rwkv_ln_b",
        "rwkv_w_o", "conv_w_pw1", "conv_b_pw1", "conv_w_dw", "conv_b_dw", "conv_ln_g", "conv_ln_b", "conv_w_pw2",
        "conv_b_pw2", "moe_w_group", "moe_b_group", "moe_w_expert", "moe_b_expert", "moe_w_gate", "moe_w_up",
        "moe_w_down"]


def kernel(**inputs):
    import numpy as _np
    import concourse.bacc as _bacc
    from concourse import mybir as _mybir
    from concourse.bass_utils import run_bass_kernel_spmd as _run

    nc = _bacc.Bacc("TRN2", target_bir_lowering=False, num_devices=1)
    arrays, args = {}, {}
    for name in _INS:
        v = _np.ascontiguousarray(inputs[name])
        arrays[f"in_{name}_dram"] = v
        args[name] = nc.dram_tensor(f"in_{name}_dram", v.shape, _mybir.dt.from_np(v.dtype), kind="ExternalInput").ap()
    out = nc.dram_tensor("out_dram", (1, T, D), _mybir.dt.float32, kind="ExternalOutput").ap()
    bass_hybrid_rwkv7_conformer_hmoe(nc, args, out)
    r = _run(nc, [arrays], core_ids=[0])
    return r.results[0]["out_dram"]
```
